# Optimizing a Trainium2 kernel written in Bass

```python
import math
import jax, jax.numpy as jnp
from jax import lax
import numpy as np

D_MODEL = 1024
BATCH = 1
SEQ = 128
DEPTH = 2
DEC_BATCH = 1
DEC_SEQ = 256
PAST_LEN = 128

GRID_W = 64
HEAD_DIM = 64
FOURIER_CH = D_MODEL // 4
FOURIER_GROUPS = 4
FOURIER_GW = FOURIER_CH // FOURIER_GROUPS
NA_DIM = D_MODEL - FOURIER_CH
NA_HEADS = NA_DIM // HEAD_DIM
NA_MAX_ROWS = 8
NA_COLS = 16
EVEN_IN = FOURIER_CH + 3 * NA_DIM
POOL_WINDOWS = (2, 4, 8, 16)
POOL_CH = D_MODEL // 4
POOL_GW = POOL_CH // len(POOL_WINDOWS)
RWKV_DIM = D_MODEL - POOL_CH
RWKV_HEADS = RWKV_DIM // HEAD_DIM
DECAY_LORA = 64
ICLR_LORA = 64
GATE_LORA = 128
RWKV_IN = 3 * RWKV_DIM + 2 * DECAY_LORA + 2 * ICLR_LORA + GATE_LORA
ODD_IN = POOL_CH + RWKV_IN
RW_SPLITS = (RWKV_DIM, 2 * RWKV_DIM, 3 * RWKV_DIM, 3 * RWKV_DIM + DECAY_LORA, 3 * RWKV_DIM + 2 * DECAY_LORA,
             3 * RWKV_DIM + 2 * DECAY_LORA + ICLR_LORA, 3 * RWKV_DIM + 2 * DECAY_LORA + 2 * ICLR_LORA)
D_FF = 2816
N_EXPERTS = 8
TOP_K = 2
D_FF_EXPERT = 1408
N_EVEN = (DEPTH + 1) // 2
N_ODD = DEPTH // 2
Q_BLOCK = 128
RMS_EPS = 1e-6
GN_EPS = 64e-5
L2_EPS = 1e-12
DECAY_SCALE = math.exp(-0.5)
NEG_INF = -1e30

kernel_name = "hybrid_flow_prefix_fourier_natten_pool_rwkv7_step"

def rmsnorm(x, g):
    xf = x.astype(jnp.float32)
    y = xf * lax.rsqrt(jnp.mean(xf * xf, axis=-1, keepdims=True) + RMS_EPS)
    return (y * g.astype(jnp.float32)).astype(x.dtype)

def adaln(cond, w, b):
    m = jax.nn.silu(cond) @ w + b
    return jnp.split(m[:, None, :], 6, axis=-1)

def modulate(x, g, shift, scale):
    return rmsnorm(x, g) * (1.0 + scale) + shift

def swiglu(x, wg, wu, wd):
    return (jax.nn.silu(x @ wg) * (x @ wu)) @ wd

def fourier_mix(f, w):
    b, n, _ = f.shape
    fg = f.astype(jnp.float32).reshape(b, n, FOURIER_GROUPS, FOURIER_GW)
    spec = jnp.fft.fft2(fg, axes=(1, 3), norm="ortho").real
    y = jnp.einsum("bngc,gcd->bngd", spec.astype(f.dtype), w)
    return y.reshape(b, n, FOURIER_CH)

def context_attention(q, k, v):
    b, n, h, d = q.shape
    scale = d ** -0.5
    qb = q.reshape(b, n // Q_BLOCK, Q_BLOCK, h, d).swapaxes(0, 1)

    def block(qi):
        s = jnp.einsum("bqhd,bkhd->bhqk", qi, k).astype(jnp.float32) * scale
        p = jax.nn.softmax(s, axis=-1).astype(v.dtype)
        return jnp.einsum("bhqk,bkhd->bqhd", p, v)

    o = lax.map(block, qb)
    return o.swapaxes(0, 1).reshape(b, n, h, d)

def neighbourhood_attention(q, k, v, ck, cv, rel_bias):
    b, n, h, d = q.shape
    rows = n // GRID_W
    wr = min(NA_MAX_ROWS, rows)
    scale = d ** -0.5
    qg = q.reshape(b, rows, GRID_W, h, d)
    kg = k.reshape(b, rows, GRID_W, h, d)
    vg = v.reshape(b, rows, GRID_W, h, d)
    cols = jnp.arange(GRID_W)
    c0 = jnp.clip(cols - NA_COLS // 2, 0, GRID_W - NA_COLS)
    col_ok = (cols[None, :] >= c0[:, None]) & (cols[None, :] < c0[:, None] + NA_COLS)
    dc = jnp.clip(cols[None, :] - cols[:, None] + NA_COLS - 1, 0, 2 * NA_COLS - 2)

    def row(i):
        r0 = jnp.clip(i - wr // 2, 0, rows - wr)
        kb = lax.dynamic_slice_in_dim(kg, r0, wr, axis=1)
        vb = lax.dynamic_slice_in_dim(vg, r0, wr, axis=1)
        qi = lax.dynamic_index_in_dim(qg, i, axis=1, keepdims=False)
        dr = r0 + jnp.arange(wr) - i + NA_MAX_ROWS - 1
        bias = rel_bias[:, dr[None, :, None], dc[:, None, :]]
        s_loc = jnp.einsum("bqhd,brkhd->bhqrk", qi, kb).astype(jnp.float32) * scale
        s_loc = s_loc + bias[None].astype(jnp.float32)
        s_loc = jnp.where(col_ok[:, None, :], s_loc, NEG_INF).reshape(b, h, GRID_W, wr * GRID_W)
        s_ctx = jnp.einsum("bqhd,bkhd->bhqk", qi, ck).astype(jnp.float32) * scale
        p = jax.nn.softmax(jnp.concatenate([s_loc, s_ctx], axis=-1), axis=-1).astype(v.dtype)
        p_loc = p[..., : wr * GRID_W].reshape(b, h, GRID_W, wr, GRID_W)
        p_ctx = p[..., wr * GRID_W:]
        return (jnp.einsum("bhqrk,brkhd->bqhd", p_loc, vb)
                + jnp.einsum("bhqk,bkhd->bqhd", p_ctx, cv.astype(v.dtype)))

    o = lax.map(row, jnp.arange(rows))
    return o.swapaxes(0, 1).reshape(b, n, h, d)

def even_mixer(h, w_in, f_w, rel_bias, w_out, ctx_kv):
    b, n, _ = h.shape
    proj = h @ w_in
    q, k, v = [t.reshape(b, n, NA_HEADS, HEAD_DIM) for t in jnp.split(proj[..., FOURIER_CH:], 3, axis=-1)]
    a_out = fourier_mix(proj[..., :FOURIER_CH], f_w)
    if ctx_kv is None:
        b_out = context_attention(q, k, v)
    else:
        b_out = neighbourhood_attention(q, k, v, ctx_kv[0], ctx_kv[1], rel_bias)
    out = jnp.concatenate([a_out, b_out.reshape(b, n, NA_DIM)], axis=-1) @ w_out
    return out, k, v

def pool_mix(x, w, scale):
    b, n, _ = x.shape
    xf = x.astype(jnp.float32)
    cs = jnp.concatenate([jnp.zeros((b, 1, POOL_CH), jnp.float32), jnp.cumsum(xf, axis=1)], axis=1)
    t = jnp.arange(n)
    groups = []
    for g, win in enumerate(POOL_WINDOWS):
        lo = jnp.clip(t - win // 2, 0, n)
        hi = jnp.clip(t + win - win // 2, 0, n)
        sl = slice(g * POOL_GW, (g + 1) * POOL_GW)
        mean = (cs[:, hi, sl] - cs[:, lo, sl]) / (hi - lo).astype(jnp.float32)[None, :, None]
        groups.append(mean - xf[:, :, sl])
    y = jnp.stack(groups, axis=2).astype(x.dtype)
    y = jnp.einsum("bngc,gcd->bngd", y, w).reshape(b, n, POOL_CH)
    return y * scale

def centred_shift(x, mu):
    prev = jnp.pad(x[:, :-1], ((0, 0), (1, 0), (0, 0)))
    nxt = jnp.pad(x[:, 1:], ((0, 0), (0, 1), (0, 0)))
    return x + mu[0] * (prev - x) + mu[1] * (nxt - x)

def wkv_scan(r, w, k, v, kk, a, s0, reverse):
    xs = tuple(jnp.swapaxes(t, 0, 1) for t in (r, w, k, v, kk, a))

    def step(s, inp):
        r_t, w_t, k_t, v_t, kk_t, a_t = inp
        sa = jnp.einsum("bhvk,bhk->bhv", s, kk_t)
        s = (s * w_t[:, :, None, :] - sa[..., None] * (kk_t * a_t)[:, :, None, :]
             + v_t[..., None] * k_t[:, :, None, :])
        return s, jnp.einsum("bhvk,bhk->bhv", s, r_t)

    s_fin, o = lax.scan(step, s0, xs, reverse=reverse)
    return jnp.swapaxes(o, 0, 1), s_fin

def rwkv7_bidir(z, s0, decay_w0, decay_up, iclr_a0, iclr_up, gate_up, k_k, k_a, r_k, gn_w, gn_b):
    b, n, _ = z.shape
    f32 = jnp.float32
    r, k, v, wl_f, wl_b, al_f, al_b, gl = jnp.split(z.astype(f32), RW_SPLITS, axis=-1)
    hd = lambda t: t.reshape(b, n, RWKV_HEADS, HEAD_DIM)
    rh, kh, vh = hd(r), hd(k), hd(v)
    kk = hd(k * k_k.astype(f32))
    kk = kk * lax.rsqrt(jnp.sum(kk * kk, axis=-1, keepdims=True) + L2_EPS)
    k_a_h = k_a.astype(f32).reshape(RWKV_HEADS, HEAD_DIM)
    outs, finals = [], []
    for dr, (wl, al) in enumerate(((wl_f, al_f), (wl_b, al_b))):
        w = jnp.exp(-DECAY_SCALE * jax.nn.sigmoid(decay_w0[dr].astype(f32) + jnp.tanh(wl) @ decay_up[dr].astype(f32)))
        a = hd(jax.nn.sigmoid(iclr_a0[dr].astype(f32) + al @ iclr_up[dr].astype(f32)))
        k_mod = kh * (1.0 + (a - 1.0) * k_a_h)
        o_d, s_d = wkv_scan(rh, hd(w), k_mod, vh, kk, a, s0[:, dr].astype(f32), dr == 1)
        outs.append(o_d)
        finals.append(s_d)
    o = outs[0] + outs[1]
    mu = jnp.mean(o, axis=-1, keepdims=True)
    var = jnp.mean(jnp.square(o - mu), axis=-1, keepdims=True)
    o = ((o - mu) * lax.rsqrt(var + GN_EPS)).reshape(b, n, RWKV_DIM) * gn_w.astype(f32) + gn_b.astype(f32)
    bonus = jnp.sum(rh * kh * r_k.astype(f32), axis=-1, keepdims=True) * vh
    g = jax.nn.sigmoid(gl) @ gate_up.astype(f32)
    y = (o + bonus.reshape(b, n, RWKV_DIM)) * g
    return y.astype(z.dtype), jnp.stack(finals, axis=1)

def odd_mixer(h, s0, w_in, pool_w, pool_scale, shift_mu, decay_w0, decay_up, iclr_a0, iclr_up,
              gate_up, k_k, k_a, r_k, gn_w, gn_b, w_out):
    proj = h @ w_in
    c_out = pool_mix(proj[..., :POOL_CH], pool_w, pool_scale)
    zr = centred_shift(proj[..., POOL_CH:], shift_mu)
    d_out, s_fin = rwkv7_bidir(zr, s0, decay_w0, decay_up, iclr_a0, iclr_up, gate_up, k_k, k_a, r_k, gn_w, gn_b)
    out = jnp.concatenate([c_out, d_out.astype(c_out.dtype)], axis=-1) @ w_out
    return out, s_fin

def moe_swiglu(x, router_w, router_b, wg, wu, wd):
    b, n, dm = x.shape
    t = x.reshape(b * n, dm)
    logits = (t @ router_w).astype(jnp.float32) + router_b.astype(jnp.float32)
    top_v, top_i = lax.top_k(logits, TOP_K)
    top_g = jax.nn.softmax(top_v, axis=-1)
    combine = jnp.sum(jax.nn.one_hot(top_i, N_EXPERTS, dtype=jnp.float32) * top_g[..., None], axis=1).astype(x.dtype)
    out = jnp.zeros_like(t)
    for e in range(N_EXPERTS):
        out = out + combine[:, e:e + 1] * swiglu(t, wg[e], wu[e], wd[e])
    return out.reshape(b, n, dm)

def setup_inputs(seed: int = 0) -> dict:
    key = jax.random.key(seed)
    ks = iter(jax.random.split(key, 64))
    f32 = jnp.float32
    nrm = lambda shape, s: jax.random.normal(next(ks), shape, f32) * s
    uni = lambda shape, lo, hi: jax.random.uniform(next(ks), shape, f32, lo, hi)
    D = D_MODEL
    inp = {}
    inp["x_prompt"] = nrm((BATCH, SEQ, D), 1.0)
    inp["x_sample"] = nrm((DEC_BATCH, DEC_SEQ, D), 1.0)
    inp["cache_na_k"] = nrm((DEC_BATCH, N_EVEN, PAST_LEN, NA_HEADS, HEAD_DIM), 1.0)
    inp["cache_na_v"] = nrm((DEC_BATCH, N_EVEN, PAST_LEN, NA_HEADS, HEAD_DIM), 1.0)
    inp["state_wkv"] = nrm((DEC_BATCH, N_ODD, 2, RWKV_HEADS, HEAD_DIM, HEAD_DIM), 1.0)
    inp["c"] = nrm((DEC_BATCH, D), 1.0)
    inp["c_ctx"] = nrm((D,), 1.0)
    inp["mod_w"] = nrm((DEPTH, D, 6 * D), 0.5 * D ** -0.5)
    inp["mod_b"] = nrm((DEPTH, 6 * D), 0.02)
    inp["norm_mix"] = 1.0 + nrm((DEPTH, D), 0.05)
    inp["norm_ffn"] = 1.0 + nrm((DEPTH, D), 0.05)
    inp["norm_final"] = 1.0 + nrm((D,), 0.05)
    inp["na_w_in"] = nrm((N_EVEN, D, EVEN_IN), D ** -0.5)
    inp["fourier_w"] = nrm((N_EVEN, FOURIER_GROUPS, FOURIER_GW, FOURIER_GW), FOURIER_GW ** -0.5)
    inp["na_rel_bias"] = nrm((N_EVEN, NA_HEADS, 2 * NA_MAX_ROWS - 1, 2 * NA_COLS - 1), 0.3)
    inp["na_w_out"] = nrm((N_EVEN, FOURIER_CH + NA_DIM, D), D ** -0.5)
    inp["ffn_w_gate"] = nrm((N_EVEN, D, D_FF), D ** -0.5)
    inp["ffn_w_up"] = nrm((N_EVEN, D, D_FF), D ** -0.5)
    inp["ffn_w_down"] = nrm((N_EVEN, D_FF, D), D_FF ** -0.5)
    inp["rw_w_in"] = nrm((N_ODD, D, ODD_IN), D ** -0.5)
    inp["pool_w"] = nrm((N_ODD, len(POOL_WINDOWS), POOL_GW, POOL_GW), POOL_GW ** -0.5)
    inp["pool_scale"] = 1.0 + nrm((N_ODD, POOL_CH), 0.1)
    inp["shift_mu"] = uni((N_ODD, 2, RWKV_IN), 0.0, 0.5)
    inp["decay_w0"] = uni((N_ODD, 2, RWKV_DIM), -4.0, 2.0)
    inp["decay_up"] = nrm((N_ODD, 2, DECAY_LORA, RWKV_DIM), 0.5 * DECAY_LORA ** -0.5)
    inp["iclr_a0"] = nrm((N_ODD, 2, RWKV_DIM), 0.5)
    inp["iclr_up"] = nrm((N_ODD, 2, ICLR_LORA, RWKV_DIM), 0.5 * ICLR_LORA ** -0.5)
    inp["gate_up"] = nrm((N_ODD, GATE_LORA, RWKV_DIM), GATE_LORA ** -0.5)
    inp["k_k"] = 1.0 + nrm((N_ODD, RWKV_DIM), 0.1)
    inp["k_a"] = 1.0 + nrm((N_ODD, RWKV_DIM), 0.1)
    inp["r_k"] = nrm((N_ODD, RWKV_HEADS, HEAD_DIM), 0.1)
    inp["gn_w"] = 1.0 + nrm((N_ODD, RWKV_DIM), 0.05)
    inp["gn_b"] = nrm((N_ODD, RWKV_DIM), 0.02)
    inp["rw_w_out"] = nrm((N_ODD, POOL_CH + RWKV_DIM, D), D ** -0.5)
    inp["router_w"] = nrm((N_ODD, D, N_EXPERTS), D ** -0.5)
    inp["router_b"] = nrm((N_ODD, N_EXPERTS), 0.01)
    inp["moe_w_gate"] = nrm((N_ODD, N_EXPERTS, D, D_FF_EXPERT), D ** -0.5)
    inp["moe_w_up"] = nrm((N_ODD, N_EXPERTS, D, D_FF_EXPERT), D ** -0.5)
    inp["moe_w_down"] = nrm((N_ODD, N_EXPERTS, D_FF_EXPERT, D), D_FF_EXPERT ** -0.5)
    return inp

def reference(x_prompt, x_sample, cache_na_k, cache_na_v, state_wkv, c, c_ctx, mod_w, mod_b, norm_mix,
              norm_ffn, norm_final, na_w_in, fourier_w, na_rel_bias, na_w_out, ffn_w_gate, ffn_w_up, ffn_w_down,
              rw_w_in, pool_w, pool_scale, shift_mu, decay_w0, decay_up, iclr_a0, iclr_up, gate_up, k_k, k_a,
              r_k, gn_w, gn_b, rw_w_out, router_w, router_b, moe_w_gate, moe_w_up, moe_w_down):
    nb = x_prompt.shape[0]
    cond_ctx = jnp.broadcast_to(c_ctx, (nb, D_MODEL))
    xp, xs = x_prompt, x_sample
    new_k, new_v, new_s = [], [], []
    for l in range(DEPTH):
        j = l // 2
        sh1p, sc1p, g1p, sh2p, sc2p, g2p = adaln(cond_ctx, mod_w[l], mod_b[l])
        sh1s, sc1s, g1s, sh2s, sc2s, g2s = adaln(c, mod_w[l], mod_b[l])
        hp = modulate(xp, norm_mix[l], sh1p, sc1p)
        hs = modulate(xs, norm_mix[l], sh1s, sc1s)
        if l % 2 == 0:
            ep = (na_w_in[j], fourier_w[j], na_rel_bias[j], na_w_out[j])
            mp, kp, vp = even_mixer(hp, *ep, None)
            ms, _, _ = even_mixer(hs, *ep, (cache_na_k[:, j], cache_na_v[:, j]))
            new_k.append(kp)
            new_v.append(vp)
        else:
            op = (rw_w_in[j], pool_w[j], pool_scale[j], shift_mu[j], decay_w0[j], decay_up[j], iclr_a0[j],
                  iclr_up[j], gate_up[j], k_k[j], k_a[j], r_k[j], gn_w[j], gn_b[j], rw_w_out[j])
            s0 = jnp.zeros((nb, 2, RWKV_HEADS, HEAD_DIM, HEAD_DIM), jnp.float32)
            mp, sp = odd_mixer(hp, s0, *op)
            ms, _ = odd_mixer(hs, state_wkv[:, j], *op)
            new_s.append(sp)
        xp = xp + g1p * mp
        xs = xs + g1s * ms
        hp = modulate(xp, norm_ffn[l], sh2p, sc2p)
        hs = modulate(xs, norm_ffn[l], sh2s, sc2s)
        if l % 2 == 0:
            fw = (ffn_w_gate[j], ffn_w_up[j], ffn_w_down[j])
            xp = xp + g2p * swiglu(hp, *fw)
            xs = xs + g2s * swiglu(hs, *fw)
        else:
            mw = (router_w[j], router_b[j], moe_w_gate[j], moe_w_up[j], moe_w_down[j])
            xp = xp + g2p * moe_swiglu(hp, *mw)
            xs = xs + g2s * moe_swiglu(hs, *mw)
    y_prompt = rmsnorm(xp, norm_final)
    y_sample = rmsnorm(xs, norm_final)
    new_cache_na_k = jnp.stack(new_k, axis=1)
    new_cache_na_v = jnp.stack(new_v, axis=1)
    new_state_wkv = jnp.stack(new_s, axis=1)
    return (y_prompt, y_sample, new_cache_na_k, new_cache_na_v, new_state_wkv)


_drawn_inputs = setup_inputs


def setup_inputs(seed=0):
    import zlib

    import numpy as np

    out = dict(_drawn_inputs(seed))
    spreads = {}
    factors = {'na_rel_bias': 4.63, 'pool_scale': 3.118, 'gn_w': 6.327, 'gn_b': 7.714, 'router_b': 8.0}
    for name, (base, spread) in spreads.items():
        noise = np.random.default_rng([zlib.crc32(name.encode()), seed]).standard_normal(out[name].shape)
        drawn = base * np.exp(spread * noise) if base else spread * noise
        out[name] = __import__('jax').numpy.asarray(drawn.astype(out[name].dtype))
    for name, factor in factors.items():
        out[name] = (out[name] * factor).astype(out[name].dtype)
    return out
```

```python
import math
from contextlib import ExitStack

import concourse.bass as bass
from concourse import mybir

F32 = mybir.dt.float32
I32 = mybir.dt.int32
ALU = mybir.AluOpType
ACT = mybir.ActivationFunctionType
AX = mybir.AxisListType

P = 128
D = 1024
KT = D // P
SEQ, DEC = 128, 256
TOK = SEQ + DEC
TT = TOK // P
BANK = 512
HD = 64
PAIRS = 6
GRID_W, ROWS, WIN = 64, 4, 16
BIAS_ROW, BIAS_HEAD = 31, 15 * 31
FF = 2816
FFE = 1408
NE = 8
C = 64
NCH = TOK // C
RMS_EPS, GN_EPS, L2_EPS = 1e-6, 64e-5, 1e-12
DECAY = math.exp(-0.5)
LEVELS = (2, 4, 8, 16, 32)
MAX_ITEMS = 13
ITEM_COLS = 16
POOL_WINDOWS = (2, 4, 8, 16)

CONSTS = {}
_at = 0
for _name, _w in (("ident", 128), ("pick", 256), ("dft_c", 256), ("dft_s", 1024), ("dft_p", 256), ("window", 64),
                  ("masks", 16 * 128), ("halves", 128), ("chunk", 384), ("inv_count", 768), ("before", 128),
                  ("ones", 128), ("slot", 128), ("item", ITEM_COLS), ("lower8", NE)):
    CONSTS[_name] = (_at, _at + _w)
    _at += _w
N_CONSTS = _at


def steps(names):
    names = list(names)
    place = {name: i for i, name in enumerate(names)}
    assert len(place) == len(names)
    given = []

    def inc(name):
        assert place[name] == len(given) % len(names), name
        given.append(name)
        return 1

    def at(name, j=0):
        return j * len(names) + place[name] + 1

    return inc, at


class Core:

    def __init__(self, nc, I, O):
        self.nc, self.I, self.O = nc, I, O


def build(nc, I, O):
    with ExitStack() as whole:
        R = Core(nc, I, O)
        R.sem = lambda name: whole.enter_context(nc.semaphore(name))
        R.passed = R.sem("wait_passed")
        R.sb = lambda name, shape, dt=F32: whole.enter_context(nc.sbuf_tensor(name, shape, dt))
        R.PS = whole.enter_context(nc.psum_tensor("banks", [P, 8, BANK], F32))
        R.B = [R.PS[:, i, :] for i in range(8)]
        R.X = R.sb("residual", [P, TT, D])
        R.HT = R.sb("normed_by_channel", [P, KT, TOK])
        R.ident = R.sb("identity", [P, P])
        R.scale_col = R.sb("scale_columns", [P, 4, KT, 2])
        R.shift_col = R.sb("shift_columns", [P, 4, KT, 2])
        R.VT = R.sb("parameter_columns", [P, 50])
        R.ffn_gate = R.sb("ffn_gate_rows", [P, 2, D])
        R.cond = R.sb("silu_cond", [P, KT, 32])
        R.bias_rows = nc.dram_tensor("bias_rows", [P, 12 * 2 * ROWS * GRID_W], F32).ap()
        R.bias_spread = R.sem("bias_spread")
        R.mod_loaded = [R.sem(f"mod_w_loaded{s}") for s in range(16)]
        prologue(R)
        layer0(R)
        dense_ffn(R)
        layer1(R)
        moe(R)
        finish(R)


def local(R):
    stack = ExitStack()
    return stack, lambda name, shape, dt=F32: stack.enter_context(R.nc.sbuf_tensor(name, shape, dt))


def const(R, name):
    a, b = CONSTS[name]
    return R.I["consts"][:, a:b]


def prologue(R):
    nc = R.nc
    stack, sb = local(R)
    with stack:
        rows = sb("parameter_rows", [50, P])
        load_x, load_rows, load_const = R.sem("x_loaded"), R.sem("rows_loaded"), R.sem("ident_loaded")
        cleared, turned, copied = R.sem("cond_cleared"), R.sem("rows_turned"), R.sem("columns_ready")
        with nc.Block() as block:

            @block.sync
            def _(sp):
                as_rows = lambda a: a.rearrange("(r p) -> r p", p=P)
                sp.dma_start(rows[0:8, :], as_rows(R.I["c_ctx"])).then_inc(load_rows, 16)
                sp.dma_start(rows[8:16, :], as_rows(R.I["c"][0])).then_inc(load_rows, 16)
                for l in range(2):
                    sp.dma_start(rows[16 + 8 * l:24 + 8 * l, :], as_rows(R.I["norm_mix"][l])).then_inc(load_rows, 16)
                    sp.dma_start(rows[32 + 8 * l:40 + 8 * l, :], as_rows(R.I["norm_ffn"][l])).then_inc(load_rows, 16)
                sp.dma_start(rows[48:50, :], as_rows(R.I["pool_scale"][0])).then_inc(load_rows, 16)
                sp.dma_start(R.ident[:, :], const(R, "ident")).then_inc(load_const, 16)
                sp.dma_start(R.X[:, 0, :], R.I["x_prompt"][0]).then_inc(load_x, 16)
                sp.dma_start(R.X[:, 1:3, :], R.I["x_sample"][0].rearrange("(t p) d -> p t d", p=P)).then_inc(load_x, 16)
                sp.wait_ge(load_x, 32)

            @block.gpsimd
            def _(pool):
                rows_of = R.bias_rows.rearrange("(a c) (h t r k) -> a t h c r k", a=2, h=12, t=2, r=ROWS)
                for i in range(ROWS):
                    for r in range(ROWS):
                        src = bass.AP(R.I["na_rel_bias"].tensor, (7 - i + r) * BIAS_ROW + 15,
                                      [[BIAS_HEAD, 12], [-1, GRID_W], [1, GRID_W]])
                        pool.dma_start(rows_of[i % 2, i // 2, :, :, r, :], src).then_inc(R.bias_spread, 16)

            @block.vector
            def _(dve):
                nc.vector.memset(R.cond[:, :, :], 0.0).then_inc(cleared, 1)

            @block.tensor
            def _(pe):
                pe.wait_ge(load_rows, 7 * 16)
                pe.wait_ge(load_const, 16)
                nc.tensor.transpose(R.B[0][:, 0:50], rows[:, :], R.ident[0:50, 0:50]).then_inc(turned, 1)

            @block.scalar
            def _(act):
                act.wait_ge(turned, 1)
                nc.scalar.activation(R.VT[:, :], R.B[0][:, 0:50], ACT.Copy).then_inc(copied, 1)
                act.wait_ge(cleared, 1)
                nc.scalar.activation(R.cond[:, :, 0], R.B[0][:, 0:8], ACT.Silu)
                nc.scalar.activation(R.cond[:, :, 1], R.B[0][:, 8:16], ACT.Silu)


def modulation(R, l, mix_gate):
    nc = R.nc
    stack, sb = local(R)
    with stack:
        W = sb(f"mod_w{l}", [P, 16, 2048])
        bias = sb(f"mod_bias{l}", [1, 3, 2048])
        one = sb(f"mod_one{l}", [1, 32])
        pick = sb(f"pick{l}", [P, 2, P])
        M = sb(f"mod_rows{l}", [P, 3, BANK])
        col = sb(f"mod_cols{l}", [P, 3, 4, 4, 2])
        loaded, SLOTS = R.mod_loaded, len(R.mod_loaded)
        layer_uses = [len(range(s, 3 * KT, SLOTS)) for s in range(SLOTS)]
        small = R.sem(f"mod_small_loaded{l}")
        used = R.sem(f"mod_w_used{l}")
        ones = R.sem(f"mod_one_set{l}")
        pe_done = R.sem(f"mod_pe{l}_done")
        pe_inc, pe_at = steps([f"{w}{g}" for g in range(3) for w in ("rows", "turned", "gate")])
        act_done = R.sem(f"mod_act{l}_done")
        act_inc, act_at = steps([f"{w}{g}" for g in range(3) for w in ("rows", "gate")])
        dve_done = R.sem(f"mod_dve{l}_done")
        dve_inc, dve_at = steps([f"cols{g}" for g in range(3)])
        gate_of = {1: (0, mix_gate), 2: (2, R.ffn_gate)}
        with nc.Block() as block:

            @block.sync
            def _(sp):
                sp.dma_start(bias[0:1, :, :], R.I["mod_b"][l:l + 1, :].rearrange("a (g n) -> a g n", g=3)).then_inc(small, 16)
                sp.dma_start(pick[:, :, :], const(R, "pick").rearrange("p (c n) -> p c n", c=2)).then_inc(small, 16)
                for u in range(3 * KT):
                    g, k = divmod(u, KT)
                    if u >= SLOTS:
                        sp.wait_ge(used, u - SLOTS + 1)
                    sp.dma_start(W[:, u % SLOTS, :], R.I["mod_w"][l, k * P:(k + 1) * P, g * 2048:(g + 1) * 2048])\
                        .then_inc(loaded[u % SLOTS], 16)

            @block.tensor
            def _(pe):
                pe.wait_ge(small, 32)
                pe.wait_ge(ones, 1)
                for g in range(3):
                    for k in range(KT):
                        u = g * KT + k
                        pe.wait_ge(loaded[u % SLOTS], 16 * (l * layer_uses[u % SLOTS] + u // SLOTS + 1))
                        for q in range(4):
                            mm = nc.tensor.matmul(R.B[g][32 * q:32 * q + 32, :], R.cond[:, k, :],
                                                  W[:, u % SLOTS, q * BANK:(q + 1) * BANK], start=(k == 0), stop=False)
                        mm.then_inc(used, 1)
                    for q in range(4):
                        mm = nc.tensor.matmul(R.B[g][32 * q:32 * q + 32, :], one[0:1, :],
                                              bias[0:1, g, q * BANK:(q + 1) * BANK], start=False, stop=True)
                    mm.then_inc(pe_done, pe_inc(f"rows{g}"))
                    pe.wait_ge(act_done, act_at(f"rows{g}"))
                    for i in range(4):
                        mm = nc.tensor.transpose(R.B[3][:, i * P:(i + 1) * P], M[:, g, i * P:(i + 1) * P], R.ident[:, :])
                    mm.then_inc(pe_done, pe_inc(f"turned{g}"))
                    if g in gate_of:
                        q0 = gate_of[g][0]
                        if g == 2:
                            pe.wait_ge(act_done, act_at("gate1"))
                        for c in range(2):
                            for h in range(2):
                                q = q0 + h
                                mm = nc.tensor.matmul(R.B[4 + 2 * c + h][:, :], pick[32 * q:32 * q + 32, c, :],
                                                      M[32 * q:32 * q + 32, g, :], start=True, stop=True,
                                                      tile_position=(32 * q, 0))
                    pe.wait_ge(dve_done, dve_at(f"cols{g}"))
                    if g not in gate_of:
                        mm = nc.tensor.transpose(R.B[7][:, 0:P], M[:, g, 0:P], R.ident[:, :])
                    mm.then_inc(pe_done, pe_inc(f"gate{g}"))

            @block.scalar
            def _(act):
                for g in range(3):
                    act.wait_ge(pe_done, pe_at(f"rows{g}"))
                    nc.scalar.activation(M[:, g, :], R.B[g][:, :], ACT.Copy).then_inc(act_done, act_inc(f"rows{g}"))
                    act.wait_ge(pe_done, pe_at(f"gate{g}"))
                    if g in gate_of:
                        for c in range(2):
                            for h in range(2):
                                a = nc.scalar.activation(gate_of[g][1][:, c, h * BANK:(h + 1) * BANK],
                                                         R.B[4 + 2 * c + h][:, :], ACT.Copy)
                    else:
                        a = nc.scalar.activation(M[:, g, 0:1], M[:, g, 0:1], ACT.Copy)
                    a.then_inc(act_done, act_inc(f"gate{g}"))

            @block.vector
            def _(dve):
                nc.vector.memset(one[:, :], 1.0).then_inc(ones, 1)
                for g in range(3):
                    dve.wait_ge(pe_done, pe_at(f"turned{g}"))
                    turned = R.B[3][:, :].rearrange("p (i q x) -> p i q x", i=4, q=4)
                    nc.vector.tensor_copy(col[:, g], turned[:, :, :, 0:2]).then_inc(dve_done, dve_inc(f"cols{g}"))
                dve.wait_ge(dve_done, dve_at("cols2"))
                for n, (shift, scale, w0) in enumerate(((0, 1, 16 + 8 * l), (3, 4, 32 + 8 * l))):
                    for h in range(2):
                        ks = slice(4 * h, 4 * h + 4)
                        weight = R.VT[:, w0 + 4 * h:w0 + 4 * h + 4].unsqueeze(2).broadcast_to([P, 4, 2])
                        nc.vector.scalar_tensor_tensor(out=R.scale_col[:, 2 * l + n, ks, :],
                                                       in0=col[:, scale // 2, :, 2 * (scale % 2) + h, :], scalar=1.0,
                                                       in1=weight, op0=ALU.add, op1=ALU.mult)
                        nc.vector.tensor_copy(R.shift_col[:, 2 * l + n, ks, :],
                                              col[:, shift // 2, :, 2 * (shift % 2) + h, :])


def normed(R, n):
    nc = R.nc
    stack, sb = local(R)
    with stack:
        XN = sb(f"scaled{n}", [P, TT, D])
        ss, ms, rt, rs = (sb(f"{w}{n}", [P, TT]) for w in ("sumsq", "meansq", "root", "rstd"))
        act_done = R.sem(f"norm_act{n}_done")
        act_inc, act_at = steps(["squares", "root", "scaled0", "scaled2"])
        dve_done = R.sem(f"norm_dve{n}_done")
        dve_inc, dve_at = steps(["mean", "rstd", "scaled1"])
        turned = R.sem(f"norm_turned{n}")
        with nc.Block() as block:

            @block.scalar
            def _(act):
                for t in range(TT):
                    a = nc.scalar.activation(XN[:, t, :], R.X[:, t, :], ACT.Square, accum_out=ss[:, t:t + 1])
                a.then_inc(act_done, act_inc("squares"))
                act.wait_ge(dve_done, dve_at("mean"))
                nc.scalar.activation(rt[:, :], ms[:, :], ACT.Sqrt).then_inc(act_done, act_inc("root"))
                act.wait_ge(dve_done, dve_at("rstd"))
                for t in (0, 2):
                    nc.scalar.activation(XN[:, t, :], R.X[:, t, :], ACT.Copy, scale=rs[:, t:t + 1]).then_inc(act_done, act_inc(f"scaled{t}"))
                for k in range(0, KT, 2):
                    act.wait_ge(turned, k + 1)
                    for c, cols in ((0, slice(0, SEQ)), (1, slice(SEQ, TOK))):
                        nc.scalar.activation(R.HT[:, k, cols], R.B[k][:, cols], ACT.Identity,
                                             bias=R.shift_col[:, n, k, c:c + 1], scale=R.scale_col[:, n, k, c:c + 1])

            @block.vector
            def _(dve):
                dve.wait_ge(act_done, act_at("squares"))
                nc.vector.tensor_scalar(ms[:, :], ss[:, :], 1.0 / D, RMS_EPS, ALU.mult, ALU.add).then_inc(dve_done, dve_inc("mean"))
                dve.wait_ge(act_done, act_at("root"))
                nc.vector.reciprocal(rs[:, :], rt[:, :]).then_inc(dve_done, dve_inc("rstd"))
                dve.wait_ge(dve_done, dve_at("rstd"))
                nc.vector.tensor_scalar(XN[:, 1, :], R.X[:, 1, :], rs[:, 1:2], None, ALU.mult).then_inc(dve_done, dve_inc("scaled1"))
                for k in range(1, KT, 2):
                    dve.wait_ge(turned, k + 1)
                    for c, cols in ((0, slice(0, SEQ)), (1, slice(SEQ, TOK))):
                        nc.vector.tensor_scalar(R.HT[:, k, cols], R.B[k][:, cols], R.scale_col[:, n, k, c:c + 1],
                                                R.shift_col[:, n, k, c:c + 1], ALU.mult, ALU.add)

            @block.tensor
            def _(pe):
                pe.wait_ge(act_done, act_at("scaled2"))
                pe.wait_ge(dve_done, dve_at("scaled1"))
                for k in range(KT):
                    for t in range(TT):
                        mm = nc.tensor.transpose(R.B[k][:, t * P:(t + 1) * P], XN[:, t, k * P:(k + 1) * P], R.ident[:, :])
                    mm.then_inc(turned, 1)


def layer0(R):
    stack, sb = local(R)
    with stack:
        R.mix_gate = sb("mix_gate_rows0", [P, 2, D])
        modulation(R, 0, R.mix_gate)
        normed(R, 0)
        R.MT = sb("mixed_by_channel0", [P, KT, TOK])
        fourier(R)
        attention(R)
        mixed(R, R.I["na_w_out"][0], 0)
    normed(R, 1)


def fourier(R):
    nc = R.nc
    stack, sb = local(R)
    with stack:
        W = sb("fourier_w_in", [P, KT, 256])
        dc, ds, dp = sb("dft_channels", [P, 256]), sb("dft_latent", [P, 4, DEC]), sb("dft_prompt", [P, 2, SEQ])
        GW = sb("group_w", [P, 2, P])
        fT = sb("fourier_in", [P, 2, TOK])
        XCS = sb("channel_dft", [P, TT, 2, 256])
        spec = sb("spectrum", [P, 2, TOK])
        w_in, tables, gw, zero = R.sem("fw_in"), R.sem("fw_tables"), R.sem("fw_group"), R.sem("fw_zero")
        pe_done = R.sem("fourier_pe_done")
        pe_inc, pe_at = steps([f"{w}{m}" for w in ("in", "chan", "spec", "out") for m in range(2)])
        act_done = R.sem("fourier_act_done")
        act_inc, act_at = steps([f"{w}{m}" for w in ("in", "chan", "spec", "out") for m in range(2)])
        with nc.Block() as block:

            @block.vector
            def _(dve):
                nc.vector.memset(GW[:, :, :], 0.0).then_inc(zero, 1)

            @block.sync
            def _(sp):
                sp.dma_start(W[:, :, :], R.I["na_w_in"][0].rearrange("(k p) n -> p k n", p=P)[:, :, 0:256]).then_inc(w_in, 16)
                sp.dma_start(dc[:, :], const(R, "dft_c")).then_inc(tables, 16)
                sp.dma_start(ds[:, :, :], const(R, "dft_s").rearrange("p (a n) -> p a n", a=4)).then_inc(tables, 16)
                sp.dma_start(dp[:, :, :], const(R, "dft_p").rearrange("p (a n) -> p a n", a=2)).then_inc(tables, 16)
                sp.wait_ge(zero, 1)
                for g in range(4):
                    sp.dma_start(GW[64 * (g % 2):64 * (g % 2) + 64, g // 2, 64 * (g % 2):64 * (g % 2) + 64],
                                 R.I["fourier_w"][0, g]).then_inc(gw, 16)

            @block.tensor
            def _(pe):
                pe.wait_ge(w_in, 16)
                for m in range(2):
                    for k in range(KT):
                        mm = nc.tensor.matmul(R.B[m][:, 0:TOK], W[:, k, m * P:(m + 1) * P], R.HT[:, k, :],
                                              start=(k == 0), stop=(k == KT - 1))
                    mm.then_inc(pe_done, pe_inc(f"in{m}"))
                pe.wait_ge(tables, 48)
                for m in range(2):
                    pe.wait_ge(act_done, act_at(f"in{m}"))
                    for t in range(TT):
                        mm = nc.tensor.matmul(R.B[2 + m + 2 * (t // 2)][:, (t % 2) * 256:(t % 2) * 256 + 256],
                                              fT[:, m, t * P:(t + 1) * P], dc[:, :], start=True, stop=True)
                    mm.then_inc(pe_done, pe_inc(f"chan{m}"))
                for m in range(2):
                    pe.wait_ge(act_done, act_at(f"chan{m}"))
                    bank = R.B[6 + m]
                    for a in range(2):
                        nc.tensor.matmul(bank[:, 0:SEQ], XCS[:, 0, m, a * P:(a + 1) * P], dp[:, a, :], start=(a == 0), stop=(a == 1))
                    for a in range(2):
                        for t in range(2):
                            mm = nc.tensor.matmul(bank[:, SEQ:TOK], XCS[:, 1 + t, m, a * P:(a + 1) * P], ds[:, 2 * a + t, :],
                                                  start=(a + t == 0), stop=(a + t == 2))
                    mm.then_inc(pe_done, pe_inc(f"spec{m}"))
                pe.wait_ge(gw, 64)
                for m in range(2):
                    pe.wait_ge(act_done, act_at(f"spec{m}"))
                    nc.tensor.matmul(R.B[m][:, 0:TOK], GW[:, m, :], spec[:, m, :], start=True, stop=True).then_inc(pe_done, pe_inc(f"out{m}"))

            @block.scalar
            def _(act):
                for m in range(2):
                    act.wait_ge(pe_done, pe_at(f"in{m}"))
                    nc.scalar.activation(fT[:, m, :], R.B[m][:, 0:TOK], ACT.Copy).then_inc(act_done, act_inc(f"in{m}"))
                for m in range(2):
                    act.wait_ge(pe_done, pe_at(f"chan{m}"))
                    nc.scalar.activation(XCS[:, 0:2, m, :], R.B[2 + m][:, :].rearrange("p (t n) -> p t n", t=2), ACT.Copy)
                    nc.scalar.activation(XCS[:, 2, m, :], R.B[4 + m][:, 0:256], ACT.Copy).then_inc(act_done, act_inc(f"chan{m}"))
                for m in range(2):
                    act.wait_ge(pe_done, pe_at(f"spec{m}"))
                    nc.scalar.activation(spec[:, m, :], R.B[6 + m][:, 0:TOK], ACT.Copy).then_inc(act_done, act_inc(f"spec{m}"))
                for m in range(2):
                    act.wait_ge(pe_done, pe_at(f"out{m}"))
                    nc.scalar.activation(R.MT[:, m, :], R.B[m][:, 0:TOK], ACT.Copy).then_inc(act_done, act_inc(f"out{m}"))


def attention(R):
    nc = R.nc
    stack, sb = local(R)
    with stack:
        W = sb("qkv_w", [P, 3, KT, P])
        qT, kT = sb("qT", [P, TOK]), sb("kT", [P, TOK])
        V = sb("v", [P, TT, P])
        ck, ckT, cv = sb("ck", [P, P]), sb("ckT", [P, P]), sb("cv", [P, P])
        kp = sb("k_prompt", [P, P])
        bias, window = sb("rel_bias", [P, 2, 2, DEC]), sb("window", [P, GRID_W])
        S = sb("scores", [P, 2, TOK])
        Pn = sb("probs", [P, 2, TOK])
        PT = sb("probs_T", [P, 2, TOK])
        neg, tot, inv = sb("neg_max", [P, 6]), sb("total", [P, 6]), sb("inv_total", [P, 6])
        units = [(h, t) for h in range(2) for t in range(TT)]
        w_loaded, c_loaded, b_loaded, win = R.sem("qkv_loaded"), R.sem("ctx_loaded"), R.sem("bias_loaded"), R.sem("win_loaded")
        stored, projected = R.sem("kv_stored"), R.sem("qkv_projected")
        proj_inc, proj_at = steps("qkv")
        pe_done = R.sem("attn_pe_done")
        pe_inc, pe_at = steps(["ck", "kp", "s0", "s1"]
                       + [x for u in range(6) for x in ([f"pt{u}", f"pv{u}"] + ([f"s{u + 2}"] if u + 2 < 6 else []))])
        act_done = R.sem("attn_act_done")
        act_inc, act_at = steps(["q", "k"] + [x for u in range(6) for x in (f"exp{u}", f"pt{u}")] + ["out"])
        dve_done = R.sem("attn_dve_done")
        dve_inc, dve_at = steps(["v", "ck", "kp", "bias"] + [x for u in range(6) for x in (f"s{u}", f"max{u}", f"inv{u}", f"p{u}")])
        w_in = R.I["na_w_in"][0].rearrange("(k p) n -> p k n", p=P)
        ckd = R.I["cache_na_k"][0, 0].rearrange("n h d -> n (h d)")
        cvd = R.I["cache_na_v"][0, 0].rearrange("n h d -> n (h d)")
        nk = R.O["new_k"][0, 0].rearrange("n h d -> n (h d)")
        nv = R.O["new_v"][0, 0].rearrange("n h d -> n (h d)")
        rel = R.I["na_rel_bias"]

        def weight_loads(sp, c):
            for m in range(3):
                sp.dma_start(W[:, m, :, :], w_in[:, :, 256 + 768 * m:1024 + 768 * m][:, :, bass.ds(c, P)]).then_inc(w_loaded, 16)

        def loads(sp, c):
            sp.dma_start(ck[:, :], ckd[:, bass.ds(c, P)]).then_inc(c_loaded, 16)
            sp.dma_start(cv[:, :], cvd[:, bass.ds(c, P)]).then_inc(c_loaded, 16)

        def bias_loads(sp, j):
            sp.dma_start(bias[:, :, :, :], R.bias_rows.rearrange("p (j n) -> p j n", j=PAIRS)[:, bass.ds(j, 1), :]
                         .rearrange("p a (h t n) -> p (a h) t n", h=2, t=2)).then_inc(b_loaded, 16)

        with nc.Block() as block:

            @block.sync
            def _(sp):
                sp.dma_start(window[:, :], const(R, "window")).then_inc(win, 16)
                weight_loads(sp, 0)
                loads(sp, 0)
                sp.wait_ge(R.bias_spread, 16 * ROWS * ROWS)
                bias_loads(sp, 0)
                sp.wait_ge(projected, proj_at("v", 0))
                weight_loads(sp, P)
                with sp.Fori(0, PAIRS - 2) as j:
                    nxt, cols, later = sp.snap(j + 1), sp.snap(j * P + P), sp.snap(j * P + 2 * P)
                    sp.wait_ge(pe_done, pe_at("pv5", j))
                    loads(sp, cols)
                    bias_loads(sp, nxt)
                    weight_loads(sp, later)
                sp.wait_ge(pe_done, pe_at("pv5", PAIRS - 2))
                loads(sp, (PAIRS - 1) * P)
                bias_loads(sp, PAIRS - 1)

            @block.gpsimd
            def _(pool):
                with pool.Fori(0, PAIRS) as j:
                    pool.wait_ge(dve_done, dve_at("kp", j))
                    pool.dma_start(nk[:, bass.ds(j * P, P)], kp[:, :]).then_inc(stored, 16)
                    pool.dma_start(nv[:, bass.ds(j * P, P)], V[:, 0, :]).then_inc(stored, 16)
                pool.wait_ge(stored, 32 * PAIRS)

            @block.tensor
            def _(pe):
                def project(i):
                    m, part = divmod(i, 4)
                    if m < 2:
                        for k in (2 * part, 2 * part + 1):
                            mm = nc.tensor.matmul(R.B[5 + m][:, 0:TOK], W[:, m, k, :], R.HT[:, k, :], start=(k == 0), stop=(k == KT - 1))
                    else:
                        for c in range(6 * part, 6 * part + 6):
                            t, k = divmod(c, KT)
                            mm = nc.tensor.matmul(R.B[7][:, t * P:(t + 1) * P], R.HT[:, k, t * P:(t + 1) * P], W[:, 2, k, :],
                                                  start=(k == 0), stop=(k == KT - 1))
                    if part == 3:
                        mm.then_inc(projected, proj_inc("qkv"[m]))

                pe.wait_ge(w_loaded, 48)
                for i in range(12):
                    project(i)

                def turn(j, more):
                    pe.wait_ge(c_loaded, 32 * j + 32)
                    nc.tensor.transpose(R.B[3][:, 0:P], ck[:, :], R.ident[:, :]).then_inc(pe_done, pe_inc("ck"))
                    pe.wait_ge(act_done, act_at("k", j))
                    nc.tensor.transpose(R.B[2][:, 0:P], kT[:, 0:SEQ], R.ident[:, :]).then_inc(pe_done, pe_inc("kp"))

                    def scores(u):
                        h, t = units[u]
                        rows = slice(64 * h, 64 * h + 64)
                        if u >= 2:
                            pe.wait_ge(dve_done, dve_at(f"s{u - 2}", j))
                        if t == 0:
                            mm = nc.tensor.matmul(R.B[u % 2][:, 0:SEQ], qT[rows, 0:SEQ], kT[rows, 0:SEQ], start=True, stop=True)
                        else:
                            q = qT[rows, t * P:(t + 1) * P]
                            nc.tensor.matmul(R.B[u % 2][:, 0:DEC], q, kT[rows, SEQ:TOK], start=True, stop=True)
                            mm = nc.tensor.matmul(R.B[u % 2][:, DEC:TOK], q, ckT[rows, :], start=True, stop=True)
                        mm.then_inc(pe_done, pe_inc(f"s{u}"))

                    pe.wait_ge(dve_done, dve_at("kp", j))
                    scores(0)
                    scores(1)
                    if more:
                        pe.wait_ge(w_loaded, 48 * j + 96)
                    for u, (h, t) in enumerate(units):
                        if more:
                            project(2 * u)
                        pe.wait_ge(dve_done, dve_at(f"p{u}", j))
                        blocks = 1 if t == 0 else 3
                        if u >= 2:
                            pe.wait_ge(act_done, act_at(f"pt{u - 2}", j))
                        for b in range(blocks):
                            mm = nc.tensor.transpose(R.B[2 + u % 2][:, b * P:(b + 1) * P], Pn[:, u % 2, b * P:(b + 1) * P], R.ident[:, :])
                        mm.then_inc(pe_done, pe_inc(f"pt{u}"))
                        if more:
                            project(2 * u + 1)
                        pe.wait_ge(act_done, act_at(f"pt{u}", j))
                        cols = slice(64 * h, 64 * h + 64)
                        values = [V[:, 0, cols]] if t == 0 else [V[:, 1, cols], V[:, 2, cols], cv[:, cols]]
                        for b, v in enumerate(values):
                            mm = nc.tensor.matmul(R.B[4][cols, t * P:(t + 1) * P], v, PT[:, u % 2, b * P:(b + 1) * P],
                                                  start=(b == 0), stop=(b == blocks - 1))
                        mm.then_inc(pe_done, pe_inc(f"pv{u}"))
                        if u + 2 < 6:
                            scores(u + 2)
                    pe.wait_ge(act_done, act_at("out", j))

                with pe.Fori(0, PAIRS - 1) as j:
                    turn(j, True)
                turn(PAIRS - 1, False)

            @block.scalar
            def _(act):
                with act.Fori(0, PAIRS) as j:
                    act.wait_ge(projected, proj_at("q", j))
                    nc.scalar.activation(qT[:, :], R.B[5][:, 0:TOK], ACT.Copy, scale=HD ** -0.5).then_inc(act_done, act_inc("q"))
                    act.wait_ge(projected, proj_at("k", j))
                    nc.scalar.activation(kT[:, :], R.B[6][:, 0:TOK], ACT.Copy).then_inc(act_done, act_inc("k"))
                    for u, (h, t) in enumerate(units):
                        n = SEQ if t == 0 else TOK
                        act.wait_ge(dve_done, dve_at(f"max{u}", j))
                        if u >= 2:
                            act.wait_ge(pe_done, pe_at(f"pt{u - 2}", j))
                        nc.scalar.activation(Pn[:, u % 2, 0:n], S[:, u % 2, 0:n], ACT.Exp, bias=neg[:, u:u + 1],
                                                           accum_out=tot[:, u:u + 1]).then_inc(act_done, act_inc(f"exp{u}"))
                        act.wait_ge(pe_done, pe_at(f"pt{u}", j))
                        if u >= 2:
                            act.wait_ge(pe_done, pe_at(f"pv{u - 2}", j))
                        nc.scalar.activation(PT[:, u % 2, 0:n], R.B[2 + u % 2][:, 0:n], ACT.Copy).then_inc(act_done, act_inc(f"pt{u}"))
                    act.wait_ge(pe_done, pe_at("pv5", j))
                    nc.scalar.activation(R.MT[:, :, :].rearrange("p k n -> p (k n)")[:, bass.ds(2 * TOK + j * TOK, TOK)],
                                                       R.B[4][:, 0:TOK], ACT.Copy).then_inc(act_done, act_inc("out"))
                    act.wait_ge(act_done, act_at("out", j))

            @block.vector
            def _(dve):
                dve.wait_ge(win, 16)
                with dve.Fori(0, PAIRS) as j:
                    dve.wait_ge(projected, proj_at("v", j))
                    nc.vector.tensor_copy(V[:, :, :], R.B[7][:, 0:TOK].rearrange("p (t n) -> p t n", t=TT)).then_inc(dve_done, dve_inc("v"))
                    dve.wait_ge(pe_done, pe_at("ck", j))
                    nc.vector.tensor_copy(ckT[:, :], R.B[3][:, 0:P]).then_inc(dve_done, dve_inc("ck"))
                    dve.wait_ge(pe_done, pe_at("kp", j))
                    nc.vector.tensor_copy(kp[:, :], R.B[2][:, 0:P]).then_inc(dve_done, dve_inc("kp"))
                    dve.wait_ge(b_loaded, 16 * j + 16)
                    flat = bias[:, :, :, :].rearrange("p h t (r k) -> p (h t r) k", k=GRID_W)
                    nc.vector.tensor_tensor(flat, flat, window[:, :].unsqueeze(1).broadcast_to([P, 16, GRID_W]), ALU.add).then_inc(dve_done, dve_inc("bias"))
                    dve.wait_ge(dve_done, dve_at("bias", j))

                    def scored(u):
                        h, t = units[u]
                        n = SEQ if t == 0 else TOK
                        dve.wait_ge(pe_done, pe_at(f"s{u}", j))
                        if u >= 2:
                            dve.wait_ge(act_done, act_at(f"exp{u - 2}", j))
                        if t == 0:
                            a = nc.vector.tensor_copy(S[:, u % 2, 0:n], R.B[u % 2][:, 0:n])
                        else:
                            nc.vector.tensor_tensor(S[:, u % 2, 0:DEC], R.B[u % 2][:, 0:DEC], bias[:, h, t - 1, :], ALU.add)
                            a = nc.vector.tensor_copy(S[:, u % 2, DEC:TOK], R.B[u % 2][:, DEC:TOK])
                        a.then_inc(dve_done, dve_inc(f"s{u}"))
                        dve.wait_ge(dve_done, dve_at(f"s{u}", j))
                        nc.vector.tensor_reduce(neg[:, u:u + 1], S[:, u % 2, 0:n], AX.X, ALU.max, negate=True).then_inc(dve_done, dve_inc(f"max{u}"))

                    def weighed(u):
                        n = SEQ if units[u][1] == 0 else TOK
                        dve.wait_ge(act_done, act_at(f"exp{u}", j))
                        nc.vector.reciprocal(inv[:, u:u + 1], tot[:, u:u + 1]).then_inc(dve_done, dve_inc(f"inv{u}"))
                        dve.wait_ge(dve_done, dve_at(f"inv{u}", j))
                        nc.vector.tensor_scalar(Pn[:, u % 2, 0:n], Pn[:, u % 2, 0:n], inv[:, u:u + 1], None, ALU.mult).then_inc(dve_done, dve_inc(f"p{u}"))

                    for u in range(6):
                        scored(u)
                        weighed(u)
                    dve.wait_ge(pe_done, pe_at("pv5", j))
                    dve.wait_ge(stored, 32 * j + 32)


def mixed(R, w_out, l):
    nc = R.nc
    stack, sb = local(R)
    with stack:
        W = sb(f"w_out{l}", [P, KT, D])
        Y = sb(f"gated{l}", [P, 6, BANK])
        loaded = [R.sem(f"w_out{l}_{q}") for q in range(4)]
        done, gated = R.sem(f"mixed_done{l}"), R.sem(f"mixed_gated{l}")
        with nc.Block() as block:

            @block.sync
            def _(sp):
                for q in range(4):
                    sp.dma_start(W[:, 2 * q:2 * q + 2, :], w_out[2 * q * P:(2 * q + 2) * P, :].rearrange("(k p) n -> p k n", p=P))\
                        .then_inc(loaded[q], 16)

            @block.tensor
            def _(pe):
                for t in range(TT):
                    for h in range(2):
                        for k in range(KT):
                            if t == 0 and h == 0 and k % 2 == 0:
                                pe.wait_ge(loaded[k // 2], 16)
                            mm = nc.tensor.matmul(R.B[2 * t + h][:, :], R.MT[:, k, t * P:(t + 1) * P], W[:, k, h * BANK:(h + 1) * BANK],
                                                  start=(k == 0), stop=(k == KT - 1))
                        mm.then_inc(done, 1)

            @block.vector
            def _(dve):
                for u in range(6):
                    t, h = divmod(u, 2)
                    dve.wait_ge(done, u + 1)
                    nc.vector.tensor_tensor(Y[:, u, :], R.B[u][:, :], R.mix_gate[:, min(t, 1), h * BANK:(h + 1) * BANK], ALU.mult)\
                        .then_inc(gated, 1)

            @block.gpsimd
            def _(pool):
                for u in range(6):
                    t, h = divmod(u, 2)
                    x = R.X[:, t, h * BANK:(h + 1) * BANK]
                    pool.wait_ge(gated, u + 1)
                    nc.gpsimd.tensor_tensor(x, x, Y[:, u, :], ALU.add)


def dense_ffn(R):
    nc = R.nc
    stack, sb = local(R)
    NF = FF // P
    with stack:
        W = sb("gate_up_w", [P, 2, 2, KT, P])
        G = sb("hidden", [P, NF, TOK])
        sil = sb("silu", [P, 2, TOK])
        WD = sb("down_w", [P, 4, 2, D])
        Y = sb("ffn_gated", [P, 6, BANK])
        loaded = [R.sem(f"gate_up_loaded{p}") for p in range(2)]
        tile_done, gate_free, up_free = R.sem("gate_up_done"), R.sem("gate_bank_free"), R.sem("up_bank_free")
        d_loaded = [R.sem(f"down_loaded{s}") for s in range(4)]
        d_used, done, gated = R.sem("down_used"), R.sem("down_done"), R.sem("ffn_was_gated")
        wg = R.I["ffn_w_gate"][0].rearrange("(k p) n -> p k n", p=P)
        wu = R.I["ffn_w_up"][0].rearrange("(k p) n -> p k n", p=P)
        acc = [R.B[(4 + i) % 8] for i in range(6)]
        with nc.Block() as block:

            @block.sync
            def _(sp):
                with sp.Fori(0, NF // 2) as i:
                    c = sp.snap(i * (2 * P))
                    for p in range(2):
                        sp.wait_ge(tile_done, 2 * i + p + 1)
                        for m, w in enumerate((wg, wu)):
                            sp.dma_start(W[:, p, m, :, :], w[:, :, bass.ds(c + p * P, P)]).then_inc(loaded[p], 16)

            @block.gpsimd
            def _(pool):
                for u in range(NF // 2):
                    if u >= 4:
                        pool.wait_ge(d_used, u - 3)
                    pool.dma_start(WD[:, u % 4, :, :], R.I["ffn_w_down"][0, 2 * u * P:(2 * u + 2) * P, :].rearrange("(k p) n -> p k n", p=P))\
                        .then_inc(d_loaded[u % 4], 16)
                for u in range(6):
                    t, h = divmod(u, 2)
                    x = R.X[:, t, h * BANK:(h + 1) * BANK]
                    pool.wait_ge(gated, u + 1)
                    nc.gpsimd.tensor_tensor(x, x, Y[:, u, :], ALU.add)

            @block.tensor
            def _(pe):
                pe.sem_inc(tile_done, 2)
                with pe.Fori(0, NF // 2) as i:
                    for p in range(2):
                        pe.wait_ge(loaded[p], 32 * i + 32)
                        pe.wait_ge(gate_free, 2 * i + p + 1)
                        pe.wait_ge(up_free, 2 * i + p + 1)
                        for m in range(2):
                            for k in range(KT):
                                mm = nc.tensor.matmul(R.B[2 * p + m][:, 0:TOK], W[:, p, m, k, :], R.HT[:, k, :],
                                                      start=(k == 0), stop=(k == KT - 1))
                        mm.then_inc(tile_done, 1)
                pe.wait_ge(up_free, 2 + NF)
                for f in range(NF):
                    if f % 2 == 0:
                        pe.wait_ge(d_loaded[f // 2 % 4], 16 * (f // 8 + 1))
                    for u in range(6):
                        t, h = divmod(u, 2)
                        mm = nc.tensor.matmul(acc[u][:, :], G[:, f, t * P:(t + 1) * P], WD[:, f // 2 % 4, f % 2, h * BANK:(h + 1) * BANK],
                                              start=(f == 0), stop=(f == NF - 1))
                        if f == NF - 1:
                            mm.then_inc(done, 1)
                        elif f % 2 == 1 and u == 5:
                            mm.then_inc(d_used, 1)

            @block.scalar
            def _(act):
                act.sem_inc(gate_free, 2)
                with act.Fori(0, NF // 2) as i:
                    for p in range(2):
                        act.wait_ge(tile_done, 2 * i + p + 3)
                        act.wait_ge(up_free, 2 * i + p + 1)
                        nc.scalar.activation(sil[:, p, :], R.B[2 * p][:, 0:TOK], ACT.Silu).then_inc(gate_free, 1)

            @block.vector
            def _(dve):
                dve.sem_inc(up_free, 2)
                with dve.Fori(0, NF // 2) as i:
                    for p in range(2):
                        dve.wait_ge(gate_free, 2 * i + p + 3)
                        nc.vector.tensor_tensor(G[:, :, :].rearrange("p f n -> p (f n)")[:, bass.ds(i * (2 * TOK) + p * TOK, TOK)],
                                                sil[:, p, :], R.B[2 * p + 1][:, 0:TOK], ALU.mult).then_inc(up_free, 1)
                for u in range(6):
                    t, h = divmod(u, 2)
                    dve.wait_ge(done, u + 1)
                    nc.vector.tensor_tensor(Y[:, u, :], acc[u][:, :], R.ffn_gate[:, min(t, 1), h * BANK:(h + 1) * BANK], ALU.mult)\
                        .then_inc(gated, 1)


def layer1(R):
    stack, sb = local(R)
    with stack:
        R.mix_gate = sb("mix_gate_rows1", [P, 2, D])
        modulation(R, 1, R.mix_gate)
        normed(R, 2)
        R.MT = sb("mixed_by_channel1", [P, KT, TOK])
        inner, sb1 = local(R)
        with inner:
            R.params = sb1("pair_params", [P, N_PARAMS, PAIRS])
            R.lora = sb1("lora_in", [P, 3, TOK])
            pool_lora(R)
            rwkv(R)
        mixed(R, R.I["rw_w_out"][0], 1)
    normed(R, 3)


PARAMS = ("w0_f", "w0_b", "a0_f", "a0_b", "k_k", "k_a", "r_k", "gn_w", "gn_b", "prev_r", "prev_k", "prev_v",
          "next_r", "next_k", "next_v", "self_r", "self_k", "self_v", "half_w0_f", "half_w0_b", "half_a0_f", "half_a0_b",
          "one_less_k_a")
N_PARAMS = len(PARAMS)
PAD = 16
PADDED = PAD + SEQ + PAD + DEC + PAD
LINE = TOK + 3
STREAMS = ((0, SEQ, 0), (SEQ, TOK, 1))


def pool_lora(R):
    nc = R.nc
    stack, sb = local(R)
    with stack:
        W = sb("pool_lora_w", [P, KT, 640])
        rows = sb("scan_rows", [96, P])
        cols = sb("scan_cols", [P, 96])
        inv = sb("inv_count", [P, 2, TOK])
        GW = sb("pool_w_pairs", [P, 2, P])
        xs = [sb(f"pool_sum{w}", [P, 2, PADDED]) for w in (1,) + POOL_WINDOWS]
        mean, dif = sb("pool_mean", [P, 2, TOK]), sb("pool_diff", [P, 2, TOK])
        raw, mid, own = sb("lora_raw", [P, 3, LINE]), sb("lora_mid", [P, 3, LINE - 2]), sb("lora_self", [P, 3])
        z = sb("lora_shifted", [P, 3, TOK])
        w_in = [R.sem(f"pool_lora_w{i}") for i in range(2)]
        r_in, t_in, g_in = R.sem("scan_rows_in"), R.sem("inv_count_in"), R.sem("pool_w_in")
        pe_done = R.sem("pl_pe_done")
        pe_inc, pe_at = steps(["rows"] + [f"m{m}" for m in range(5)] + ["pool0", "pool1"])
        act_done = R.sem("pl_act_done")
        act_inc, act_at = steps(["rows"] + [f"m{m}" for m in range(5)])
        dve_done = R.sem("pl_dve_done")
        dve_inc, dve_at = steps(["zero", "self", "params", "mid0", "mid1", "z", "s2", "s4", "s8", "s16", "mean", "dif"])
        w = R.I["rw_w_in"][0].rearrange("(k p) n -> p k n", p=P)
        with nc.Block() as block:

            @block.sync
            def _(sp):
                q = 0

                def put(a):
                    nonlocal q
                    n = a.shape[0] // P
                    sp.dma_start(rows[q:q + n, :], a.rearrange("(r p) -> r p", p=P)).then_inc(r_in, 16)
                    q += n

                for name in ("decay_w0", "iclr_a0"):
                    put(R.I[name][0].rearrange("d n -> (d n)"))
                for name in ("k_k", "k_a"):
                    put(R.I[name][0])
                put(R.I["r_k"][0].rearrange("h d -> (h d)"))
                put(R.I["gn_w"][0])
                put(R.I["gn_b"][0])
                for d in range(2):
                    put(R.I["shift_mu"][0, d, 0:3 * 768])
                for d in range(2):
                    put(R.I["shift_mu"][0, d, 3 * 768:3 * 768 + 384])
                assert q == 96
                sp.dma_start(W[:, :, 256:640], w[:, :, 256 + 2304:256 + 2304 + 384]).then_inc(w_in[0], 16)
                sp.dma_start(W[:, :, 0:256], w[:, :, 0:256]).then_inc(w_in[1], 16)
                sp.dma_start(inv[:, :, :], const(R, "inv_count").rearrange("p (a n) -> p a n", a=2)).then_inc(t_in, 16)
                sp.wait_ge(dve_done, dve_at("zero"))
                for g in range(4):
                    h = slice(64 * (g % 2), 64 * (g % 2) + 64)
                    sp.dma_start(GW[h, g // 2, h], R.I["pool_w"][0, g]).then_inc(g_in, 16)

            @block.tensor
            def _(pe):
                pe.wait_ge(r_in, 16 * 11)
                nc.tensor.transpose(R.B[7][:, 0:96], rows[:, :], R.ident[0:96, 0:96]).then_inc(pe_done, pe_inc("rows"))
                for n, m in enumerate((2, 3, 4, 0, 1)):
                    if n in (0, 3):
                        pe.wait_ge(w_in[n // 3], 16)
                    for k in range(KT):
                        mm = nc.tensor.matmul(R.B[n][:, 0:TOK], W[:, k, m * P:(m + 1) * P], R.HT[:, k, :], start=(k == 0), stop=(k == KT - 1))
                    mm.then_inc(pe_done, pe_inc(f"m{n}"))
                pe.wait_ge(g_in, 64)
                pe.wait_ge(dve_done, dve_at("dif"))
                for m in range(2):
                    nc.tensor.matmul(R.B[5 + m][:, 0:TOK], GW[:, m, :], dif[:, m, :], start=True, stop=True).then_inc(pe_done, pe_inc(f"pool{m}"))

            @block.scalar
            def _(act):
                act.wait_ge(pe_done, pe_at("rows"))
                nc.scalar.activation(cols[:, :], R.B[7][:, 0:96], ACT.Copy).then_inc(act_done, act_inc("rows"))
                act.wait_ge(dve_done, dve_at("zero"))
                for n in range(5):
                    act.wait_ge(pe_done, pe_at(f"m{n}"))
                    for a, b, s in STREAMS:
                        out = raw[:, n, 1 + a + s:1 + b + s] if n < 3 else xs[0][:, n - 3, PAD * (1 + s) + a:PAD * (1 + s) + b]
                        i = nc.scalar.activation(out, R.B[n][:, a:b], ACT.Copy)
                    i.then_inc(act_done, act_inc(f"m{n}"))
                act.wait_ge(dve_done, dve_at("z"))
                nc.scalar.activation(R.lora[:, 0, :], z[:, 0, :], ACT.Tanh)
                nc.scalar.activation(R.lora[:, 1, :], z[:, 1, :], ACT.Copy)
                nc.scalar.activation(R.lora[:, 2, :], z[:, 2, :], ACT.Sigmoid)
                for m in range(2):
                    act.wait_ge(pe_done, pe_at(f"pool{m}"))
                    nc.scalar.activation(R.MT[:, m, :], R.B[5 + m][:, 0:TOK], ACT.Copy, scale=R.VT[:, 48 + m:49 + m])

            @block.vector
            def _(dve):
                nc.vector.memset(raw[:, :, :], 0.0)
                nc.vector.memset(GW[:, :, :], 0.0)
                nc.vector.memset(xs[0][:, :, :], 0.0).then_inc(dve_done, dve_inc("zero"))
                dve.wait_ge(act_done, act_at("rows"))
                par = R.params
                flat = par[:, :, :].rearrange("p q j -> p (q j)")
                nc.vector.tensor_copy(flat[:, 0:90], cols[:, 0:90])
                nc.vector.tensor_scalar(flat[:, 108:132], cols[:, 0:24], 0.5, None, ALU.mult)
                nc.vector.tensor_scalar(flat[:, 132:138], cols[:, 30:36], -1.0, 1.0, ALU.mult, ALU.add)
                nc.vector.tensor_tensor(flat[:, 90:108], cols[:, 54:72], cols[:, 72:90], ALU.add)
                nc.vector.tensor_tensor(own[:, :], cols[:, 90:93], cols[:, 93:96], ALU.add).then_inc(dve_done, dve_inc("self"))
                dve.wait_ge(dve_done, dve_at("self"))
                nc.vector.tensor_scalar(flat[:, 90:108], flat[:, 90:108], -1.0, 1.0, ALU.mult, ALU.add)
                nc.vector.tensor_scalar(own[:, :], own[:, :], -1.0, 1.0, ALU.mult, ALU.add).then_inc(dve_done, dve_inc("params"))
                dve.wait_ge(dve_done, dve_at("params"))
                dve.wait_ge(act_done, act_at("m2"))
                for m in range(3):
                    i = nc.vector.tensor_scalar(mid[:, m, :], raw[:, m, 1:LINE - 1], own[:, m:m + 1], None, ALU.mult)
                i.then_inc(dve_done, dve_inc("mid0"))
                dve.wait_ge(dve_done, dve_at("mid0"))
                for m in range(3):
                    i = nc.vector.scalar_tensor_tensor(out=mid[:, m, :], in0=raw[:, m, 0:LINE - 2], scalar=cols[:, 90 + m:91 + m],
                                                       in1=mid[:, m, :], op0=ALU.mult, op1=ALU.add)
                i.then_inc(dve_done, dve_inc("mid1"))
                dve.wait_ge(dve_done, dve_at("mid1"))
                for m in range(3):
                    for a, b, s in STREAMS:
                        i = nc.vector.scalar_tensor_tensor(out=z[:, m, a:b], in0=raw[:, m, 2 + a + s:2 + b + s], scalar=cols[:, 93 + m:94 + m],
                                                           in1=mid[:, m, a + s:b + s], op0=ALU.mult, op1=ALU.add)
                i.then_inc(dve_done, dve_inc("z"))
                dve.wait_ge(act_done, act_at("m4"))
                prev, lo, hi = xs[0], 0, PADDED
                for i, wd in enumerate(POOL_WINDOWS):
                    a, b = (1, 0) if wd == 2 else (wd // 4, wd // 4)
                    lo, hi = lo + a, hi - b
                    nc.vector.tensor_tensor(xs[i + 1][:, :, lo:hi], xs[i][:, :, lo - a:hi - a], xs[i][:, :, lo + b:hi + b], ALU.add).then_inc(dve_done, dve_inc(f"s{wd}"))
                    dve.wait_ge(dve_done, dve_at(f"s{wd}"))
                dve.wait_ge(t_in, 16)
                for g in range(4):
                    h = slice(64 * (g % 2), 64 * (g % 2) + 64)
                    for a, b, s in STREAMS:
                        o = PAD * (1 + s)
                        i = nc.vector.tensor_tensor(mean[h, g // 2, a:b], xs[g + 1][h, g // 2, o + a:o + b], inv[h, g // 2, a:b], ALU.mult)
                i.then_inc(dve_done, dve_inc("mean"))
                dve.wait_ge(dve_done, dve_at("mean"))
                for a, b, s in STREAMS:
                    o = PAD * (1 + s)
                    i = nc.vector.tensor_tensor(dif[:, :, a:b], mean[:, :, a:b], xs[0][:, :, o + a:o + b], ALU.subtract)
                i.then_inc(dve_done, dve_inc("dif"))


CHAINS = [(1, 0, [2, 3, 4, 5], 3), (1, 1, [5, 4, 3, 2], 3), (0, 0, [0, 1], 0), (0, 1, [1, 0], 0)]
SLOTS = 8
CHAIN_STEPS = [(s, n) for s in range(4) for n, ch in enumerate(CHAINS) if s < len(ch[2])]


def before_slot(d, chunk):
    return next(first + chunks.index(chunk) for _, dr, chunks, first in CHAINS if dr == d and chunk in chunks)


def rwkv(R):
    nc = R.nc
    stack, sb = local(R)
    with stack:
        W = sb("rkv_w", [P, 3, KT, P])
        up = sb("lora_up", [P, 3, P])
        s0 = sb("state_in", [HD, 2, 2, HD])
        masks = sb("scan_masks", [P, 2, 8, P])
        halves, chunk = sb("same_head", [P, P]), sb("chunk_starts", [P, TOK])
        par, par_next = sb("params_now", [P, N_PARAMS]), sb("params_next", [P, N_PARAMS])
        raw, mid, z = sb("rkv_raw", [P, 3, LINE]), sb("rkv_mid", [P, 3, LINE - 2]), sb("rkv", [P, 3, TOK])
        lw, a, g = sb("log_decay", [P, 2, TOK]), sb("in_rate", [P, 2, TOK]), sb("out_gate", [P, TOK])
        L, D0, D1 = sb("log_sum", [P, 2, TOK]), sb("before_own", [P, 2, TOK]), sb("after_own", [P, 2, TOK])
        E12 = sb("decay_before_and_to", [P, 2, 2, TOK])
        E1, E2 = E12[:, 0], E12[:, 1]
        E3, E4 = (sb(n, [P, 2, TOK]) for n in ("growth", "decay_after"))
        ET = sb("chunk_decay", [P, 2, NCH])
        kkr, sq, nrm, kk = (sb(n, [P, TOK]) for n in ("kk_raw", "kk_sq", "kk_norm", "kk"))
        rn = nrm
        km, nka = sb("k_mod", [P, 2, TOK]), sb("neg_kk_a", [P, 2, TOK])
        ka, rh, be, kt = E1, E2, sb("beta", [P, 2, 2, TOK]), sb("k_grown", [P, 2, 2, TOK])
        Kc, Bc = L, lw
        TM = sb("token_major", [P, TT, 7, P])
        LB = TM[:, 0, 0:3, :].rearrange("p q n -> p (q n)")
        AT, Q1, BT, Q2, T, TI, XM = (sb(n, [P, TT, 4, P]) for n in ("A_T", "Q1_T", "B_T", "Q2_T", "inv", "inv_T", "masked"))
        BV = km[:, :, :].rearrange("p a n -> p (a n)").rearrange("p (t q n) -> p t q n", t=TT, q=4)
        U = nka[:, :, :].rearrange("p a n -> p (a n)").rearrange("p (t d h n) -> p t d h n", t=TT, d=2, h=2)
        NN = T[:, :, :, :].rearrange("p t q n -> p (t q n)")[:, 0:TT * 4 * HD].rearrange("p (t q n) -> p t q n", t=TT, q=4)
        MX = E3[:, :, :].rearrange("p a n -> p (a n)").rearrange("p (t d n) -> p t d n", t=TT, d=2)
        ST = sb("states", [P, 2, SLOTS, HD])
        OS, so = E4[:, 0, :], sb("state_out", [HD, 2, P])
        rk, bonus, y = D0, D1, mid
        B = R.B
        w_in, up_in, s_in, c_in, stored = (R.sem(n) for n in ("rkv_w_in", "lora_up_in", "state_in_loaded", "scan_consts_in", "state_stored"))
        NL = len(LEVELS)
        lvl = [(l, t) for l in range(NL) for t in range(TT)]
        projected, wv_in, raw_ready = R.sem("rkv_projected"), R.sem("v_w_in"), R.sem("rkv_raw_ready")
        (proj_inc, proj_at), (raw_inc, raw_at) = steps("rkv"), steps("rkv")
        RAW_BANK = (6, 7, 0)
        early = R.sem("rk_prepared")
        early_inc, early_at = steps(["par", "z0", "z1", "z", "kkr"])
        pe_done = R.sem("scan_pe_done")
        pe_inc, pe_at = steps(["dec0", "dec1", "rate0", "rate1", "gate", "s0", "norm"]
                       + [f"{n}{t}" for t in range(TT) for n in "ab"]
                       + [f"t0_{t}" for t in range(TT)] + [f"tm{t}{i}" for t in range(TT) for i in "ab"]
                       + [f"{x}{l}_{t}" for l in range(NL) for x in ("x", "w", "tr") for t in range(TT) if (x, l) != ("tr", NL - 1)]
                       + [f"{n}{t}" for t in range(TT) for n in ("bv", "mx")]
                       + [f"nn{t}" for t in range(TT)]
                       + [f"{x}{s}_{n}" for s in range(4) for x in "us" for n in range(4) if (s, n) in CHAIN_STEPS]
                       + ["out", "mean", "var", "bonus", "states"])
        act_done = R.sem("scan_act_done")
        act_inc, act_at = steps(["th0", "th1", "lw", "rate0", "rate1", "a", "fac", "gate", "s0", "exp", "root"]
                        + [f"t0_{t}" for t in range(TT)] + [f"tm{t}{i}" for t in range(TT) for i in "ab"]
                        + [f"tr{l}_{t}" for l, t in lvl if l < NL - 1]
                        + [f"{n}{t}" for t in range(TT) for n in ("bv", "mx")]
                        + [f"nn{t}" for t in range(TT)] + ["out", "root2", "states"])
        dve_done = R.sem("scan_dve_done")
        dve_inc, dve_at = steps(["par", "z0v", "z1v", "zv", "sq", "L", "D", "LB", "norm", "rn", "kk", "km", "nka", "ops"]
                        + [x for t in range(TT) for x in (f"at{t}", f"q1{t}", f"bt{t}", f"q2{t}", f"m{t}", f"ti{t}")]
                        + [x for l in range(NL) for x in [f"xm{l}_{t}" for t in range(TT)] + [f"up{l}_{t}" for t in range(TT)]]
                        + [f"{x}{s}_{n}" for s in range(4) for x in "us" for n in range(4) if (s, n) in CHAIN_STEPS]
                        + ["d", "dd", "var", "rstd", "yn", "yw", "bonus", "yb", "y"])
        pool_done = R.sem("scan_pool_done")
        pool_inc, pool_at = steps(["zero", "ops", "rk0", "rk"])
        w_dram = R.I["rw_w_in"][0].rearrange("(k p) n -> p k n", p=P)
        ups = [R.I[n][0].rearrange("d l n -> (d l) n") for n in ("decay_up", "iclr_up")] + [R.I["gate_up"][0]]
        st_in = R.I["state_wkv"][0, 0].rearrange("d h v k -> v d h k")
        st_out = R.O["new_state"][0, 0].rearrange("d h v k -> v d h k")
        of = lambda name, par=par: par[:, PARAMS.index(name):PARAMS.index(name) + 1]
        four = lambda ap: ap.rearrange("p (q n) -> p q n", q=4)
        score_bank = lambda t, i, h: B[(4 * t + 2 * i + h) % 6]
        two = lambda ap: ap.unsqueeze(1).broadcast_to([P, 2, TOK])

        def weight_loads(q, c, ms):
            for m in ms:
                q.dma_start(W[:, m, :, :], w_dram[:, :, 256 + 768 * m:1024 + 768 * m][:, :, bass.ds(c, P)]).then_inc(w_in if m < 2 else wv_in, 16)

        def loads(q, c, h):
            for m in range(3):
                q.dma_start(up[:, m, :], ups[m][:, bass.ds(c, P)]).then_inc(up_in, 16)
            for d in range(2):
                q.dma_start(s0[:, d, :, :], st_in[:, d, bass.ds(h, 2), :]).then_inc(s_in, 16)

        with nc.Block() as block:

            @block.sync
            def _(sp):
                weight_loads(sp, 0, range(3))
                loads(sp, 0, 0)
                sp.dma_start(masks[:, :, :, :], const(R, "masks").rearrange("p (d i n) -> p d i n", d=2, i=8)).then_inc(c_in, 16)
                sp.dma_start(halves[:, :], const(R, "halves")).then_inc(c_in, 16)
                sp.dma_start(chunk[:, :], const(R, "chunk")).then_inc(c_in, 16)
                sp.wait_ge(projected, proj_at("v", 0))
                weight_loads(sp, P, range(3))
                with sp.Fori(0, PAIRS - 2) as j:
                    c, h, later = sp.snap(j * P + P), sp.snap(j * 2 + 2), sp.snap(j * P + 2 * P)
                    sp.wait_ge(pe_done, pe_at("s0", j))
                    loads(sp, c, h)
                    sp.wait_ge(projected, proj_at("k", j + 1))
                    weight_loads(sp, later, (0, 1))
                    sp.wait_ge(projected, proj_at("v", j + 1))
                    weight_loads(sp, later, (2,))
                sp.wait_ge(pe_done, pe_at("s0", PAIRS - 2))
                loads(sp, (PAIRS - 1) * P, (PAIRS - 1) * 2)

            @block.gpsimd
            def _(pool):
                with pool.Fori(0, PAIRS) as j:
                    nc.gpsimd.memset(ST[:, :, 0, :], 0.0).then_inc(pool_done, pool_inc("zero"))
                    pool.wait_ge(dve_done, dve_at("nka", j))
                    pool.wait_ge(act_done, act_at("exp", j))
                    nc.gpsimd.tensor_tensor(Kc[:, :, :], km[:, :, :], E4[:, :, :], ALU.mult)
                    nc.gpsimd.tensor_tensor(Bc[:, :, :], nka[:, :, :], E4[:, :, :], ALU.mult).then_inc(pool_done, pool_inc("ops"))
                    pool.wait_ge(dve_done, dve_at("ops", j))
                    pool.sem_inc(R.passed, 1)
                    nc.gpsimd.tensor_scalar(rk[:, 0, :], z[:, 0, :], of("r_k"), None, ALU.mult).then_inc(pool_done, pool_inc("rk0"))
                    pool.wait_ge(pool_done, pool_at("rk0", j))
                    nc.gpsimd.tensor_tensor(rk[:, 0, :], rk[:, 0, :], z[:, 1, :], ALU.mult).then_inc(pool_done, pool_inc("rk"))
                    pool.wait_ge(act_done, act_at("states", j))
                    for d in range(2):
                        pool.dma_start(st_out[:, d, bass.ds(j * 2, 2), :], so[:, d, :].rearrange("v (h k) -> v h k", h=2)).then_inc(stored, 16)
                    pool.wait_ge(dve_done, dve_at("y", j))
                    pool.wait_ge(pe_done, pe_at("states", j))
                pool.wait_ge(stored, 32 * PAIRS)

            @block.tensor
            def _(pe):

                def project(m, ks=range(KT)):
                    for k in ks:
                        mm = nc.tensor.matmul(B[RAW_BANK[m]][:, 0:TOK], W[:, m, k, :], R.HT[:, k, :], start=(k == 0), stop=(k == KT - 1))
                    if k == KT - 1:
                        mm.then_inc(projected, proj_inc("rkv"[m]))

                def turn(j, more):
                    pe.wait_ge(up_in, 48 * j + 48)
                    for m, name in enumerate(("dec", "rate")):
                        for d in range(2):
                            h = slice(64 * d, 64 * d + 64)
                            nc.tensor.matmul(B[3 + 2 * m + d][:, 0:TOK], up[h, m, :], R.lora[h, m, :], start=True, stop=True).then_inc(pe_done, pe_inc(f"{name}{d}"))
                    nc.tensor.matmul(B[7][:, 0:TOK], up[:, 2, :], R.lora[:, 2, :], start=True, stop=True).then_inc(pe_done, pe_inc("gate"))
                    pe.wait_ge(s_in, 32 * j + 32)
                    pe.wait_ge(raw_ready, raw_at("v", j))
                    pe.sem_inc(R.passed, 1)
                    for d in range(2):
                        mm = nc.tensor.transpose(B[0][:, d * HD:(d + 1) * HD], s0[:, d, :, :].rearrange("v h k -> v (h k)"), R.ident[0:HD, 0:HD])
                    mm.then_inc(pe_done, pe_inc("s0"))
                    if more:
                        pe.wait_ge(w_in, 32 * j + 64)
                        pe.wait_ge(act_done, act_at("rate1", j))
                        project(0)
                    pe.wait_ge(dve_done, dve_at("sq", j))
                    nc.tensor.matmul(B[1][:, 0:TOK], halves[:, :], sq[:, :], start=True, stop=True).then_inc(pe_done, pe_inc("norm"))
                    if more:
                        pe.wait_ge(act_done, act_at("gate", j))
                        project(1)
                    pe.wait_ge(dve_done, dve_at("ops", j))
                    pe.wait_ge(act_done, act_at("gate", j))
                    for t in range(TT):
                        cols = slice(t * P, (t + 1) * P)
                        for i, left in enumerate((be, kt)):
                            if 2 * t + i >= 3:
                                pe.wait_ge(dve_done, dve_at(f"{('q1', 'q2')[(2 * t + i - 3) % 2]}{(2 * t + i - 3) // 2}", j))
                            for h in range(2):
                                out = score_bank(t, i, h).rearrange("p (m d n) -> p m d n", m=2, d=2)
                                for d in range(2):
                                    mm = nc.tensor.matmul(out[:, :, d, :], left[:, h, d, cols], E12[:, :, d, cols], start=True, stop=True)
                            mm.then_inc(pe_done, pe_inc(f"{('a', 'b')[i]}{t}"))
                    for t in range(TT):
                        pe.wait_ge(dve_done, dve_at(f"ti{t}", j))
                        if t == 0:
                            pe.wait_ge(dve_done, dve_at("q22", j))
                        for q in range(4):
                            mm = nc.tensor.transpose(B[t][:, q * P:(q + 1) * P], TI[:, t, q, :], R.ident[:, :])
                        mm.then_inc(pe_done, pe_inc(f"t0_{t}"))
                    pe.wait_ge(pool_done, pool_at("ops", j))
                    if more:
                        pe.wait_ge(raw_ready, raw_at("k", j + 1))
                    for t in range(TT):
                        cols = slice(t * P, (t + 1) * P)
                        for i, srcs in enumerate(([ka[:, 0, cols], ka[:, 1, cols], Kc[:, 0, cols], Kc[:, 1, cols]],
                                                  [Bc[:, 0, cols], Bc[:, 1, cols], z[:, 2, cols]])):
                            if t:
                                pe.wait_ge(act_done, act_at(f"tm{t - 1}{'ab'[i]}", j))
                            for n, src in enumerate(srcs):
                                mm = nc.tensor.transpose(B[6 + i][:, n * P:(n + 1) * P], src, R.ident[:, :])
                            mm.then_inc(pe_done, pe_inc(f"tm{t}{'ab'[i]}"))
                    for l in range(NL):
                        for t in range(TT):
                            pe.wait_ge(act_done, act_at(f"tr{l - 1}_{t}" if l else f"t0_{t}", j))
                            for q in range(4):
                                mm = nc.tensor.matmul(B[t][:, q * P:(q + 1) * P], AT[:, t, q, :], T[:, t, q, :], start=True, stop=True)
                            mm.then_inc(pe_done, pe_inc(f"x{l}_{t}"))
                        for t in range(TT):
                            pe.wait_ge(dve_done, dve_at(f"xm{l}_{t}", j))
                            for q in range(4):
                                left, right = (TI, XM) if l < NL - 1 else (XM, TI)
                                mm = nc.tensor.matmul(B[3 + t][:, q * P:(q + 1) * P], left[:, t, q, :], right[:, t, q, :], start=True, stop=True)
                            mm.then_inc(pe_done, pe_inc(f"w{l}_{t}"))
                        if l < NL - 1:
                            for t in range(TT):
                                pe.wait_ge(dve_done, dve_at(f"up{l}_{t}", j))
                                for q in range(4):
                                    mm = nc.tensor.transpose(B[t][:, q * P:(q + 1) * P], T[:, t, q, :], R.ident[:, :])
                                mm.then_inc(pe_done, pe_inc(f"tr{l}_{t}"))
                    for t in range(TT):
                        pe.wait_ge(dve_done, dve_at(f"up{NL - 1}_{t}", j))
                        pe.wait_ge(act_done, act_at(f"tm{t}b", j))
                        for q in range(4):
                            h = slice(64 * (q % 2), 64 * (q % 2) + 64)
                            mm = nc.tensor.matmul(B[t][:, q * HD:(q + 1) * HD], BT[:, t, q, :], TM[:, t, 6, h], start=True, stop=True)
                        mm.then_inc(pe_done, pe_inc(f"bv{t}"))
                        for q in range(4):
                            h = slice(64 * (q % 2), 64 * (q % 2) + 64)
                            mm = nc.tensor.matmul(B[3 + t][h, (q // 2) * P:(q // 2 + 1) * P], TM[:, t, q // 2, h], TI[:, t, q, :], start=True, stop=True)
                        mm.then_inc(pe_done, pe_inc(f"mx{t}"))
                    for t in range(TT):
                        pe.wait_ge(act_done, act_at(f"bv{t}", j))
                        for q in range(4):
                            mm = nc.tensor.matmul(B[t][:, (4 + q) * HD:(5 + q) * HD], TI[:, t, q, :], BV[:, t, q, :], start=True, stop=True)
                        mm.then_inc(pe_done, pe_inc(f"nn{t}"))
                    pe.wait_ge(act_done, act_at("nn2", j))
                    pe.wait_ge(pool_done, pool_at("zero", j))
                    for s in range(4):
                        now = [n for n in range(4) if (s, n) in CHAIN_STEPS]
                        for n in now:
                            _, d, chunks, first = CHAINS[n]
                            t, cp = divmod(chunks[s], 2)
                            c = slice(64 * cp, 64 * cp + 64)
                            if s:
                                pe.wait_ge(dve_done, dve_at(f"s{s - 1}_{n}", j))
                                pe.sem_inc(R.passed, 1)
                            else:
                                pe.wait_ge(act_done, act_at("nn2", j))
                                pe.sem_inc(R.passed, 1)
                            for h in range(2):
                                hr = slice(64 * h, 64 * h + 64)
                                mm = nc.tensor.matmul(B[2 * n + h][c, 0:HD], MX[hr, t, d, c], ST[hr, d, first + s, :], start=True, stop=True)
                            mm.then_inc(pe_done, pe_inc(f"u{s}_{n}"))
                        for n in now:
                            _, d, chunks, first = CHAINS[n]
                            t, cp = divmod(chunks[s], 2)
                            c = slice(64 * cp, 64 * cp + 64)
                            pe.wait_ge(dve_done, dve_at(f"u{s}_{n}", j))
                            pe.sem_inc(R.passed, 1)
                            for h in range(2):
                                hr = slice(64 * h, 64 * h + 64)
                                out = B[2 * n][hr, 2 * HD:3 * HD]
                                nc.tensor.matmul(out, TM[c, t, 2 + d, hr], TM[c, t, 6, hr], start=True, stop=False)
                                mm = nc.tensor.matmul(out, TM[c, t, 4 + d, hr], U[c, t, d, h, :], start=False, stop=True)
                            mm.then_inc(pe_done, pe_inc(f"s{s}_{n}"))
                    for n in range(4):
                        pe.wait_ge(dve_done, dve_at(f"s{len(CHAINS[n][2]) - 1}_{n}", j))
                    for t in range(TT):
                        for h in range(2):
                            hr = slice(64 * h, 64 * h + 64)
                            for d in range(2):
                                q = 2 * d + h
                                out = B[4][hr, t * P:(t + 1) * P]
                                nc.tensor.matmul(out, TM[:, t, 6, hr], Q2[:, t, q, :], start=(d == 0), stop=False)
                                nc.tensor.matmul(out, U[:, t, d, h, :], Q1[:, t, q, :], start=False, stop=False)
                                for cp in range(2):
                                    ch = 2 * t + cp
                                    mm = nc.tensor.matmul(B[4][hr, ch * C:(ch + 1) * C], ST[hr, d, before_slot(d, ch), :],
                                                          rh[hr, d, ch * C:(ch + 1) * C], start=False, stop=(d == 1 and cp == 1))
                    mm.then_inc(pe_done, pe_inc("out"))
                    if more:
                        pe.wait_ge(wv_in, 16 * j + 32)
                        project(2, range(4))
                    pe.wait_ge(act_done, act_at("out", j))
                    nc.tensor.matmul(B[5][:, 0:TOK], halves[:, :], OS[:, :], start=True, stop=True).then_inc(pe_done, pe_inc("mean"))
                    if more:
                        project(2, range(4, KT))
                    pe.wait_ge(dve_done, dve_at("dd", j))
                    nc.tensor.matmul(B[4][:, 0:TOK], halves[:, :], sq[:, :], start=True, stop=True).then_inc(pe_done, pe_inc("var"))
                    pe.wait_ge(pool_done, pool_at("rk", j))
                    nc.tensor.matmul(B[6][:, 0:TOK], halves[:, :], rk[:, 0, :], start=True, stop=True).then_inc(pe_done, pe_inc("bonus"))
                    for d in range(2):
                        mm = nc.tensor.transpose(B[7][0:HD, d * P:(d + 1) * P], ST[:, d, 2, :], R.ident[:, :])
                    mm.then_inc(pe_done, pe_inc("states"))
                    pe.wait_ge(dve_done, dve_at("y", j))
                    pe.wait_ge(act_done, act_at("states", j))

                pe.wait_ge(w_in, 32)
                pe.wait_ge(wv_in, 16)
                for m in range(3):
                    project(m)
                pe.wait_ge(c_in, 48)
                pe.wait_ge(raw_ready, raw_at("v", 0))
                with pe.Fori(0, PAIRS - 1) as j:
                    turn(j, True)
                turn(PAIRS - 1, False)

            @block.scalar
            def _(act):
                def copy_raw(m, j):
                    act.wait_ge(projected, proj_at("rkv"[m], j))
                    for a0, b0, s in STREAMS:
                        i = nc.scalar.activation(raw[:, m, 1 + a0 + s:1 + b0 + s], B[RAW_BANK[m]][:, a0:b0], ACT.Copy)
                    i.then_inc(raw_ready, raw_inc("rkv"[m]))

                def turn(j, more):
                    act.wait_ge(dve_done, dve_at("par", j))
                    for m, (name, dst, ev) in enumerate((("dec", lw, "th"), ("rate", a, "rate"))):
                        for d in range(2):
                            act.wait_ge(pe_done, pe_at(f"{name}{d}", j))
                            nc.scalar.activation(dst[:, d, :], B[3 + 2 * m + d][:, 0:TOK], ACT.Tanh, scale=0.5,
                                                               bias=of(("half_w0_", "half_a0_")[m] + "fb"[d])).then_inc(act_done, act_inc(f"{ev}{d}"))
                        act.wait_ge(act_done, act_at(f"{ev}1", j))
                        if m == 0:
                            nc.scalar.activation(lw[:, :, :], lw[:, :, :], ACT.Copy, scale=-DECAY / 2, bias=-DECAY / 2).then_inc(act_done, act_inc("lw"))
                        else:
                            nc.scalar.activation(a[:, :, :], a[:, :, :], ACT.Copy, scale=0.5, bias=0.5).then_inc(act_done, act_inc("a"))
                            act.wait_ge(act_done, act_at("a", j))
                            nc.scalar.activation(km[:, :, :], a[:, :, :], ACT.Identity, scale=of("k_a"), bias=of("one_less_k_a"))\
                                .then_inc(act_done, act_inc("fac"))
                    act.wait_ge(pe_done, pe_at("gate", j))
                    nc.scalar.activation(g[:, :], B[7][:, 0:TOK], ACT.Copy).then_inc(act_done, act_inc("gate"))
                    act.wait_ge(pe_done, pe_at("s0", j))
                    nc.scalar.activation(ST[:, :, 3, :], B[0][:, 0:P].rearrange("p (d n) -> p d n", d=2), ACT.Copy).then_inc(act_done, act_inc("s0"))
                    act.wait_ge(dve_done, dve_at("LB", j))
                    nc.scalar.activation(ET[:, :, :], L[:, :, C - 1:TOK:C], ACT.Exp)
                    for dst, f, b, sc in ((E3, L[:, 0, :], LB[:, :], -1.0), (E1, D0[:, 0, :], D1[:, 1, :], 1.0),
                                          (E2, L[:, 0, :], LB[:, :], 1.0), (E4, D1[:, 0, :], D0[:, 1, :], 1.0)):
                        nc.scalar.activation(dst[:, 0, :], f, ACT.Exp, scale=sc)
                        i = nc.scalar.activation(dst[:, 1, :], b, ACT.Exp, scale=sc)
                    i.then_inc(act_done, act_inc("exp"))
                    act.wait_ge(dve_done, dve_at("norm", j))
                    nc.scalar.activation(rn[:, :], nrm[:, :], ACT.Sqrt).then_inc(act_done, act_inc("root"))
                    if more:
                        for m in range(2):
                            copy_raw(m, j + 1)
                    for t in range(TT):
                        act.wait_ge(pe_done, pe_at(f"t0_{t}", j))
                        nc.scalar.activation(T[:, t, :, :], four(B[t][:, :]), ACT.Copy).then_inc(act_done, act_inc(f"t0_{t}"))
                    for t in range(TT):
                        act.wait_ge(pe_done, pe_at(f"tm{t}a", j))
                        nc.scalar.activation(TM[:, t, 0:4, :], four(B[6][:, :]), ACT.Copy).then_inc(act_done, act_inc(f"tm{t}a"))
                        act.wait_ge(pe_done, pe_at(f"tm{t}b", j))
                        nc.scalar.activation(TM[:, t, 4:7, :], B[7][:, 0:TOK].rearrange("p (q n) -> p q n", q=3), ACT.Copy).then_inc(act_done, act_inc(f"tm{t}b"))
                    for l in range(NL - 1):
                        for t in range(TT):
                            act.wait_ge(pe_done, pe_at(f"tr{l}_{t}", j))
                            nc.scalar.activation(TI[:, t, :, :], four(B[t][:, :]), ACT.Copy).then_inc(act_done, act_inc(f"tr{l}_{t}"))
                    for t in range(TT):
                        act.wait_ge(pe_done, pe_at(f"bv{t}", j))
                        nc.scalar.activation(BV[:, t, :, :], B[t][:, 0:4 * HD].rearrange("p (q n) -> p q n", q=4), ACT.Copy).then_inc(act_done, act_inc(f"bv{t}"))
                        act.wait_ge(pe_done, pe_at(f"mx{t}", j))
                        nc.scalar.activation(MX[:, t, :, :], B[3 + t][:, 0:2 * P].rearrange("p (d n) -> p d n", d=2), ACT.Copy).then_inc(act_done, act_inc(f"mx{t}"))
                    for t in range(TT):
                        act.wait_ge(pe_done, pe_at(f"nn{t}", j))
                        nc.scalar.activation(NN[:, t, :, :], B[t][:, 4 * HD:8 * HD].rearrange("p (q n) -> p q n", q=4), ACT.Copy).then_inc(act_done, act_inc(f"nn{t}"))
                    act.wait_ge(pe_done, pe_at("out", j))
                    nc.scalar.activation(OS[:, :], B[4][:, 0:TOK], ACT.Copy).then_inc(act_done, act_inc("out"))
                    act.wait_ge(dve_done, dve_at("var", j))
                    nc.scalar.activation(rn[:, :], nrm[:, :], ACT.Sqrt).then_inc(act_done, act_inc("root2"))
                    if more:
                        copy_raw(2, j + 1)
                    act.wait_ge(pe_done, pe_at("states", j))
                    act.wait_ge(stored, 32 * j)
                    nc.scalar.activation(so[:, :, :], B[7][0:HD, 0:2 * P].rearrange("p (d n) -> p d n", d=2), ACT.Copy).then_inc(act_done, act_inc("states"))
                    act.wait_ge(dve_done, dve_at("y", j))

                for m in range(3):
                    copy_raw(m, 0)
                with act.Fori(0, PAIRS - 1) as j:
                    turn(j, True)
                turn(PAIRS - 1, False)

            @block.vector
            def _(dve):
                v = nc.vector
                for c in (0, SEQ + 1, LINE - 1):
                    v.memset(raw[:, :, c:c + 1], 0.0)
                for h in range(2):
                    other = slice(64 - 64 * h, 128 - 64 * h)
                    v.memset(be[other, h, :, :], 0.0)
                    v.memset(kt[other, h, :, :], 0.0)

                def shifted_keys(j, last):
                    v.tensor_copy(par_next[:, :], R.params[:, :, bass.ds(j, 1)].rearrange("p q a -> p (q a)")).then_inc(early, early_inc("par"))
                    dve.wait_ge(early, early_at("par", j))
                    dve.wait_ge(raw_ready, raw_at("k", j))
                    if last is not None:
                        dve.wait_ge(pool_done, pool_at("rk", last))
                    for m, name in enumerate("rk"):
                        i = v.tensor_scalar(mid[:, m, :], raw[:, m, 1:LINE - 1], of("self_" + name, par_next), None, ALU.mult)
                    i.then_inc(early, early_inc("z0"))
                    dve.wait_ge(early, early_at("z0", j))
                    for m, name in enumerate("rk"):
                        i = v.scalar_tensor_tensor(out=mid[:, m, :], in0=raw[:, m, 0:LINE - 2], scalar=of("prev_" + name, par_next), in1=mid[:, m, :],
                                                   op0=ALU.mult, op1=ALU.add)
                    i.then_inc(early, early_inc("z1"))
                    dve.wait_ge(early, early_at("z1", j))
                    for m, name in enumerate("rk"):
                        for a0, b0, s in STREAMS:
                            i = v.scalar_tensor_tensor(out=z[:, m, a0:b0], in0=raw[:, m, 2 + a0 + s:2 + b0 + s], scalar=of("next_" + name, par_next),
                                                       in1=mid[:, m, a0 + s:b0 + s], op0=ALU.mult, op1=ALU.add)
                    i.then_inc(early, early_inc("z"))
                    dve.wait_ge(early, early_at("z", j))
                    v.tensor_scalar(kkr[:, :], z[:, 1, :], of("k_k", par_next), None, ALU.mult).then_inc(early, early_inc("kkr"))

                def turn(j, more):

                    v.tensor_copy(par[:, :], R.params[:, :, bass.ds(j, 1)].rearrange("p q a -> p (q a)")).then_inc(dve_done, dve_inc("par"))
                    dve.wait_ge(dve_done, dve_at("par", j))
                    dve.wait_ge(raw_ready, raw_at("v", j))
                    v.tensor_scalar(mid[:, 2, :], raw[:, 2, 1:LINE - 1], of("self_v"), None, ALU.mult).then_inc(dve_done, dve_inc("z0v"))
                    dve.wait_ge(dve_done, dve_at("z0v", j))
                    v.scalar_tensor_tensor(out=mid[:, 2, :], in0=raw[:, 2, 0:LINE - 2], scalar=of("prev_v"), in1=mid[:, 2, :],
                                           op0=ALU.mult, op1=ALU.add).then_inc(dve_done, dve_inc("z1v"))
                    dve.wait_ge(dve_done, dve_at("z1v", j))
                    for a0, b0, s in STREAMS:
                        i = v.scalar_tensor_tensor(out=z[:, 2, a0:b0], in0=raw[:, 2, 2 + a0 + s:2 + b0 + s], scalar=of("next_v"),
                                                   in1=mid[:, 2, a0 + s:b0 + s], op0=ALU.mult, op1=ALU.add)
                    i.then_inc(dve_done, dve_inc("zv"))
                    dve.wait_ge(early, early_at("kkr", j))
                    v.tensor_tensor(sq[:, :], kkr[:, :], kkr[:, :], ALU.mult).then_inc(dve_done, dve_inc("sq"))
                    dve.wait_ge(act_done, act_at("lw", j))
                    for d in range(2):
                        i = v.tensor_tensor_scan(L[:, d, :], chunk[:, :], lw[:, d, :], 0.0, ALU.mult, ALU.add)
                    i.then_inc(dve_done, dve_inc("L"))
                    dve.wait_ge(dve_done, dve_at("L", j))
                    v.tensor_tensor(D0[:, :, :], L[:, :, :], lw[:, :, :], ALU.subtract)
                    by_chunk = lambda x: x[:, :, :].rearrange("p d (c n) -> p (d c) n", n=C)
                    v.tensor_tensor(by_chunk(D1), by_chunk(L)[:, :, C - 1:C].broadcast_to([P, 2 * NCH, C]), by_chunk(L), ALU.subtract).then_inc(dve_done, dve_inc("D"))
                    dve.wait_ge(dve_done, dve_at("D", j))
                    v.tensor_tensor(LB[:, :], D1[:, 1, :], lw[:, 1, :], ALU.add).then_inc(dve_done, dve_inc("LB"))
                    dve.wait_ge(pe_done, pe_at("norm", j))
                    v.tensor_scalar(nrm[:, :], B[1][:, 0:TOK], L2_EPS, None, ALU.add).then_inc(dve_done, dve_inc("norm"))
                    dve.wait_ge(act_done, act_at("root", j))
                    v.reciprocal(rn[:, :], rn[:, :]).then_inc(dve_done, dve_inc("rn"))
                    dve.wait_ge(dve_done, dve_at("rn", j))
                    v.tensor_tensor(kk[:, :], kkr[:, :], rn[:, :], ALU.mult).then_inc(dve_done, dve_inc("kk"))
                    dve.wait_ge(dve_done, dve_at("kk", j))
                    dve.wait_ge(act_done, act_at("fac", j))
                    v.tensor_tensor(km[:, :, :], km[:, :, :], two(z[:, 1, :]), ALU.mult).then_inc(dve_done, dve_inc("km"))
                    v.scalar_tensor_tensor(out=nka[:, :, :], in0=two(kk[:, :]), scalar=-1.0, in1=a[:, :, :], op0=ALU.mult, op1=ALU.mult).then_inc(dve_done, dve_inc("nka"))
                    dve.wait_ge(dve_done, dve_at("nka", j))
                    dve.wait_ge(act_done, act_at("exp", j))
                    for h in range(2):
                        hr = slice(64 * h, 64 * h + 64)
                        v.tensor_tensor(be[hr, h, :, :], nka[hr, :, :], E3[hr, :, :], ALU.mult)
                    v.tensor_tensor(ka[:, :, :], E1[:, :, :], two(kk[:, :]), ALU.mult)
                    v.tensor_tensor(rh[:, :, :], E2[:, :, :], two(z[:, 0, :]), ALU.mult)
                    for h in range(2):
                        hr = slice(64 * h, 64 * h + 64)
                        i = v.tensor_tensor(kt[hr, h, :, :], km[hr, :, :], E3[hr, :, :], ALU.mult)
                    i.then_inc(dve_done, dve_inc("ops"))
                    as4 = lambda ap: ap.rearrange("p (d h n) -> p d h n", d=2, h=2)
                    sq4 = lambda x, t: x[:, t, :, :].rearrange("p (d h) n -> p d h n", d=2)
                    for t in range(TT):
                        for i, (name, dst, m) in enumerate((("at", AT, 0), ("q1", Q1, 1), ("bt", BT, 0), ("q2", Q2, 1))):
                            dve.wait_ge(pe_done, pe_at(f"{'ab'[i // 2]}{t}", j))
                            for h in range(2):
                                src = score_bank(t, i // 2, h)[:, (i % 2) * 2 * P:(i % 2 + 1) * 2 * P].rearrange("p (d n) -> p d n", d=2)
                                ins = v.tensor_tensor(dst[:, t, h:4:2, :], src, masks[:, :, m, :], ALU.mult)
                            ins.then_inc(dve_done, dve_inc(f"{name}{t}"))
                        dve.wait_ge(dve_done, dve_at(f"at{t}", j))
                        for d in range(2):
                            ins = v.tensor_tensor(XM[:, t, 2 * d:2 * d + 2, :], AT[:, t, 2 * d:2 * d + 2, :],
                                                  masks[:, d, 2, :].unsqueeze(1).broadcast_to([P, 2, P]), ALU.mult)
                        ins.then_inc(dve_done, dve_inc(f"m{t}"))
                        dve.wait_ge(dve_done, dve_at(f"m{t}", j))
                        v.tensor_tensor(TI[:, t, :, :], XM[:, t, :, :], R.ident[:, :].unsqueeze(1).broadcast_to([P, 4, P]), ALU.add)\
                            .then_inc(dve_done, dve_inc(f"ti{t}"))
                    if more:
                        shifted_keys(j + 1, j)
                    for l in range(NL):
                        for t in range(TT):
                            dve.wait_ge(pe_done, pe_at(f"x{l}_{t}", j))
                            for d in range(2):
                                ins = v.tensor_tensor(XM[:, t, 2 * d:2 * d + 2, :], four(B[t][:, :])[:, 2 * d:2 * d + 2, :],
                                                      masks[:, d, 3 + l, :].unsqueeze(1).broadcast_to([P, 2, P]), ALU.mult)
                            ins.then_inc(dve_done, dve_inc(f"xm{l}_{t}"))
                        for t in range(TT):
                            dve.wait_ge(pe_done, pe_at(f"w{l}_{t}", j))
                            dst = T if l < NL - 1 else TI
                            v.tensor_tensor(dst[:, t, :, :], dst[:, t, :, :], four(B[3 + t][:, :]), ALU.add).then_inc(dve_done, dve_inc(f"up{l}_{t}"))
                    for s in range(4):
                        now = [n for n in range(4) if (s, n) in CHAIN_STEPS]
                        for n in now:
                            _, d, chunks, _ = CHAINS[n]
                            t, cp = divmod(chunks[s], 2)
                            c = slice(64 * cp, 64 * cp + 64)
                            dve.wait_ge(pe_done, pe_at(f"u{s}_{n}", j))
                            if s == 0:
                                dve.wait_ge(act_done, act_at("nn2", j))
                            v.tensor_tensor(U[c, t, d, :, :], R.PS[c, 2 * n:2 * n + 2, 0:HD], NN[c, t, 2 * d:2 * d + 2, :], ALU.add).then_inc(dve_done, dve_inc(f"u{s}_{n}"))
                        for n in now:
                            _, d, chunks, first = CHAINS[n]
                            dve.wait_ge(pe_done, pe_at(f"s{s}_{n}", j))
                            if s:
                                dve.wait_ge(dve_done, dve_at(f"s{s - 1}_{n}", j))
                            v.scalar_tensor_tensor(out=ST[:, d, first + s + 1, :], in0=ST[:, d, first + s, :], scalar=ET[:, d, chunks[s]:chunks[s] + 1],
                                                       in1=B[2 * n][:, 2 * HD:3 * HD], op0=ALU.mult, op1=ALU.add).then_inc(dve_done, dve_inc(f"s{s}_{n}"))
                    dve.wait_ge(pe_done, pe_at("mean", j))
                    v.scalar_tensor_tensor(out=OS[:, :], in0=B[5][:, 0:TOK], scalar=-1.0 / HD, in1=OS[:, :], op0=ALU.mult, op1=ALU.add).then_inc(dve_done, dve_inc("d"))
                    dve.wait_ge(dve_done, dve_at("d", j))
                    v.tensor_tensor(sq[:, :], OS[:, :], OS[:, :], ALU.mult).then_inc(dve_done, dve_inc("dd"))
                    dve.wait_ge(pe_done, pe_at("var", j))
                    v.tensor_scalar(nrm[:, :], B[4][:, 0:TOK], 1.0 / HD, GN_EPS, ALU.mult, ALU.add).then_inc(dve_done, dve_inc("var"))
                    dve.wait_ge(act_done, act_at("root2", j))
                    v.reciprocal(rn[:, :], rn[:, :]).then_inc(dve_done, dve_inc("rstd"))
                    dve.wait_ge(dve_done, dve_at("rstd", j))
                    v.tensor_tensor(y[:, 0, 0:TOK], OS[:, :], rn[:, :], ALU.mult).then_inc(dve_done, dve_inc("yn"))
                    dve.wait_ge(dve_done, dve_at("yn", j))
                    v.tensor_scalar(y[:, 0, 0:TOK], y[:, 0, 0:TOK], of("gn_w"), of("gn_b"), ALU.mult, ALU.add).then_inc(dve_done, dve_inc("yw"))
                    dve.wait_ge(pe_done, pe_at("bonus", j))
                    v.tensor_tensor(bonus[:, 0, :], z[:, 2, :], B[6][:, 0:TOK], ALU.mult).then_inc(dve_done, dve_inc("bonus"))
                    dve.wait_ge(dve_done, dve_at("bonus", j))
                    v.tensor_tensor(y[:, 0, 0:TOK], y[:, 0, 0:TOK], bonus[:, 0, :], ALU.add).then_inc(dve_done, dve_inc("yb"))
                    dve.wait_ge(dve_done, dve_at("yb", j))
                    v.tensor_tensor(R.MT[:, :, :].rearrange("p k n -> p (k n)")[:, bass.ds(2 * TOK + j * TOK, TOK)],
                                        y[:, 0, 0:TOK], g[:, :], ALU.mult).then_inc(dve_done, dve_inc("y"))
                    dve.wait_ge(pe_done, pe_at("states", j))

                shifted_keys(0, None)
                dve.wait_ge(c_in, 48)
                with dve.Fori(0, PAIRS - 1) as j:
                    turn(j, True)
                turn(PAIRS - 1, False)


def moe(R):
    stack, sb = local(R)
    with stack:
        R.H = sb("normed_by_token", [P, TT, D])
        R.place = sb("place_in_item", [P, TT, ITEM_COLS])
        R.weight = sb("weight_in_item", [P, TT, ITEM_COLS])
        R.slots = sb("slot_numbers", [P, P])
        R.items = sb("item_experts", [1, ITEM_COLS + 1], I32)
        routed(R)
        experts(R)


def routed(R):
    nc = R.nc
    stack, sb = local(R)
    with stack:
        RW, rb, one = sb("router_cols", [P, KT, NE]), sb("router_bias", [1, NE]), sb("router_one", [1, P])
        before, ones = sb("before_token", [P, P]), sb("all_ones", [P, P])
        item, lower = sb("item_numbers", [P, ITEM_COLS]), sb("lower_first", [P, NE])
        lg, eq, o1, o2, mk, cb, rank = (sb(f"route_{n}", [P, TT, NE]) for n in ("logits", "equal", "first", "second", "mask", "combine", "rank"))
        m1, m2, rm, df, g1, g2 = (sb(f"route_{n}", [P, TT]) for n in ("max1", "max2", "pick", "diff", "gate1", "gate2"))
        cnt, nb, big, end, start = (sb(f"expert_{n}", [P, NE]) for n in ("count", "blocks", "third", "end", "start"))
        own, low, prod = (sb(f"item_{n}", [P, ITEM_COLS, NE]) for n in ("owner", "low", "product"))
        base, ex, itf = sb("item_base", [P, ITEM_COLS]), sb("item_expert", [P, ITEM_COLS]), sb("item_row", [1, ITEM_COLS + 1])
        loaded = R.sem("router_loaded")
        turned, t_out = R.sem("h_turned"), R.sem("h_copied")
        pe_done = R.sem("route_pe_done")
        pe_inc, pe_at = steps(["logits", "rank"])
        act_done = R.sem("route_act_done")
        act_inc, act_at = steps(["exp"])
        dve_done = R.sem("route_dve_done")
        dve_inc, dve_at = steps(["one", "lg", "m1", "eq1", "pr1", "rm1", "o1", "lg2", "m2", "eq2", "pr2", "rm2", "o2", "df",
                                         "den", "g1", "g2", "mask", "c1", "c2", "cb", "cnt", "nb1", "nb2", "nb", "end", "start",
                                         "low", "own0", "own", "ps", "bs", "b1", "base", "pe", "ex", "row", "items", "rk1", "rk2"]
                        + [x for t in range(TT) for x in (f"pp{t}", f"pl{t}", f"place{t}", f"pw{t}", f"w{t}")])
        with nc.Block() as block:

            @block.sync
            def _(sp):
                sp.dma_start(RW[:, :, :], R.I["router_w"][0].rearrange("(k p) e -> p k e", p=P)).then_inc(loaded, 16)
                sp.dma_start(rb[:, :], R.I["router_b"]).then_inc(loaded, 16)
                for buf, name in ((before, "before"), (ones, "ones"), (R.slots, "slot"), (item, "item"), (lower, "lower8")):
                    sp.dma_start(buf[:, :], const(R, name)).then_inc(loaded, 16)

            @block.tensor
            def _(pe):
                pe.wait_ge(loaded, 7 * 16)
                pe.wait_ge(dve_done, dve_at("one"))
                for t in range(TT):
                    for k in range(KT):
                        nc.tensor.matmul(R.B[0][:, t * NE:(t + 1) * NE], R.HT[:, k, t * P:(t + 1) * P], RW[:, k, :], start=(k == 0), stop=False)
                    mm = nc.tensor.matmul(R.B[0][:, t * NE:(t + 1) * NE], one[0:1, :], rb[0:1, :], start=False, stop=True)
                mm.then_inc(pe_done, pe_inc("logits"))
                for t in range(TT):
                    for h in range(2):
                        for k in range(4):
                            mm = nc.tensor.transpose(R.B[2 + 2 * t + h][:, k * P:(k + 1) * P], R.HT[:, 4 * h + k, t * P:(t + 1) * P], R.ident[:, :])
                        mm.then_inc(turned, 1)
                pe.wait_ge(dve_done, dve_at("mask"))
                for t in range(TT):
                    for s in range(t):
                        nc.tensor.matmul(R.B[1][:, t * NE:(t + 1) * NE], ones[:, :], mk[:, s, :], start=(s == 0), stop=False)
                    nc.tensor.matmul(R.B[1][:, t * NE:(t + 1) * NE], before[:, :], mk[:, t, :], start=(t == 0), stop=True)
                for s in range(TT):
                    mm = nc.tensor.matmul(R.B[1][:, TT * NE:(TT + 1) * NE], ones[:, :], mk[:, s, :], start=(s == 0), stop=(s == TT - 1))
                mm.then_inc(pe_done, pe_inc("rank"))

            @block.scalar
            def _(act):
                for u in range(2 * TT):
                    act.wait_ge(turned, u + 1)
                    nc.scalar.activation(R.H[:, u // 2, (u % 2) * BANK:(u % 2 + 1) * BANK], R.B[2 + u][:, :], ACT.Copy)
                act.wait_ge(dve_done, dve_at("df"))
                nc.scalar.activation(g2[:, :], df[:, :], ACT.Exp).then_inc(act_done, act_inc("exp"))

            @block.vector
            def _(dve):
                v = nc.vector


                wide = lambda x: x.unsqueeze(2).broadcast_to([P, TT, NE])
                per_e = lambda x: x.unsqueeze(1).broadcast_to([P, ITEM_COLS, NE])
                per_i = lambda x: x.unsqueeze(2).broadcast_to([P, ITEM_COLS, NE])
                v.memset(one[:, :], 1.0).then_inc(dve_done, dve_inc("one"))
                dve.wait_ge(loaded, 7 * 16)
                dve.wait_ge(pe_done, pe_at("logits"))
                v.tensor_copy(lg[:, :, :], R.B[0][:, 0:TT * NE].rearrange("p (t e) -> p t e", t=TT)).then_inc(dve_done, dve_inc("lg"))
                dve.wait_ge(dve_done, dve_at("lg"))
                for n, (m, o) in enumerate(((m1, o1), (m2, o2)), 1):
                    v.tensor_reduce(m[:, :], lg[:, :, :], AX.X, ALU.max).then_inc(dve_done, dve_inc(f"m{n}"))
                    dve.wait_ge(dve_done, dve_at(f"m{n}"))
                    v.tensor_tensor(eq[:, :, :], lg[:, :, :], wide(m[:, :]), ALU.is_equal).then_inc(dve_done, dve_inc(f"eq{n}"))
                    dve.wait_ge(dve_done, dve_at(f"eq{n}"))
                    v.tensor_tensor(eq[:, :, :], eq[:, :, :], lower[:, :].unsqueeze(1).broadcast_to([P, TT, NE]), ALU.mult).then_inc(dve_done, dve_inc(f"pr{n}"))
                    dve.wait_ge(dve_done, dve_at(f"pr{n}"))
                    v.tensor_reduce(rm[:, :], eq[:, :, :], AX.X, ALU.max).then_inc(dve_done, dve_inc(f"rm{n}"))
                    dve.wait_ge(dve_done, dve_at(f"rm{n}"))
                    v.tensor_tensor(o[:, :, :], eq[:, :, :], wide(rm[:, :]), ALU.is_equal).then_inc(dve_done, dve_inc(f"o{n}"))
                    dve.wait_ge(dve_done, dve_at(f"o{n}"))
                    if n == 1:
                        v.scalar_tensor_tensor(out=lg[:, :, :], in0=o1[:, :, :], scalar=-1e30, in1=lg[:, :, :], op0=ALU.mult, op1=ALU.add).then_inc(dve_done, dve_inc("lg2"))
                        dve.wait_ge(dve_done, dve_at("lg2"))
                v.tensor_tensor(df[:, :], m2[:, :], m1[:, :], ALU.subtract).then_inc(dve_done, dve_inc("df"))
                dve.wait_ge(act_done, act_at("exp"))
                v.tensor_scalar(g1[:, :], g2[:, :], 1.0, None, ALU.add).then_inc(dve_done, dve_inc("den"))
                dve.wait_ge(dve_done, dve_at("den"))
                v.reciprocal(g1[:, :], g1[:, :]).then_inc(dve_done, dve_inc("g1"))
                dve.wait_ge(dve_done, dve_at("g1"))
                v.tensor_tensor(g2[:, :], g2[:, :], g1[:, :], ALU.mult).then_inc(dve_done, dve_inc("g2"))
                dve.wait_ge(dve_done, dve_at("g2"))
                v.tensor_tensor(mk[:, :, :], o1[:, :, :], o2[:, :, :], ALU.add).then_inc(dve_done, dve_inc("mask"))
                dve.wait_ge(dve_done, dve_at("mask"))
                v.tensor_tensor(o1[:, :, :], o1[:, :, :], wide(g1[:, :]), ALU.mult).then_inc(dve_done, dve_inc("c1"))
                v.tensor_tensor(o2[:, :, :], o2[:, :, :], wide(g2[:, :]), ALU.mult).then_inc(dve_done, dve_inc("c2"))
                dve.wait_ge(dve_done, dve_at("c2"))
                v.tensor_tensor(cb[:, :, :], o1[:, :, :], o2[:, :, :], ALU.add).then_inc(dve_done, dve_inc("cb"))
                dve.wait_ge(dve_done, dve_at("cb"))
                dve.wait_ge(pe_done, pe_at("rank"))
                v.tensor_copy(rank[:, :, :], R.B[1][:, 0:TT * NE].rearrange("p (t e) -> p t e", t=TT))
                v.tensor_copy(cnt[:, :], R.B[1][:, TT * NE:(TT + 1) * NE]).then_inc(dve_done, dve_inc("cnt"))
                dve.wait_ge(dve_done, dve_at("cnt"))
                v.tensor_scalar(nb[:, :], cnt[:, :], float(P), 1.0, ALU.is_gt, ALU.add).then_inc(dve_done, dve_inc("nb1"))
                v.tensor_scalar(big[:, :], cnt[:, :], float(2 * P), None, ALU.is_gt).then_inc(dve_done, dve_inc("nb2"))
                dve.wait_ge(dve_done, dve_at("nb2"))
                v.tensor_tensor(nb[:, :], nb[:, :], big[:, :], ALU.add).then_inc(dve_done, dve_inc("nb"))
                dve.wait_ge(dve_done, dve_at("nb"))
                v.tensor_tensor_scan(end[:, :], ones[:, 0:NE], nb[:, :], 0.0, ALU.mult, ALU.add).then_inc(dve_done, dve_inc("end"))
                dve.wait_ge(dve_done, dve_at("end"))
                v.tensor_tensor(start[:, :], end[:, :], nb[:, :], ALU.subtract).then_inc(dve_done, dve_inc("start"))
                dve.wait_ge(dve_done, dve_at("start"))
                v.tensor_tensor(low[:, :, :], per_i(item[:, :]), per_e(start[:, :]), ALU.is_ge).then_inc(dve_done, dve_inc("low"))
                v.tensor_tensor(own[:, :, :], per_i(item[:, :]), per_e(end[:, :]), ALU.is_lt).then_inc(dve_done, dve_inc("own0"))
                dve.wait_ge(dve_done, dve_at("own0"))
                v.tensor_tensor(own[:, :, :], own[:, :, :], low[:, :, :], ALU.mult).then_inc(dve_done, dve_inc("own"))
                dve.wait_ge(dve_done, dve_at("own"))
                v.tensor_tensor(prod[:, :, :], own[:, :, :], per_e(start[:, :]), ALU.mult).then_inc(dve_done, dve_inc("ps"))
                dve.wait_ge(dve_done, dve_at("ps"))
                v.tensor_reduce(base[:, :], prod[:, :, :], AX.X, ALU.add).then_inc(dve_done, dve_inc("bs"))
                dve.wait_ge(dve_done, dve_at("bs"))
                v.tensor_tensor(base[:, :], item[:, :], base[:, :], ALU.subtract).then_inc(dve_done, dve_inc("b1"))
                dve.wait_ge(dve_done, dve_at("b1"))
                v.tensor_scalar(base[:, :], base[:, :], float(P), None, ALU.mult).then_inc(dve_done, dve_inc("base"))
                dve.wait_ge(dve_done, dve_at("base"))
                v.tensor_tensor(prod[:, :, :], own[:, :, :], per_e(lower[:, :]), ALU.mult).then_inc(dve_done, dve_inc("pe"))
                dve.wait_ge(dve_done, dve_at("pe"))
                v.tensor_reduce(ex[:, :], prod[:, :, :], AX.X, ALU.add).then_inc(dve_done, dve_inc("ex"))
                dve.wait_ge(dve_done, dve_at("ex"))
                v.tensor_copy(itf[0:1, ITEM_COLS:ITEM_COLS + 1], end[0:1, NE - 1:NE])
                v.tensor_scalar(itf[0:1, 0:ITEM_COLS], ex[0:1, :], -1.0, float(NE), ALU.mult, ALU.add).then_inc(dve_done, dve_inc("row"))
                dve.wait_ge(dve_done, dve_at("row"))
                v.tensor_copy(R.items[:, :], itf[:, :]).then_inc(dve_done, dve_inc("items"))
                v.scalar_tensor_tensor(out=rank[:, :, :], in0=rank[:, :, :], scalar=1e4, in1=mk[:, :, :], op0=ALU.add, op1=ALU.mult).then_inc(dve_done, dve_inc("rk1"))
                dve.wait_ge(dve_done, dve_at("rk1"))
                v.tensor_scalar(rank[:, :, :], rank[:, :, :], -1e4, None, ALU.add).then_inc(dve_done, dve_inc("rk2"))
                dve.wait_ge(dve_done, dve_at("rk2"))
                for t in range(TT):
                    v.tensor_tensor(prod[:, :, :], own[:, :, :], per_e(rank[:, t, :]), ALU.mult).then_inc(dve_done, dve_inc(f"pp{t}"))
                    dve.wait_ge(dve_done, dve_at(f"pp{t}"))
                    v.tensor_reduce(R.place[:, t, :], prod[:, :, :], AX.X, ALU.add).then_inc(dve_done, dve_inc(f"pl{t}"))
                    dve.wait_ge(dve_done, dve_at(f"pl{t}"))
                    v.tensor_tensor(R.place[:, t, :], R.place[:, t, :], base[:, :], ALU.subtract).then_inc(dve_done, dve_inc(f"place{t}"))
                    v.tensor_tensor(prod[:, :, :], own[:, :, :], per_e(cb[:, t, :]), ALU.mult).then_inc(dve_done, dve_inc(f"pw{t}"))
                    dve.wait_ge(dve_done, dve_at(f"pw{t}"))
                    v.tensor_reduce(R.weight[:, t, :], prod[:, :, :], AX.X, ALU.add).then_inc(dve_done, dve_inc(f"w{t}"))
                    dve.wait_ge(dve_done, dve_at(f"w{t}"))


def experts(R):
    nc = R.nc
    stack, sb = local(R)
    NF = FFE // P
    with stack:
        W = sb("expert_gate_up", [P, KT, 2, FFE])
        WD = sb("expert_down", [P, NF, D])
        hg = sb("gathered", [P, KT, P])
        gu, guT = sb("expert_hidden", [P, FFE]), sb("expert_hidden_T", [P, NF, P])
        Y = sb("expert_out", [P, D])
        G, GW, GT = (sb(n, [P, TT, P]) for n in ("one_hot", "one_hot_weighted", "scatter"))
        acc = R.HT[:, :, :].rearrange("p k n -> p (k n)").rearrange("p (t d) -> p t d", t=TT)
        B = R.B
        w_in, d_in = [R.sem(f"gate_up_in{k}") for k in range(KT)], [R.sem(f"down_in{f}") for f in range(NF)]
        w_used, d_used = R.sem("gate_up_slots_used"), R.sem("down_slots_used")
        CH = ((0, 512), (512, 1024), (1024, FFE))
        pe_done = R.sem("exp_pe_done")
        pe_inc, pe_at = steps(["hg0", "hg1", "gate", "up", "tw", "t0", "t1", "t2", "down"] + [f"sc{u}" for u in range(6)])
        act_done = R.sem("exp_act_done")
        act_inc, act_at = steps(["hg0", "silu", "t0", "t1", "t2", "y"])
        dve_done = R.sem("exp_dve_done")
        dve_inc, dve_at = steps(["G", "GW", "hg1", "gu", "tw"] + [f"acc{u}" for u in range(6)])
        zero, gated = R.sem("acc_cleared"), R.sem("experts_gated")
        n_items = lambda e: e.value_load(R.items[0:1, ITEM_COLS:ITEM_COLS + 1], min_val=NE, max_val=MAX_ITEMS)
        with nc.Block() as block:

            @block.sync
            def _(sp):
                n = n_items(sp)
                with sp.Fori(0, n) as i:
                    e = sp.value_load(R.items[0:1, bass.ds(i, 1)], min_val=0, max_val=NE - 1)
                    for k in range(KT):
                        sp.wait_ge(w_used, i * KT + (k + 1))
                        sp.sem_inc(R.passed, 1)
                        for m, w in enumerate(("moe_w_gate", "moe_w_up")):
                            sp.dma_start(W[:, k, m, :], R.I[w][0, bass.ds(e, 1), k * P:(k + 1) * P, :].rearrange("a p n -> (a p) n"))\
                                .then_inc(w_in[k], 16)
                    for f in range(NF):
                        sp.wait_ge(d_used, i * NF + (f + 1))
                        sp.sem_inc(R.passed, 1)
                        sp.dma_start(WD[:, f, :], R.I["moe_w_down"][0, bass.ds(e, 1), f * P:(f + 1) * P, :].rearrange("a p n -> (a p) n"))\
                            .then_inc(d_in[f], 16)

            @block.tensor
            def _(pe):
                pe.sem_inc(w_used, KT)
                pe.sem_inc(d_used, NF)
                n = n_items(pe)
                with pe.Fori(0, n) as i:
                    pe.wait_ge(dve_done, dve_at("G", i))
                    for k in range(KT):
                        for t in range(TT):
                            mm = nc.tensor.matmul(B[6 + k // 4][:, (k % 4) * P:(k % 4 + 1) * P], R.H[:, t, k * P:(k + 1) * P], G[:, t, :],
                                                  start=(t == 0), stop=(t == TT - 1))
                        if k % 4 == 3:
                            mm.then_inc(pe_done, pe_inc(f"hg{k // 4}"))
                    for k in range(KT):
                        pe.wait_ge(w_in[k], 32 * i + 32)
                        if k == 0:
                            pe.wait_ge(act_done, act_at("hg0", i))
                        elif k == 4:
                            pe.wait_ge(dve_done, dve_at("hg1", i))
                        for m in range(2):
                            for c, (a, b) in enumerate(CH):
                                mm = nc.tensor.matmul(B[3 * m + c][:, 0:b - a], hg[:, k, :], W[:, k, m, a:b], start=(k == 0), stop=(k == KT - 1))
                            if k == KT - 1:
                                if m == 0:
                                    mm.then_inc(pe_done, pe_inc("gate"))
                                else:
                                    mm.then_inc(pe_done, pe_inc("up"))
                        if k < KT - 1:
                            mm.then_inc(w_used, 1)
                    for t in range(TT):
                        mm = nc.tensor.transpose(B[7][:, t * P:(t + 1) * P], GW[:, t, :], R.ident[:, :])
                        if t == 0:
                            mm.then_inc(w_used, 1)
                    mm.then_inc(pe_done, pe_inc("tw"))
                    pe.wait_ge(dve_done, dve_at("gu", i))
                    for c in range(3):
                        fs = range(4 * c, min(4 * c + 4, NF))
                        for f in fs:
                            mm = nc.tensor.transpose(B[c][:, (f % 4) * P:(f % 4 + 1) * P], gu[:, f * P:(f + 1) * P], R.ident[:, :])
                        mm.then_inc(pe_done, pe_inc(f"t{c}"))
                    pe.wait_ge(dve_done, dve_at("tw", i))
                    for f in range(NF):
                        pe.wait_ge(d_in[f], 16 * i + 16)
                        if f % 4 == 0:
                            pe.wait_ge(act_done, act_at(f"t{f // 4}", i))
                        for h in range(2):
                            mm = nc.tensor.matmul(B[6 + h][:, :], guT[:, f, :], WD[:, f, h * BANK:(h + 1) * BANK], start=(f == 0), stop=(f == NF - 1))
                        if f < NF - 1:
                            mm.then_inc(d_used, 1)
                    mm.then_inc(pe_done, pe_inc("down"))
                    pe.wait_ge(act_done, act_at("y", i))
                    pe.sem_inc(d_used, 1)
                    for u in range(6):
                        t, h = divmod(u, 2)
                        nc.tensor.matmul(B[u][:, :], GT[:, t, :], Y[:, h * BANK:(h + 1) * BANK], start=True, stop=True).then_inc(pe_done, pe_inc(f"sc{u}"))
                    pe.wait_ge(dve_done, dve_at("acc5", i))

            @block.scalar
            def _(act):
                n = n_items(act)
                with act.Fori(0, n) as i:
                    act.wait_ge(pe_done, pe_at("hg0", i))
                    nc.scalar.activation(hg[:, 0:4, :], B[6][:, :].rearrange("p (k n) -> p k n", k=4), ACT.Copy).then_inc(act_done, act_inc("hg0"))
                    act.wait_ge(pe_done, pe_at("gate", i))
                    for c, (a, b) in enumerate(CH):
                        ins = nc.scalar.activation(gu[:, a:b], B[c][:, 0:b - a], ACT.Silu)
                    ins.then_inc(act_done, act_inc("silu"))
                    for c in range(3):
                        fs = slice(4 * c, min(4 * c + 4, NF))
                        w = (fs.stop - fs.start) * P
                        act.wait_ge(pe_done, pe_at(f"t{c}", i))
                        nc.scalar.activation(guT[:, fs, :], B[c][:, 0:w].rearrange("p (k n) -> p k n", n=P), ACT.Copy).then_inc(act_done, act_inc(f"t{c}"))
                    act.wait_ge(pe_done, pe_at("down", i))
                    for h in range(2):
                        ins = nc.scalar.activation(Y[:, h * BANK:(h + 1) * BANK], B[6 + h][:, :], ACT.Copy)
                    ins.then_inc(act_done, act_inc("y"))
                    act.wait_ge(pe_done, pe_at("sc5", i))

            @block.vector
            def _(dve):
                v = nc.vector
                v.memset(acc, 0.0).then_inc(zero, 1)
                dve.wait_ge(zero, 1)
                n = n_items(dve)
                with dve.Fori(0, n) as i:
                    for t in range(TT):
                        ins = v.tensor_scalar(G[:, t, :], R.slots[:, :], R.place[:, t, bass.ds(i, 1)], None, ALU.is_equal)
                    ins.then_inc(dve_done, dve_inc("G"))
                    for t in range(TT):
                        ins = v.tensor_scalar(GW[:, t, :], R.slots[:, :], R.place[:, t, bass.ds(i, 1)], R.weight[:, t, bass.ds(i, 1)],
                                              ALU.is_equal, ALU.mult)
                    ins.then_inc(dve_done, dve_inc("GW"))
                    dve.wait_ge(pe_done, pe_at("hg1", i))
                    v.tensor_copy(hg[:, 4:8, :], B[7][:, :].rearrange("p (k n) -> p k n", k=4)).then_inc(dve_done, dve_inc("hg1"))
                    dve.wait_ge(pe_done, pe_at("up", i))
                    dve.wait_ge(act_done, act_at("silu", i))
                    for c, (a, b) in enumerate(CH):
                        ins = v.tensor_tensor(gu[:, a:b], gu[:, a:b], B[3 + c][:, 0:b - a], ALU.mult)
                    ins.then_inc(dve_done, dve_inc("gu"))
                    dve.wait_ge(pe_done, pe_at("tw", i))
                    v.tensor_copy(GT[:, :, :], B[7][:, 0:TT * P].rearrange("p (t n) -> p t n", t=TT)).then_inc(dve_done, dve_inc("tw"))
                    for u in range(6):
                        t, h = divmod(u, 2)
                        x = acc[:, t, h * BANK:(h + 1) * BANK]
                        dve.wait_ge(pe_done, pe_at(f"sc{u}", i))
                        v.tensor_tensor(x, x, B[u][:, :], ALU.add).then_inc(dve_done, dve_inc(f"acc{u}"))
                    dve.wait_ge(dve_done, dve_at("acc5", i))
                for t in range(TT):
                    v.tensor_tensor(acc[:, t, :], acc[:, t, :], R.ffn_gate[:, min(t, 1), :], ALU.mult).then_inc(gated, 1)

            @block.gpsimd
            def _(pool):
                for t in range(TT):
                    pool.wait_ge(gated, t + 1)
                    nc.gpsimd.tensor_tensor(R.X[:, t, :], R.X[:, t, :], acc[:, t, :], ALU.add)


def finish(R):
    nc = R.nc
    stack, sb = local(R)
    with stack:
        XN = sb("final", [P, TT, D])
        wrow = sb("final_weight", [P, D])
        ss, ms, rt, rs = (sb(f"{w}_last", [P, TT]) for w in ("sumsq", "meansq", "root", "rstd"))
        act_done = R.sem("last_act_done")
        act_inc, act_at = steps(["squares", "root"])
        dve_done = R.sem("last_dve_done")
        dve_inc, dve_at = steps(["mean", "rstd"] + [f"y{t}" for t in range(TT)])
        w_loaded, stored = R.sem("final_weight_loaded"), R.sem("y_stored")
        with nc.Block() as block:

            @block.sync
            def _(sp):
                sp.dma_start(wrow[:, :], R.I["norm_final"].partition_broadcast(P)).then_inc(w_loaded, 16)
                ys = R.O["y_sample"][0].rearrange("(t p) d -> p t d", p=P)
                for t in range(TT):
                    sp.wait_ge(dve_done, dve_at(f"y{t}"))
                    sp.dma_start(R.O["y_prompt"][0] if t == 0 else ys[:, t - 1, :], XN[:, t, :]).then_inc(stored, 16)
                sp.wait_ge(stored, 16 * TT)

            @block.scalar
            def _(act):
                for t in range(TT):
                    a = nc.scalar.activation(XN[:, t, :], R.X[:, t, :], ACT.Square, accum_out=ss[:, t:t + 1])
                a.then_inc(act_done, act_inc("squares"))
                act.wait_ge(dve_done, dve_at("mean"))
                nc.scalar.activation(rt[:, :], ms[:, :], ACT.Sqrt).then_inc(act_done, act_inc("root"))

            @block.vector
            def _(dve):
                dve.wait_ge(act_done, act_at("squares"))
                nc.vector.tensor_scalar(ms[:, :], ss[:, :], 1.0 / D, RMS_EPS, ALU.mult, ALU.add).then_inc(dve_done, dve_inc("mean"))
                dve.wait_ge(act_done, act_at("root"))
                nc.vector.reciprocal(rs[:, :], rt[:, :]).then_inc(dve_done, dve_inc("rstd"))
                dve.wait_ge(dve_done, dve_at("rstd"))
                dve.wait_ge(w_loaded, 16)
                for t in range(TT):
                    nc.vector.scalar_tensor_tensor(out=XN[:, t, :], in0=R.X[:, t, :], scalar=rs[:, t:t + 1], in1=wrow[:, :],
                                                                 op0=ALU.mult, op1=ALU.mult).then_inc(dve_done, dve_inc(f"y{t}"))


def constants(np):
    a = np.zeros((P, N_CONSTS), np.float32)

    def put(name, x):
        lo, hi = CONSTS[name]
        a[:, lo:hi] = np.asarray(x, np.float32).reshape(P, hi - lo)

    p, f = np.arange(P)[:, None], np.arange(P)[None, :]
    put("ident", p == f)
    put("pick", np.stack([np.broadcast_to(p % 32 == c, (P, P)) for c in range(2)], 1))
    same = (p // 64 == f // 64)
    ang = 2 * np.pi * ((p % 64) * (f % 64) % 64) / 64
    put("dft_c", np.concatenate([same * np.cos(ang), same * np.sin(ang)], 1))
    n, m = np.arange(DEC)[:, None], np.arange(DEC)[None, :]
    ang = 2 * np.pi * (n * m % DEC) / DEC
    both = np.stack([np.cos(ang), -np.sin(ang)]) / np.sqrt(DEC * 64)
    put("dft_s", both.reshape(2, 2, P, DEC).transpose(2, 0, 1, 3))
    n, m = np.arange(SEQ)[:, None], np.arange(SEQ)[None, :]
    ang = 2 * np.pi * (n * m % SEQ) / SEQ
    put("dft_p", (np.stack([np.cos(ang), -np.sin(ang)]) / np.sqrt(SEQ * 64)).transpose(1, 0, 2))
    c0 = np.clip(p % GRID_W - WIN // 2, 0, GRID_W - WIN)
    k = np.arange(GRID_W)[None, :]
    put("window", np.where((k >= c0) & (k < c0 + WIN), 0.0, -1e30))
    masks = np.zeros((P, 2, 8, P))
    for d in range(2):
        early = (p < f) if d == 0 else (p > f)
        masks[:, d, 0] = same & early
        masks[:, d, 1] = same & (early | (p == f))
        masks[:, d, 2] = early & (p // 2 == f // 2)
        for i, m in enumerate(LEVELS):
            late = (p > f) if d == 0 else (p < f)
            masks[:, d, 3 + i] = late & (p // (2 * m) == f // (2 * m)) & (p // m != f // m)
    put("masks", masks)
    put("halves", same)
    put("chunk", np.broadcast_to(np.arange(TOK) % C != 0, (P, TOK)))
    inv = np.zeros((P, 2, TOK))
    for g, w in enumerate(POOL_WINDOWS):
        for o, n in ((0, SEQ), (SEQ, DEC)):
            t = np.arange(n)
            inv[64 * (g % 2):64 * (g % 2) + 64, g // 2, o:o + n] = 1.0 / (np.clip(t + w - w // 2, 0, n) - np.clip(t - w // 2, 0, n))
    put("inv_count", inv)
    put("before", p < f)
    put("ones", np.ones((P, P)))
    put("slot", np.broadcast_to(f, (P, P)))
    put("item", np.broadcast_to(np.arange(ITEM_COLS), (P, ITEM_COLS)))
    put("lower8", np.broadcast_to(NE - np.arange(NE), (P, NE)))
    return a


_OUTS = [("y_prompt", (1, SEQ, D)), ("y_sample", (1, DEC, D)), ("new_k", (1, 1, SEQ, 12, HD)),
         ("new_v", (1, 1, SEQ, 12, HD)), ("new_state", (1, 1, 2, 12, HD, HD))]


def kernel(**inputs):
    import numpy as np
    from concourse import bacc
    from concourse.bass_utils import run_bass_kernel_spmd

    nc = bacc.Bacc("TRN2", target_bir_lowering=False, num_devices=1)
    arrays = {f"in_{n}": np.ascontiguousarray(a) for n, a in inputs.items()}
    arrays["in_consts"] = constants(np)
    I = {n[3:]: nc.dram_tensor(n, a.shape, mybir.dt.from_np(a.dtype), kind="ExternalInput").ap() for n, a in arrays.items()}
    O = {n: nc.dram_tensor(f"out_{n}", s, F32, kind="ExternalOutput").ap() for n, s in _OUTS}
    build(nc, I, O)
    r = run_bass_kernel_spmd(nc, [arrays], core_ids=[0])
    return tuple(r.results[0][f"out_{n}"] for n, _ in _OUTS)
```

```python
import math
from contextlib import ExitStack

import concourse.bass as bass
from concourse import mybir

F32 = mybir.dt.float32
F32R = mybir.dt.float32r
I32 = mybir.dt.int32
ALU = mybir.AluOpType
ACT = mybir.ActivationFunctionType
AX = mybir.AxisListType

P = 128
D = 1024
KT = D // P
SEQ, DEC = 128, 256
TOK = SEQ + DEC
TT = TOK // P
BANK = 512
HD = 64
PAIRS = 6
GRID_W, ROWS, WIN = 64, 4, 16
BIAS_ROW, BIAS_HEAD = 31, 15 * 31
FF = 2816
FFE = 1408
NE = 8
C = 64
NCH = TOK // C
RMS_EPS, GN_EPS, L2_EPS = 1e-6, 64e-5, 1e-12
DECAY = math.exp(-0.5)
LEVELS = (2, 4, 8, 16, 32)
MAX_ITEMS = 13
ITEM_COLS = 16
POOL_WINDOWS = (2, 4, 8, 16)

CONSTS = {}
_at = 0
for _name, _w in (("ident", 128), ("pick", 256), ("dft_c", 256), ("dft_s", 1024), ("dft_p", 256), ("window", 64),
                  ("masks", 16 * 128), ("halves", 128), ("chunk", 384), ("inv_count", 768), ("before", 128),
                  ("ones", 128), ("slot", 128), ("item", ITEM_COLS), ("lower8", NE)):
    CONSTS[_name] = (_at, _at + _w)
    _at += _w
N_CONSTS = _at


def steps(names):
    names = list(names)
    place = {name: i for i, name in enumerate(names)}
    assert len(place) == len(names)
    given = []

    def inc(name):
        assert place[name] == len(given) % len(names), name
        given.append(name)
        return 1

    def at(name, j=0):
        return j * len(names) + place[name] + 1

    return inc, at


class Core:

    def __init__(self, nc, I, O):
        self.nc, self.I, self.O = nc, I, O


def build(nc, I, O):
    with ExitStack() as whole:
        R = Core(nc, I, O)
        R.sem = lambda name: whole.enter_context(nc.semaphore(name))
        R.passed = R.sem("wait_passed")
        R.sb = lambda name, shape, dt=F32: whole.enter_context(nc.sbuf_tensor(name, shape, dt))
        R.PS = whole.enter_context(nc.psum_tensor("banks", [P, 8, BANK], F32))
        R.B = [R.PS[:, i, :] for i in range(8)]
        R.X = R.sb("residual", [P, TT, D])
        R.HT = R.sb("normed_by_channel", [P, KT, TOK])
        R.ident = R.sb("identity", [P, P])
        R.spot = R.sb("spot", [P, 8])
        R.scale_col = R.sb("scale_columns", [P, 4, KT, 2])
        R.shift_col = R.sb("shift_columns", [P, 4, KT, 2])
        R.VT = R.sb("parameter_columns", [P, 50])
        R.ffn_gate = R.sb("ffn_gate_rows", [P, 2, D])
        R.cond = R.sb("silu_cond", [P, KT, 32])
        R.bias_rows = nc.dram_tensor("bias_rows", [P, 12 * 2 * ROWS * GRID_W], F32).ap()
        R.bias_spread = R.sem("bias_spread")
        R.x_loaded, R.mod_small = R.sem("x_loaded"), R.sem("mod_small_loaded")
        R.mod_loaded = [R.sem(f"mod_w_loaded{s}") for s in range(10)]
        gates, sb = local(R)
        with gates:
            R.mix_gate = sb("mix_gate_rows", [P, 2, D])
            layer0(R)
            layer1(R)
        moe(R)
        finish(R)


def local(R):
    stack = ExitStack()
    return stack, lambda name, shape, dt=F32: stack.enter_context(R.nc.sbuf_tensor(name, shape, dt))


def tables_for(R, function, place):
    R.nc.scalar.activation(R.spot[:, place:place + 1], R.spot[:, 0:1], function)


def const(R, name):
    a, b = CONSTS[name]
    return R.I["consts"][:, a:b]


def prologue(R):
    nc = R.nc
    stack, sb = local(R)
    with stack:
        rows = sb("parameter_rows", [50, P])
        load_rows, load_const = R.sem("rows_loaded"), R.sem("ident_loaded")
        cleared, turned, copied = R.sem("cond_cleared"), R.sem("rows_turned"), R.sem("columns_ready")
        with nc.Block() as block:

            @block.sync
            def _(sp):
                as_rows = lambda a: a.rearrange("(r p) -> r p", p=P)
                sp.dma_start(rows[0:8, :], as_rows(R.I["c_ctx"])).then_inc(load_rows, 16)
                sp.dma_start(rows[8:16, :], as_rows(R.I["c"][0])).then_inc(load_rows, 16)
                for l in range(2):
                    sp.dma_start(rows[16 + 8 * l:24 + 8 * l, :], as_rows(R.I["norm_mix"][l])).then_inc(load_rows, 16)
                    sp.dma_start(rows[32 + 8 * l:40 + 8 * l, :], as_rows(R.I["norm_ffn"][l])).then_inc(load_rows, 16)
                sp.dma_start(rows[48:50, :], as_rows(R.I["pool_scale"][0])).then_inc(load_rows, 16)
                sp.dma_start(R.ident[:, :], const(R, "ident")).then_inc(load_const, 16)
                modulation_rows(R, sp)
                modulation_loads(R, sp, range(len(R.mod_loaded)))
                sp.dma_start(R.X[:, 0, :], R.I["x_prompt"][0]).then_inc(R.x_loaded, 16)
                sp.dma_start(R.X[:, 1:3, :], R.I["x_sample"][0].rearrange("(t p) d -> p t d", p=P)).then_inc(R.x_loaded, 16)

            @block.vector
            def _(dve):
                nc.vector.memset(R.spot[:, :], 1.0)
                nc.vector.memset(R.cond[:, :, :], 0.0).then_inc(cleared, 1)

            @block.tensor
            def _(pe):
                pe.wait_ge(load_rows, 7 * 16)
                pe.wait_ge(load_const, 16)
                nc.tensor.transpose(R.B[0][:, 0:50], rows[:, :], R.ident[0:50, 0:50]).then_inc(turned, 1)

            @block.scalar
            def _(act):
                act.wait_ge(turned, 1)
                nc.scalar.activation(R.VT[:, :], R.B[0][:, 0:50], ACT.Copy).then_inc(copied, 1)
                act.wait_ge(cleared, 1)
                nc.scalar.activation(R.cond[:, :, 0], R.B[0][:, 0:8], ACT.Silu)
                nc.scalar.activation(R.cond[:, :, 1], R.B[0][:, 8:16], ACT.Silu)


def modulation_buffers(R, sb):
    R.mod_w = sb("mod_w_slots", [P, len(R.mod_loaded), 2048])
    R.mod_bias, R.mod_pick = sb("mod_bias_row", [1, 3, 2048]), sb("pick", [P, 2, P])


def modulation_rows(R, sp):
    sp.dma_start(R.mod_bias[0:1, :, :], R.I["mod_b"][0:1, :].rearrange("a (g n) -> a g n", g=3)).then_inc(R.mod_small, 16)
    sp.dma_start(R.mod_pick[:, :, :], const(R, "pick").rearrange("p (c n) -> p c n", c=2)).then_inc(R.mod_small, 16)


def modulation_loads(R, sp, chunks):
    for u in chunks:
        g, k = divmod(u, KT)
        s = u % len(R.mod_loaded)
        sp.dma_start(R.mod_w[:, s, :], R.I["mod_w"][0, k * P:(k + 1) * P, g * 2048:(g + 1) * 2048]).then_inc(R.mod_loaded[s], 16)


def modulation(R, ahead):
    nc = R.nc
    stack, sb = local(R)
    with stack:
        W = R.mod_w
        bias, pick, small = R.mod_bias, R.mod_pick, R.mod_small
        one = sb("mod_one", [1, 32])
        M = sb("mod_rows", [P, 3, BANK])
        col = sb("mod_cols", [P, 3, 4, 4, 2])
        loaded, SLOTS = R.mod_loaded, len(R.mod_loaded)
        used = R.sem("mod_w_used")
        ones = R.sem("mod_one_set")
        pe_done = R.sem("mod_pe_done")
        pe_inc, pe_at = steps([f"{w}{g}" for g in range(3) for w in ("rows", "turned", "gate")])
        act_done = R.sem("mod_act_done")
        act_inc, act_at = steps([f"{w}{g}" for g in range(3) for w in ("rows", "gate")])
        dve_done = R.sem("mod_dve_done")
        dve_inc, dve_at = steps([f"cols{g}" for g in range(3)])
        gate_of = {1: (0, R.mix_gate), 2: (2, R.ffn_gate)}
        with nc.Block() as block:

            @block.sync
            def _(sp):
                for u in range(SLOTS, 3 * KT):
                    sp.wait_ge(used, u - SLOTS + 1)
                    modulation_loads(R, sp, [u])
                ahead(sp)
                sp.wait_ge(R.x_loaded, 32)

            @block.tensor
            def _(pe):
                pe.wait_ge(small, 32)
                pe.wait_ge(ones, 1)
                for g in range(3):
                    for k in range(KT):
                        u = g * KT + k
                        pe.wait_ge(loaded[u % SLOTS], 16 * (u // SLOTS + 1))
                        for q in range(4):
                            mm = nc.tensor.matmul(R.B[g][32 * q:32 * q + 32, :], R.cond[:, k, :],
                                                  W[:, u % SLOTS, q * BANK:(q + 1) * BANK], start=(k == 0), stop=False)
                        mm.then_inc(used, 1)
                    for q in range(4):
                        mm = nc.tensor.matmul(R.B[g][32 * q:32 * q + 32, :], one[0:1, :],
                                              bias[0:1, g, q * BANK:(q + 1) * BANK], start=False, stop=True)
                    mm.then_inc(pe_done, pe_inc(f"rows{g}"))
                    pe.wait_ge(act_done, act_at(f"rows{g}"))
                    for i in range(4):
                        mm = nc.tensor.transpose(R.B[3][:, i * P:(i + 1) * P], M[:, g, i * P:(i + 1) * P], R.ident[:, :])
                    mm.then_inc(pe_done, pe_inc(f"turned{g}"))
                    if g in gate_of:
                        q0 = gate_of[g][0]
                        if g == 2:
                            pe.wait_ge(act_done, act_at("gate1"))
                        for c in range(2):
                            for h in range(2):
                                q = q0 + h
                                mm = nc.tensor.matmul(R.B[4 + 2 * c + h][:, :], pick[32 * q:32 * q + 32, c, :],
                                                      M[32 * q:32 * q + 32, g, :], start=True, stop=True,
                                                      tile_position=(32 * q, 0))
                    pe.wait_ge(dve_done, dve_at(f"cols{g}"))
                    if g not in gate_of:
                        mm = nc.tensor.transpose(R.B[7][:, 0:P], M[:, g, 0:P], R.ident[:, :])
                    mm.then_inc(pe_done, pe_inc(f"gate{g}"))

            @block.scalar
            def _(act):
                for g in range(3):
                    act.wait_ge(pe_done, pe_at(f"rows{g}"))
                    nc.scalar.activation(M[:, g, :], R.B[g][:, :], ACT.Copy).then_inc(act_done, act_inc(f"rows{g}"))
                    act.wait_ge(pe_done, pe_at(f"gate{g}"))
                    if g in gate_of:
                        for c in range(2):
                            for h in range(2):
                                a = nc.scalar.activation(gate_of[g][1][:, c, h * BANK:(h + 1) * BANK],
                                                         R.B[4 + 2 * c + h][:, :], ACT.Copy)
                    else:
                        a = nc.scalar.activation(M[:, g, 0:1], M[:, g, 0:1], ACT.Copy)
                    a.then_inc(act_done, act_inc(f"gate{g}"))

            @block.vector
            def _(dve):
                nc.vector.memset(one[:, :], 1.0).then_inc(ones, 1)
                for g in range(3):
                    dve.wait_ge(pe_done, pe_at(f"turned{g}"))
                    turned = R.B[3][:, :].rearrange("p (i q x) -> p i q x", i=4, q=4)
                    nc.vector.tensor_copy(col[:, g], turned[:, :, :, 0:2]).then_inc(dve_done, dve_inc(f"cols{g}"))
                dve.wait_ge(dve_done, dve_at("cols2"))
                for n, (shift, scale, w0) in enumerate(((0, 1, 16), (3, 4, 32))):
                    for h in range(2):
                        ks = slice(4 * h, 4 * h + 4)
                        weight = R.VT[:, w0 + 4 * h:w0 + 4 * h + 4].unsqueeze(2).broadcast_to([P, 4, 2])
                        nc.vector.scalar_tensor_tensor(out=R.scale_col[:, n, ks, :],
                                                       in0=col[:, scale // 2, :, 2 * (scale % 2) + h, :], scalar=1.0,
                                                       in1=weight, op0=ALU.add, op1=ALU.mult)
                        nc.vector.tensor_copy(R.shift_col[:, n, ks, :],
                                              col[:, shift // 2, :, 2 * (shift % 2) + h, :])


def second_modulation(R):
    nc = R.nc
    stack, sb = local(R)
    with stack:
        ones = sb("sum_ones", [P, P])
        set_ones = R.sem("sum_ones_set")
        pe_done = R.sem("mod1_pe_done")
        pe_inc, pe_at = steps(["mixer", "ffn"] + [f"gate{i}" for i in range(8)])
        A = R.mod_sums
        gates = [(first + h * BANK, c, to, h) for first, to in ((2 * D, R.mix_gate), (5 * D, R.ffn_gate)) for c in range(2) for h in range(2)]
        with nc.Block() as block:

            @block.tensor
            def _(pe):
                pe.wait_ge(set_ones, 1)
                pe.wait_ge(R.mod_sums_done, 6 * KT)
                for n in range(2):
                    for i in range(2):
                        for k in range(KT):
                            for c in range(2):
                                col = (3 * n + i) * D + k * P
                                at = (i * KT + k) * 2 + c
                                mm = nc.tensor.matmul(R.B[6 + n][:, at:at + 1], A[:, c, col:col + P], ones[:, 0:1], start=True, stop=True)
                    mm.then_inc(pe_done, pe_inc(("mixer", "ffn")[n]))
                for i, (col, c, _, _) in enumerate(gates):
                    if i >= 6:
                        pe.wait_ge(R.mod_columns, 1)
                    nc.tensor.matmul(R.B[i][:, :], ones[:, :], A[:, c, col:col + BANK], start=True, stop=True).then_inc(pe_done, pe_inc(f"gate{i}"))

            @block.scalar
            def _(act):
                for i in range(0, 8, 2):
                    _, c, to, h = gates[i]
                    act.wait_ge(pe_done, pe_at(f"gate{i}"))
                    nc.scalar.activation(to[:, c, h * BANK:(h + 1) * BANK], R.B[i][:, :], ACT.Copy)

            @block.vector
            def _(dve):
                nc.vector.memset(ones[:, :], 1.0).then_inc(set_ones, 1)
                for n in range(2):
                    dve.wait_ge(pe_done, pe_at(("mixer", "ffn")[n]))
                    shift, scale = (R.B[6 + n][:, i * 2 * KT:(i + 1) * 2 * KT].rearrange("p (k c) -> p k c", c=2) for i in range(2))
                    weight = R.VT[:, (24, 40)[n]:(24, 40)[n] + KT].unsqueeze(2).broadcast_to([P, KT, 2])
                    nc.vector.scalar_tensor_tensor(out=R.scale_col[:, 2 + n, :, :], in0=scale, scalar=1.0, in1=weight, op0=ALU.add, op1=ALU.mult)
                    ins = nc.vector.tensor_copy(R.shift_col[:, 2 + n, :, :], shift)
                ins.then_inc(R.mod_columns, 1)
                for i in range(1, 8, 2):
                    _, c, to, h = gates[i]
                    dve.wait_ge(pe_done, pe_at(f"gate{i}"))
                    nc.vector.tensor_copy(to[:, c, h * BANK:(h + 1) * BANK], R.B[i][:, :])


def normed(R, n, ahead=None):
    nc = R.nc
    stack, sb = local(R)
    with stack:
        XN = sb(f"scaled{n}", [P, TT, D])
        ss, ms, rt, rs = (sb(f"{w}{n}", [P, TT]) for w in ("sumsq", "meansq", "root", "rstd"))
        act_done = R.sem(f"norm_act{n}_done")
        act_inc, act_at = steps(["squares", "root", "scaled0", "scaled2"])
        dve_done = R.sem(f"norm_dve{n}_done")
        dve_inc, dve_at = steps(["mean", "rstd", "scaled1"])
        turned = R.sem(f"norm_turned{n}")
        with nc.Block() as block:

            if ahead is not None:

                @block.sync
                def _(sp):
                    ahead(sp)

            @block.scalar
            def _(act):
                for t in range(TT):
                    a = nc.scalar.activation(XN[:, t, :], R.X[:, t, :], ACT.Square, accum_out=ss[:, t:t + 1])
                a.then_inc(act_done, act_inc("squares"))
                act.wait_ge(dve_done, dve_at("mean"))
                nc.scalar.activation(rt[:, :], ms[:, :], ACT.Sqrt).then_inc(act_done, act_inc("root"))
                act.wait_ge(dve_done, dve_at("rstd"))
                for t in (0, 2):
                    nc.scalar.activation(XN[:, t, :], R.X[:, t, :], ACT.Copy, scale=rs[:, t:t + 1]).then_inc(act_done, act_inc(f"scaled{t}"))
                for k in range(0, KT, 2):
                    act.wait_ge(turned, k + 1)
                    for c, cols in ((0, slice(0, SEQ)), (1, slice(SEQ, TOK))):
                        nc.scalar.activation(R.HT[:, k, cols], R.B[k][:, cols], ACT.Identity,
                                             bias=R.shift_col[:, n, k, c:c + 1], scale=R.scale_col[:, n, k, c:c + 1])

            @block.vector
            def _(dve):
                dve.wait_ge(act_done, act_at("squares"))
                nc.vector.tensor_scalar(ms[:, :], ss[:, :], 1.0 / D, RMS_EPS, ALU.mult, ALU.add).then_inc(dve_done, dve_inc("mean"))
                dve.wait_ge(act_done, act_at("root"))
                nc.vector.reciprocal(rs[:, :], rt[:, :]).then_inc(dve_done, dve_inc("rstd"))
                dve.wait_ge(dve_done, dve_at("rstd"))
                nc.vector.tensor_scalar(XN[:, 1, :], R.X[:, 1, :], rs[:, 1:2], None, ALU.mult).then_inc(dve_done, dve_inc("scaled1"))
                for k in range(1, KT, 2):
                    dve.wait_ge(turned, k + 1)
                    for c, cols in ((0, slice(0, SEQ)), (1, slice(SEQ, TOK))):
                        nc.vector.tensor_scalar(R.HT[:, k, cols], R.B[k][:, cols], R.scale_col[:, n, k, c:c + 1],
                                                R.shift_col[:, n, k, c:c + 1], ALU.mult, ALU.add)

            @block.tensor
            def _(pe):
                pe.wait_ge(act_done, act_at("scaled2"))
                pe.wait_ge(dve_done, dve_at("scaled1"))
                for k in range(KT):
                    for t in range(TT):
                        mm = nc.tensor.transpose(R.B[k][:, t * P:(t + 1) * P], XN[:, t, k * P:(k + 1) * P], R.ident[:, :])
                    mm.then_inc(turned, 1)


def layer0(R):
    whole, sb = local(R)
    with whole:
        dense_buffers(R, sb)
        stack, sb = local(R)
        with stack:
            attention_buffers(R, sb)
            inner, sb1 = local(R)
            with inner:
                fourier_buffers(R, sb1)
                slots, sb2 = local(R)
                with slots:
                    modulation_buffers(R, sb2)
                    prologue(R)
                    modulation(R, ahead=lambda sp: fourier_loads(R, sp))
                normed(R, 0)
                R.MT = sb1("mixed_by_channel0", [P, KT, TOK])
                w_out, sb2 = local(R)
                with w_out:
                    mixed_buffers(R, sb2, 0)

                    def first_pair(sp):
                        for m in range(3):
                            qkv_load(R, sp, m, 0)
                        ctx_k_load(R, sp, 0)
                        ctx_v_load(R, sp, 0)

                    fourier(R, ahead=first_pair)
                    attention(R, ahead=lambda sp: mixed_loads(R, sp, R.I["na_w_out"][0]))

                    def first_tiles(sp):
                        for p in range(2):
                            dense_loads(R, sp, p, p * P)

                    mixed(R, 0, ahead=first_tiles)
        normed(R, 1)
        sums, sb = local(R)
        with sums:
            R.mod_sums = sb("mod_sums", [P, 2, 6 * D])
            R.mod_sums_done, R.mod_columns = R.sem("mod_sums_done"), R.sem("mod_columns_copied")
            dense_ffn(R)
            second_modulation(R)


def fourier_buffers(R, sb):
    R.f_w = sb("fourier_w_in", [P, KT, 256])
    R.f_tables = sb("dft_channels", [P, 256]), sb("dft_latent", [P, 4, DEC]), sb("dft_prompt", [P, 2, SEQ])
    R.f_w_in, R.f_tables_in = R.sem("fw_in"), R.sem("fw_tables")


def fourier_loads(R, sp):
    dc, ds, dp = R.f_tables
    sp.dma_start(R.f_w[:, :, :], R.I["na_w_in"][0].rearrange("(k p) n -> p k n", p=P)[:, :, 0:256]).then_inc(R.f_w_in, 16)
    sp.dma_start(dc[:, :], const(R, "dft_c")).then_inc(R.f_tables_in, 16)
    sp.dma_start(ds[:, :, :], const(R, "dft_s").rearrange("p (a n) -> p a n", a=4)).then_inc(R.f_tables_in, 16)
    sp.dma_start(dp[:, :, :], const(R, "dft_p").rearrange("p (a n) -> p a n", a=2)).then_inc(R.f_tables_in, 16)


def fourier(R, ahead):
    nc = R.nc
    stack, sb = local(R)
    with stack:
        W, (dc, ds, dp) = R.f_w, R.f_tables
        GW = sb("group_w", [P, 2, P])
        fT = sb("fourier_in", [P, 2, TOK])
        XCS = sb("channel_dft", [P, TT, 2, 256])
        spec = sb("spectrum", [P, 2, TOK])
        w_in, tables, gw, zero = R.f_w_in, R.f_tables_in, R.sem("fw_group"), R.sem("fw_zero")
        pe_done = R.sem("fourier_pe_done")
        pe_inc, pe_at = steps([f"{w}{m}" for w in ("in", "chan", "spec", "out") for m in range(2)])
        act_done = R.sem("fourier_act_done")
        act_inc, act_at = steps([f"{w}{m}" for w in ("in", "chan", "spec", "out") for m in range(2)])
        with nc.Block() as block:

            @block.vector
            def _(dve):
                nc.vector.memset(GW[:, :, :], 0.0).then_inc(zero, 1)

            @block.sync
            def _(sp):
                sp.wait_ge(zero, 1)
                for g in range(4):
                    sp.dma_start(GW[64 * (g % 2):64 * (g % 2) + 64, g // 2, 64 * (g % 2):64 * (g % 2) + 64],
                                 R.I["fourier_w"][0, g]).then_inc(gw, 16)
                ahead(sp)

            @block.gpsimd
            def _(pool):
                rows_of = R.bias_rows.rearrange("(a c) (h t r k) -> a t h c r k", a=2, h=12, t=2, r=ROWS)
                for i in range(ROWS):
                    for r in range(ROWS):
                        src = bass.AP(R.I["na_rel_bias"].tensor, (7 - i + r) * BIAS_ROW + 15,
                                      [[BIAS_HEAD, 12], [-1, GRID_W], [1, GRID_W]])
                        pool.dma_start(rows_of[i % 2, i // 2, :, :, r, :], src).then_inc(R.bias_spread, 16)

            @block.tensor
            def _(pe):
                pe.wait_ge(w_in, 16)
                for m in range(2):
                    for k in range(KT):
                        mm = nc.tensor.matmul(R.B[m][:, 0:TOK], W[:, k, m * P:(m + 1) * P], R.HT[:, k, :],
                                              start=(k == 0), stop=(k == KT - 1))
                    mm.then_inc(pe_done, pe_inc(f"in{m}"))
                pe.wait_ge(tables, 48)
                for m in range(2):
                    pe.wait_ge(act_done, act_at(f"in{m}"))
                    for t in range(TT):
                        mm = nc.tensor.matmul(R.B[2 + m + 2 * (t // 2)][:, (t % 2) * 256:(t % 2) * 256 + 256],
                                              fT[:, m, t * P:(t + 1) * P], dc[:, :], start=True, stop=True)
                    mm.then_inc(pe_done, pe_inc(f"chan{m}"))
                for m in range(2):
                    pe.wait_ge(act_done, act_at(f"chan{m}"))
                    bank = R.B[6 + m]
                    for a in range(2):
                        nc.tensor.matmul(bank[:, 0:SEQ], XCS[:, 0, m, a * P:(a + 1) * P], dp[:, a, :], start=(a == 0), stop=(a == 1))
                    for a in range(2):
                        for t in range(2):
                            mm = nc.tensor.matmul(bank[:, SEQ:TOK], XCS[:, 1 + t, m, a * P:(a + 1) * P], ds[:, 2 * a + t, :],
                                                  start=(a + t == 0), stop=(a + t == 2))
                    mm.then_inc(pe_done, pe_inc(f"spec{m}"))
                pe.wait_ge(gw, 64)
                for m in range(2):
                    pe.wait_ge(act_done, act_at(f"spec{m}"))
                    nc.tensor.matmul(R.B[m][:, 0:TOK], GW[:, m, :], spec[:, m, :], start=True, stop=True).then_inc(pe_done, pe_inc(f"out{m}"))

            @block.scalar
            def _(act):
                for m in range(2):
                    act.wait_ge(pe_done, pe_at(f"in{m}"))
                    nc.scalar.activation(fT[:, m, :], R.B[m][:, 0:TOK], ACT.Copy).then_inc(act_done, act_inc(f"in{m}"))
                for m in range(2):
                    act.wait_ge(pe_done, pe_at(f"chan{m}"))
                    nc.scalar.activation(XCS[:, 0:2, m, :], R.B[2 + m][:, :].rearrange("p (t n) -> p t n", t=2), ACT.Copy)
                    nc.scalar.activation(XCS[:, 2, m, :], R.B[4 + m][:, 0:256], ACT.Copy).then_inc(act_done, act_inc(f"chan{m}"))
                for m in range(2):
                    act.wait_ge(pe_done, pe_at(f"spec{m}"))
                    nc.scalar.activation(spec[:, m, :], R.B[6 + m][:, 0:TOK], ACT.Copy).then_inc(act_done, act_inc(f"spec{m}"))
                for m in range(2):
                    act.wait_ge(pe_done, pe_at(f"out{m}"))
                    nc.scalar.activation(R.MT[:, m, :], R.B[m][:, 0:TOK], ACT.Copy).then_inc(act_done, act_inc(f"out{m}"))


def attention_buffers(R, sb):
    R.qkv_w, R.ctx_k, R.ctx_v = sb("qkv_w", [P, 3, KT, P]), sb("ck", [P, P]), sb("cv", [P, P])
    R.qkv_in = [R.sem(f"{m}_w_loaded") for m in "qkv"]
    R.ctx_k_in, R.ctx_v_in = R.sem("ctx_k_loaded"), R.sem("ctx_v_loaded")


def qkv_load(R, sp, m, c):
    w_in = R.I["na_w_in"][0].rearrange("(k p) n -> p k n", p=P)
    sp.dma_start(R.qkv_w[:, m, :, :], w_in[:, :, 256 + 768 * m:1024 + 768 * m][:, :, bass.ds(c, P)]).then_inc(R.qkv_in[m], 16)


def ctx_k_load(R, sp, c):
    sp.dma_start(R.ctx_k[:, :], R.I["cache_na_k"][0, 0].rearrange("n h d -> n (h d)")[:, bass.ds(c, P)]).then_inc(R.ctx_k_in, 16)


def ctx_v_load(R, sp, c):
    sp.dma_start(R.ctx_v[:, :], R.I["cache_na_v"][0, 0].rearrange("n h d -> n (h d)")[:, bass.ds(c, P)]).then_inc(R.ctx_v_in, 16)


def attention(R, ahead):
    nc = R.nc
    stack, sb = local(R)
    with stack:
        W, ck, cv = R.qkv_w, R.ctx_k, R.ctx_v
        qT, kT = sb("qT", [P, TOK]), sb("kT", [P, TOK])
        V = sb("v", [P, TT, P])
        ckT = sb("ckT", [P, P])
        kp = sb("k_prompt", [P, P])
        bias, window = sb("rel_bias", [P, 2, 2, DEC]), sb("window", [P, GRID_W])
        S = sb("scores", [P, 2, TOK])
        Pn = sb("probs", [P, 2, TOK])
        PT = sb("probs_T", [P, 2, TOK])
        neg, tot, inv = sb("neg_max", [P, 6]), sb("total", [P, 6]), sb("inv_total", [P, 6])
        units = [(h, t) for h in range(2) for t in range(TT)]
        w_loaded, b_loaded, win = R.qkv_in, R.sem("bias_loaded"), R.sem("win_loaded")
        stored, projected = R.sem("kv_stored"), R.sem("qkv_projected")
        proj_inc, proj_at = steps("qkv")
        pe_done = R.sem("attn_pe_done")
        pe_inc, pe_at = steps(["ck", "kp", "s0", "s1"]
                       + [x for u in range(6) for x in ([f"pt{u}", f"pv{u}"] + ([f"s{u + 2}"] if u + 2 < 6 else []))])
        act_done = R.sem("attn_act_done")
        act_inc, act_at = steps(["q", "k"] + [x for u in range(6) for x in (f"exp{u}", f"pt{u}")] + ["out"])
        dve_done = R.sem("attn_dve_done")
        dve_inc, dve_at = steps(["v", "ck", "kp", "bias"] + [x for u in range(6) for x in (f"s{u}", f"max{u}", f"inv{u}", f"p{u}")])
        nk = R.O["new_k"][0, 0].rearrange("n h d -> n (h d)")
        nv = R.O["new_v"][0, 0].rearrange("n h d -> n (h d)")
        rel = R.I["na_rel_bias"]

        def bias_loads(sp, j):
            sp.dma_start(bias[:, :, :, :], R.bias_rows.rearrange("p (j n) -> p j n", j=PAIRS)[:, bass.ds(j, 1), :]
                         .rearrange("p a (h t n) -> p (a h) t n", h=2, t=2)).then_inc(b_loaded, 16)

        with nc.Block() as block:

            @block.sync
            def _(sp):
                sp.dma_start(window[:, :], const(R, "window")).then_inc(win, 16)
                sp.wait_ge(R.bias_spread, 16 * ROWS * ROWS)
                bias_loads(sp, 0)
                for m in range(3):
                    sp.wait_ge(projected, proj_at("qkv"[m], 0))
                    qkv_load(R, sp, m, P)
                with sp.Fori(0, PAIRS - 2) as j:
                    nxt, cols, later = sp.snap(j + 1), sp.snap(j * P + P), sp.snap(j * P + 2 * P)
                    sp.wait_ge(pe_done, pe_at("ck", j))
                    ctx_k_load(R, sp, cols)
                    for m in range(2):
                        sp.wait_ge(projected, proj_at("qkv"[m], j + 1))
                        qkv_load(R, sp, m, later)
                    sp.wait_ge(dve_done, dve_at("s5", j))
                    bias_loads(sp, nxt)
                    sp.wait_ge(projected, proj_at("v", j + 1))
                    qkv_load(R, sp, 2, later)
                    sp.wait_ge(pe_done, pe_at("pv5", j))
                    ctx_v_load(R, sp, cols)
                sp.wait_ge(pe_done, pe_at("ck", PAIRS - 2))
                ctx_k_load(R, sp, (PAIRS - 1) * P)
                sp.wait_ge(dve_done, dve_at("s5", PAIRS - 2))
                bias_loads(sp, PAIRS - 1)
                sp.wait_ge(pe_done, pe_at("pv5", PAIRS - 2))
                ctx_v_load(R, sp, (PAIRS - 1) * P)
                ahead(sp)

            @block.gpsimd
            def _(pool):
                with pool.Fori(0, PAIRS) as j:
                    pool.wait_ge(dve_done, dve_at("kp", j))
                    pool.dma_start(nk[:, bass.ds(j * P, P)], kp[:, :]).then_inc(stored, 16)
                    pool.dma_start(nv[:, bass.ds(j * P, P)], V[:, 0, :]).then_inc(stored, 16)
                pool.wait_ge(stored, 32 * PAIRS)

            @block.tensor
            def _(pe):
                def project(i, j):
                    m, part = divmod(i, 4)
                    if part == 0:
                        pe.wait_ge(w_loaded[m], 16 * j + 16)
                    if m < 2:
                        for k in (2 * part, 2 * part + 1):
                            mm = nc.tensor.matmul(R.B[5 + m][:, 0:TOK], W[:, m, k, :], R.HT[:, k, :], start=(k == 0), stop=(k == KT - 1))
                    else:
                        for c in range(6 * part, 6 * part + 6):
                            t, k = divmod(c, KT)
                            mm = nc.tensor.matmul(R.B[7][:, t * P:(t + 1) * P], R.HT[:, k, t * P:(t + 1) * P], W[:, 2, k, :],
                                                  start=(k == 0), stop=(k == KT - 1))
                    if part == 3:
                        mm.then_inc(projected, proj_inc("qkv"[m]))

                for i in range(12):
                    project(i, 0)

                def turn(j, more):
                    pe.wait_ge(R.ctx_k_in, 16 * j + 16)
                    nc.tensor.transpose(R.B[3][:, 0:P], ck[:, :], R.ident[:, :]).then_inc(pe_done, pe_inc("ck"))
                    pe.wait_ge(act_done, act_at("k", j))
                    nc.tensor.transpose(R.B[2][:, 0:P], kT[:, 0:SEQ], R.ident[:, :]).then_inc(pe_done, pe_inc("kp"))

                    def scores(u):
                        h, t = units[u]
                        rows = slice(64 * h, 64 * h + 64)
                        if u >= 2:
                            pe.wait_ge(dve_done, dve_at(f"s{u - 2}", j))
                        if t == 0:
                            mm = nc.tensor.matmul(R.B[u % 2][:, 0:SEQ], qT[rows, 0:SEQ], kT[rows, 0:SEQ], start=True, stop=True)
                        else:
                            q = qT[rows, t * P:(t + 1) * P]
                            nc.tensor.matmul(R.B[u % 2][:, 0:DEC], q, kT[rows, SEQ:TOK], start=True, stop=True)
                            mm = nc.tensor.matmul(R.B[u % 2][:, DEC:TOK], q, ckT[rows, :], start=True, stop=True)
                        mm.then_inc(pe_done, pe_inc(f"s{u}"))

                    pe.wait_ge(dve_done, dve_at("kp", j))
                    scores(0)
                    scores(1)
                    for u, (h, t) in enumerate(units):
                        if more:
                            project(2 * u, j + 1)
                        pe.wait_ge(dve_done, dve_at(f"p{u}", j))
                        blocks = 1 if t == 0 else 3
                        if u >= 2:
                            pe.wait_ge(act_done, act_at(f"pt{u - 2}", j))
                        for b in range(blocks):
                            mm = nc.tensor.transpose(R.B[2 + u % 2][:, b * P:(b + 1) * P], Pn[:, u % 2, b * P:(b + 1) * P], R.ident[:, :])
                        mm.then_inc(pe_done, pe_inc(f"pt{u}"))
                        if more:
                            project(2 * u + 1, j + 1)
                        pe.wait_ge(act_done, act_at(f"pt{u}", j))
                        cols = slice(64 * h, 64 * h + 64)
                        if u == 1:
                            pe.wait_ge(R.ctx_v_in, 16 * j + 16)
                        values = [V[:, 0, cols]] if t == 0 else [V[:, 1, cols], V[:, 2, cols], cv[:, cols]]
                        for b, v in enumerate(values):
                            mm = nc.tensor.matmul(R.B[4][cols, t * P:(t + 1) * P], v, PT[:, u % 2, b * P:(b + 1) * P],
                                                  start=(b == 0), stop=(b == blocks - 1))
                        mm.then_inc(pe_done, pe_inc(f"pv{u}"))
                        if u + 2 < 6:
                            scores(u + 2)
                    pe.wait_ge(act_done, act_at("out", j))

                with pe.Fori(0, PAIRS - 1) as j:
                    turn(j, True)
                turn(PAIRS - 1, False)

            @block.scalar
            def _(act):
                with act.Fori(0, PAIRS) as j:
                    act.wait_ge(projected, proj_at("q", j))
                    nc.scalar.activation(qT[:, :], R.B[5][:, 0:TOK], ACT.Copy, scale=HD ** -0.5).then_inc(act_done, act_inc("q"))
                    act.wait_ge(projected, proj_at("k", j))
                    nc.scalar.activation(kT[:, :], R.B[6][:, 0:TOK], ACT.Copy).then_inc(act_done, act_inc("k"))
                    for u, (h, t) in enumerate(units):
                        n = SEQ if t == 0 else TOK
                        act.wait_ge(dve_done, dve_at(f"max{u}", j))
                        if u >= 2:
                            act.wait_ge(pe_done, pe_at(f"pt{u - 2}", j))
                        nc.scalar.activation(Pn[:, u % 2, 0:n], S[:, u % 2, 0:n], ACT.Exp, bias=neg[:, u:u + 1],
                                                           accum_out=tot[:, u:u + 1]).then_inc(act_done, act_inc(f"exp{u}"))
                        act.wait_ge(pe_done, pe_at(f"pt{u}", j))
                        if u >= 2:
                            act.wait_ge(pe_done, pe_at(f"pv{u - 2}", j))
                        nc.scalar.activation(PT[:, u % 2, 0:n], R.B[2 + u % 2][:, 0:n], ACT.Copy).then_inc(act_done, act_inc(f"pt{u}"))
                    act.wait_ge(pe_done, pe_at("pv5", j))
                    nc.scalar.activation(R.MT[:, :, :].rearrange("p k n -> p (k n)")[:, bass.ds(2 * TOK + j * TOK, TOK)],
                                                       R.B[4][:, 0:TOK], ACT.Copy).then_inc(act_done, act_inc("out"))
                    act.wait_ge(act_done, act_at("out", j))

            @block.vector
            def _(dve):
                dve.wait_ge(win, 16)
                with dve.Fori(0, PAIRS) as j:
                    dve.wait_ge(projected, proj_at("v", j))
                    nc.vector.tensor_copy(V[:, :, :], R.B[7][:, 0:TOK].rearrange("p (t n) -> p t n", t=TT)).then_inc(dve_done, dve_inc("v"))
                    dve.wait_ge(pe_done, pe_at("ck", j))
                    nc.vector.tensor_copy(ckT[:, :], R.B[3][:, 0:P]).then_inc(dve_done, dve_inc("ck"))
                    dve.wait_ge(pe_done, pe_at("kp", j))
                    nc.vector.tensor_copy(kp[:, :], R.B[2][:, 0:P]).then_inc(dve_done, dve_inc("kp"))
                    dve.wait_ge(b_loaded, 16 * j + 16)
                    flat = bias[:, :, :, :].rearrange("p h t (r k) -> p (h t r) k", k=GRID_W)
                    nc.vector.tensor_tensor(flat, flat, window[:, :].unsqueeze(1).broadcast_to([P, 16, GRID_W]), ALU.add).then_inc(dve_done, dve_inc("bias"))
                    dve.wait_ge(dve_done, dve_at("bias", j))

                    def scored(u):
                        h, t = units[u]
                        n = SEQ if t == 0 else TOK
                        dve.wait_ge(pe_done, pe_at(f"s{u}", j))
                        if u >= 2:
                            dve.wait_ge(act_done, act_at(f"exp{u - 2}", j))
                        if t == 0:
                            a = nc.vector.tensor_copy(S[:, u % 2, 0:n], R.B[u % 2][:, 0:n])
                        else:
                            nc.vector.tensor_tensor(S[:, u % 2, 0:DEC], R.B[u % 2][:, 0:DEC], bias[:, h, t - 1, :], ALU.add)
                            a = nc.vector.tensor_copy(S[:, u % 2, DEC:TOK], R.B[u % 2][:, DEC:TOK])
                        a.then_inc(dve_done, dve_inc(f"s{u}"))
                        dve.wait_ge(dve_done, dve_at(f"s{u}", j))
                        nc.vector.tensor_reduce(neg[:, u:u + 1], S[:, u % 2, 0:n], AX.X, ALU.max, negate=True).then_inc(dve_done, dve_inc(f"max{u}"))

                    def weighed(u):
                        n = SEQ if units[u][1] == 0 else TOK
                        dve.wait_ge(act_done, act_at(f"exp{u}", j))
                        nc.vector.reciprocal(inv[:, u:u + 1], tot[:, u:u + 1]).then_inc(dve_done, dve_inc(f"inv{u}"))
                        dve.wait_ge(dve_done, dve_at(f"inv{u}", j))
                        nc.vector.tensor_scalar(Pn[:, u % 2, 0:n], Pn[:, u % 2, 0:n], inv[:, u:u + 1], None, ALU.mult).then_inc(dve_done, dve_inc(f"p{u}"))

                    for u in range(6):
                        scored(u)
                        weighed(u)
                    dve.wait_ge(pe_done, pe_at("pv5", j))
                    dve.wait_ge(stored, 32 * j + 32)


def mixed_buffers(R, sb, l):
    R.w_out, R.w_out_in = sb(f"w_out{l}", [P, KT, D]), [R.sem(f"w_out{l}_{q}") for q in range(4)]


def mixed_loads(R, sp, w_out):
    for q in range(4):
        sp.dma_start(R.w_out[:, 2 * q:2 * q + 2, :], w_out[2 * q * P:(2 * q + 2) * P, :].rearrange("(k p) n -> p k n", p=P))\
            .then_inc(R.w_out_in[q], 16)


def mixed(R, l, ahead):
    nc = R.nc
    stack, sb = local(R)
    with stack:
        W, loaded = R.w_out, R.w_out_in
        Y = sb(f"gated{l}", [P, 6, BANK])
        done, gated = R.sem(f"mixed_done{l}"), R.sem(f"mixed_gated{l}")
        with nc.Block() as block:

            @block.sync
            def _(sp):
                ahead(sp)

            @block.tensor
            def _(pe):
                for t in range(TT):
                    for h in range(2):
                        for k in range(KT):
                            if t == 0 and h == 0 and k % 2 == 0:
                                pe.wait_ge(loaded[k // 2], 16)
                            mm = nc.tensor.matmul(R.B[2 * t + h][:, :], R.MT[:, k, t * P:(t + 1) * P], W[:, k, h * BANK:(h + 1) * BANK],
                                                  start=(k == 0), stop=(k == KT - 1))
                        mm.then_inc(done, 1)

            @block.scalar
            def _(act):
                tables_for(R, ACT.Sqrt, 1)

            @block.vector
            def _(dve):
                for u in range(6):
                    t, h = divmod(u, 2)
                    dve.wait_ge(done, u + 1)
                    nc.vector.tensor_tensor(Y[:, u, :], R.B[u][:, :], R.mix_gate[:, min(t, 1), h * BANK:(h + 1) * BANK], ALU.mult)\
                        .then_inc(gated, 1)

            @block.gpsimd
            def _(pool):
                for u in range(6):
                    t, h = divmod(u, 2)
                    x = R.X[:, t, h * BANK:(h + 1) * BANK]
                    pool.wait_ge(gated, u + 1)
                    nc.gpsimd.tensor_tensor(x, x, Y[:, u, :], ALU.add)


def dense_buffers(R, sb):
    R.gu_w, R.gu_in = sb("gate_up_w", [P, 2, 2, KT, P]), [R.sem(f"gate_up_loaded{p}") for p in range(2)]


def dense_loads(R, sp, p, c):
    for m, name in enumerate(("ffn_w_gate", "ffn_w_up")):
        w = R.I[name][0].rearrange("(k p) n -> p k n", p=P)
        sp.dma_start(R.gu_w[:, p, m, :, :], w[:, :, bass.ds(c, P)]).then_inc(R.gu_in[p], 16)


def dense_ffn(R):
    nc = R.nc
    stack, sb = local(R)
    NF = FF // P
    with stack:
        W, loaded = R.gu_w, R.gu_in
        G = sb("hidden", [P, NF, TOK])
        sil = sb("silu", [P, 2, TOK])
        ND = 3
        WD = sb("down_w", [P, ND, 2, D])
        Y = sb("ffn_gated", [P, 6, BANK])
        MW = sb("next_mod_w", [P, 3, 2 * D])
        m_loaded, m_used = [R.sem(f"next_mod_w_loaded{g}") for g in range(3)], R.sem("next_mod_w_used")
        cleared, biased = R.sem("mod_sums_cleared"), R.sem("mod_bias_loaded")
        tile_done, gate_free, up_free = R.sem("gate_up_done"), R.sem("gate_bank_free"), R.sem("up_bank_free")
        d_loaded = [R.sem(f"down_loaded{s}") for s in range(ND)]
        d_used, done, gated = R.sem("down_used"), R.sem("down_done"), R.sem("ffn_was_gated")
        acc = [R.B[(4 + i) % 8] for i in range(6)]
        with nc.Block() as block:

            @block.sync
            def _(sp):
                with sp.Fori(0, NF // 2 - 1) as i:
                    c = sp.snap(i * (2 * P) + 2 * P)
                    for p in range(2):
                        sp.wait_ge(tile_done, 2 * i + p + 3)
                        dense_loads(R, sp, p, c + p * P)

            @block.gpsimd
            def _(pool):
                nc.gpsimd.memset(R.mod_sums[:, :, :], 0.0).then_inc(cleared, 1)
                pool.wait_ge(cleared, 1)
                for c in range(2):
                    pool.dma_start(R.mod_sums[0:1, c, :], R.I["mod_b"][1:2, :]).then_inc(biased, 16)
                with pool.Fori(0, KT) as k:
                    for g in range(3):
                        pool.wait_ge(m_used, 3 * k + g + 1)
                        pool.dma_start(MW[:, g, :], R.I["mod_w"][1, bass.ds(k * P, P), 2 * D * g:2 * D * (g + 1)]).then_inc(m_loaded[g], 16)
                for u in range(NF // 2):
                    if u >= ND:
                        pool.wait_ge(d_used, u - ND + 1)
                    pool.dma_start(WD[:, u % ND, :, :], R.I["ffn_w_down"][0, 2 * u * P:(2 * u + 2) * P, :].rearrange("(k p) n -> p k n", p=P))\
                        .then_inc(d_loaded[u % ND], 16)
                for u in range(6):
                    t, h = divmod(u, 2)
                    x = R.X[:, t, h * BANK:(h + 1) * BANK]
                    pool.wait_ge(gated, u + 1)
                    nc.gpsimd.tensor_tensor(x, x, Y[:, u, :], ALU.add)

            @block.tensor
            def _(pe):
                pe.sem_inc(tile_done, 2)
                with pe.Fori(0, NF // 2) as i:
                    for p in range(2):
                        pe.wait_ge(loaded[p], 32 * i + 32)
                        pe.wait_ge(gate_free, 2 * i + p + 1)
                        pe.wait_ge(up_free, 2 * i + p + 1)
                        for m in range(2):
                            for k in range(KT):
                                mm = nc.tensor.matmul(R.B[2 * p + m][:, 0:TOK], W[:, p, m, k, :], R.HT[:, k, :],
                                                      start=(k == 0), stop=(k == KT - 1))
                        mm.then_inc(tile_done, 1)
                pe.wait_ge(up_free, 2 + NF)
                for f in range(NF):
                    if f % 2 == 0:
                        pe.wait_ge(d_loaded[f // 2 % ND], 16 * (f // 2 // ND + 1))
                    for u in range(6):
                        t, h = divmod(u, 2)
                        mm = nc.tensor.matmul(acc[u][:, :], G[:, f, t * P:(t + 1) * P], WD[:, f // 2 % ND, f % 2, h * BANK:(h + 1) * BANK],
                                              start=(f == 0), stop=(f == NF - 1))
                        if f == NF - 1:
                            mm.then_inc(done, 1)
                        elif f % 2 == 1 and u == 5:
                            mm.then_inc(d_used, 1)

            @block.scalar
            def _(act):
                act.sem_inc(gate_free, 2)
                with act.Fori(0, NF // 2) as i:
                    for p in range(2):
                        act.wait_ge(tile_done, 2 * i + p + 3)
                        act.wait_ge(up_free, 2 * i + p + 1)
                        nc.scalar.activation(sil[:, p, :], R.B[2 * p][:, 0:TOK], ACT.Silu).then_inc(gate_free, 1)

            @block.vector
            def _(dve):
                dve.sem_inc(up_free, 2)
                dve.sem_inc(m_used, 3)
                dve.wait_ge(biased, 32)

                def gated_tiles(i):
                    for p in range(2):
                        dve.wait_ge(gate_free, 2 * i + p + 3)
                        nc.vector.tensor_tensor(G[:, :, :].rearrange("p f n -> p (f n)")[:, bass.ds(i * (2 * TOK) + p * TOK, TOK)],
                                                sil[:, p, :], R.B[2 * p + 1][:, 0:TOK], ALU.mult).then_inc(up_free, 1)

                with dve.Fori(0, KT) as k:
                    gated_tiles(k)
                    dve.wait_ge(R.mod_sums_done, 6 * k)
                    for g in range(3):
                        dve.wait_ge(m_loaded[g], 16 * k + 16)
                        for c in range(2):
                            sums = R.mod_sums[:, c, 2 * D * g:2 * D * (g + 1)]
                            ins = nc.vector.scalar_tensor_tensor(out=sums, in0=MW[:, g, :], in1=sums, op0=ALU.mult, op1=ALU.add,
                                                                 scalar=R.cond[:, bass.ds(k, 1), c:c + 1].rearrange("p a b -> p (a b)"))
                            ins.then_inc(R.mod_sums_done, 1)
                        dve.wait_ge(R.mod_sums_done, 6 * k + 2 * g + 2)
                        dve.sem_inc(m_used, 1)
                with dve.Fori(KT, NF // 2) as i:
                    gated_tiles(i)
                for u in range(6):
                    t, h = divmod(u, 2)
                    dve.wait_ge(done, u + 1)
                    nc.vector.tensor_tensor(Y[:, u, :], acc[u][:, :], R.ffn_gate[:, min(t, 1), h * BANK:(h + 1) * BANK], ALU.mult)\
                        .then_inc(gated, 1)


def layer1(R):
    stack, sb = local(R)
    with stack:
        normed(R, 2)
        R.MT = sb("mixed_by_channel1", [P, KT, TOK])
        inner, sb1 = local(R)
        with inner:
            R.params = sb1("pair_params", [P, N_PARAMS, PAIRS])
            R.lora = sb1("lora_in", [P, 3, TOK])
            scan_buffers(R, sb1)
            pool_lora(R, ahead=lambda sp: scan_loads(R, sp))
            rwkv(R)
        w_out, sb1 = local(R)
        with w_out:
            mixed_buffers(R, sb1, 1)
            mixed(R, 1, ahead=lambda sp: mixed_loads(R, sp, R.I["rw_w_out"][0]))


PARAMS = ("w0_f", "w0_b", "a0_f", "a0_b", "k_k", "k_a", "r_k", "gn_w", "gn_b", "prev_r", "prev_k", "prev_v",
          "next_r", "next_k", "next_v", "self_r", "self_k", "self_v", "half_w0_f", "half_w0_b", "half_a0_f", "half_a0_b",
          "one_less_k_a")
N_PARAMS = len(PARAMS)
PAD = 16
PADDED = PAD + SEQ + PAD + DEC + PAD
LINE = TOK + 3
STREAMS = ((0, SEQ, 0), (SEQ, TOK, 1))


def pool_lora(R, ahead):
    nc = R.nc
    stack, sb = local(R)
    with stack:
        W = sb("pool_lora_w", [P, KT, 640])
        rows = sb("scan_rows", [96, P])
        cols = sb("scan_cols", [P, 96])
        inv = sb("inv_count", [P, 2, TOK])
        GW = sb("pool_w_pairs", [P, 2, P])
        xs = [sb(f"pool_sum{w}", [P, 2, PADDED]) for w in (1,) + POOL_WINDOWS]
        mean, dif = sb("pool_mean", [P, 2, TOK]), sb("pool_diff", [P, 2, TOK])
        raw, mid, own = sb("lora_raw", [P, 3, LINE]), sb("lora_mid", [P, 3, LINE - 2]), sb("lora_self", [P, 3])
        z = sb("lora_shifted", [P, 3, TOK])
        w_in = [R.sem(f"pool_lora_w{i}") for i in range(2)]
        r_in, t_in, g_in = R.sem("scan_rows_in"), R.sem("inv_count_in"), R.sem("pool_w_in")
        pe_done = R.sem("pl_pe_done")
        pe_inc, pe_at = steps(["rows"] + [f"m{m}" for m in range(5)] + ["pool0", "pool1"])
        act_done = R.sem("pl_act_done")
        act_inc, act_at = steps(["rows"] + [f"m{m}" for m in range(5)])
        dve_done = R.sem("pl_dve_done")
        dve_inc, dve_at = steps(["zero", "self", "params", "mid0", "mid1", "z", "s2", "s4", "s8", "s16", "mean", "dif"])
        w = R.I["rw_w_in"][0].rearrange("(k p) n -> p k n", p=P)
        with nc.Block() as block:

            @block.sync
            def _(sp):
                q = 0

                def put(a):
                    nonlocal q
                    n = a.shape[0] // P
                    sp.dma_start(rows[q:q + n, :], a.rearrange("(r p) -> r p", p=P)).then_inc(r_in, 16)
                    q += n

                for name in ("decay_w0", "iclr_a0"):
                    put(R.I[name][0].rearrange("d n -> (d n)"))
                for name in ("k_k", "k_a"):
                    put(R.I[name][0])
                put(R.I["r_k"][0].rearrange("h d -> (h d)"))
                put(R.I["gn_w"][0])
                put(R.I["gn_b"][0])
                for d in range(2):
                    put(R.I["shift_mu"][0, d, 0:3 * 768])
                for d in range(2):
                    put(R.I["shift_mu"][0, d, 3 * 768:3 * 768 + 384])
                assert q == 96
                sp.dma_start(W[:, :, 256:640], w[:, :, 256 + 2304:256 + 2304 + 384]).then_inc(w_in[0], 16)
                sp.dma_start(W[:, :, 0:256], w[:, :, 0:256]).then_inc(w_in[1], 16)
                sp.dma_start(inv[:, :, :], const(R, "inv_count").rearrange("p (a n) -> p a n", a=2)).then_inc(t_in, 16)
                sp.wait_ge(dve_done, dve_at("zero"))
                for g in range(4):
                    h = slice(64 * (g % 2), 64 * (g % 2) + 64)
                    sp.dma_start(GW[h, g // 2, h], R.I["pool_w"][0, g]).then_inc(g_in, 16)
                ahead(sp)

            @block.tensor
            def _(pe):
                pe.wait_ge(r_in, 16 * 11)
                nc.tensor.transpose(R.B[7][:, 0:96], rows[:, :], R.ident[0:96, 0:96]).then_inc(pe_done, pe_inc("rows"))
                for n, m in enumerate((2, 3, 4, 0, 1)):
                    if n in (0, 3):
                        pe.wait_ge(w_in[n // 3], 16)
                    for k in range(KT):
                        mm = nc.tensor.matmul(R.B[n][:, 0:TOK], W[:, k, m * P:(m + 1) * P], R.HT[:, k, :], start=(k == 0), stop=(k == KT - 1))
                    mm.then_inc(pe_done, pe_inc(f"m{n}"))
                pe.wait_ge(g_in, 64)
                pe.wait_ge(dve_done, dve_at("dif"))
                for m in range(2):
                    nc.tensor.matmul(R.B[5 + m][:, 0:TOK], GW[:, m, :], dif[:, m, :], start=True, stop=True).then_inc(pe_done, pe_inc(f"pool{m}"))

            @block.scalar
            def _(act):
                act.wait_ge(pe_done, pe_at("rows"))
                nc.scalar.activation(cols[:, :], R.B[7][:, 0:96], ACT.Copy).then_inc(act_done, act_inc("rows"))
                act.wait_ge(dve_done, dve_at("zero"))
                for n in range(5):
                    act.wait_ge(pe_done, pe_at(f"m{n}"))
                    for a, b, s in STREAMS:
                        out = raw[:, n, 1 + a + s:1 + b + s] if n < 3 else xs[0][:, n - 3, PAD * (1 + s) + a:PAD * (1 + s) + b]
                        i = nc.scalar.activation(out, R.B[n][:, a:b], ACT.Copy)
                    i.then_inc(act_done, act_inc(f"m{n}"))
                act.wait_ge(dve_done, dve_at("z"))
                nc.scalar.activation(R.lora[:, 0, :], z[:, 0, :], ACT.Tanh)
                nc.scalar.activation(R.lora[:, 1, :], z[:, 1, :], ACT.Copy)
                nc.scalar.activation(R.lora[:, 2, :], z[:, 2, :], ACT.Sigmoid)
                for m in range(2):
                    act.wait_ge(pe_done, pe_at(f"pool{m}"))
                    nc.scalar.activation(R.MT[:, m, :], R.B[5 + m][:, 0:TOK], ACT.Copy, scale=R.VT[:, 48 + m:49 + m])

            @block.vector
            def _(dve):
                nc.vector.memset(raw[:, :, :], 0.0)
                nc.vector.memset(GW[:, :, :], 0.0)
                nc.vector.memset(xs[0][:, :, :], 0.0).then_inc(dve_done, dve_inc("zero"))
                dve.wait_ge(act_done, act_at("rows"))
                par = R.params
                flat = par[:, :, :].rearrange("p q j -> p (q j)")
                nc.vector.tensor_copy(flat[:, 0:90], cols[:, 0:90])
                nc.vector.tensor_scalar(flat[:, 108:132], cols[:, 0:24], 0.5, None, ALU.mult)
                nc.vector.tensor_scalar(flat[:, 132:138], cols[:, 30:36], -1.0, 1.0, ALU.mult, ALU.add)
                nc.vector.tensor_tensor(flat[:, 90:108], cols[:, 54:72], cols[:, 72:90], ALU.add)
                nc.vector.tensor_tensor(own[:, :], cols[:, 90:93], cols[:, 93:96], ALU.add).then_inc(dve_done, dve_inc("self"))
                dve.wait_ge(dve_done, dve_at("self"))
                nc.vector.tensor_scalar(flat[:, 90:108], flat[:, 90:108], -1.0, 1.0, ALU.mult, ALU.add)
                nc.vector.tensor_scalar(own[:, :], own[:, :], -1.0, 1.0, ALU.mult, ALU.add).then_inc(dve_done, dve_inc("params"))
                dve.wait_ge(dve_done, dve_at("params"))
                dve.wait_ge(act_done, act_at("m2"))
                for m in range(3):
                    i = nc.vector.tensor_scalar(mid[:, m, :], raw[:, m, 1:LINE - 1], own[:, m:m + 1], None, ALU.mult)
                i.then_inc(dve_done, dve_inc("mid0"))
                dve.wait_ge(dve_done, dve_at("mid0"))
                for m in range(3):
                    i = nc.vector.scalar_tensor_tensor(out=mid[:, m, :], in0=raw[:, m, 0:LINE - 2], scalar=cols[:, 90 + m:91 + m],
                                                       in1=mid[:, m, :], op0=ALU.mult, op1=ALU.add)
                i.then_inc(dve_done, dve_inc("mid1"))
                dve.wait_ge(dve_done, dve_at("mid1"))
                for m in range(3):
                    for a, b, s in STREAMS:
                        i = nc.vector.scalar_tensor_tensor(out=z[:, m, a:b], in0=raw[:, m, 2 + a + s:2 + b + s], scalar=cols[:, 93 + m:94 + m],
                                                           in1=mid[:, m, a + s:b + s], op0=ALU.mult, op1=ALU.add)
                i.then_inc(dve_done, dve_inc("z"))
                dve.wait_ge(act_done, act_at("m4"))
                prev, lo, hi = xs[0], 0, PADDED
                for i, wd in enumerate(POOL_WINDOWS):
                    a, b = (1, 0) if wd == 2 else (wd // 4, wd // 4)
                    lo, hi = lo + a, hi - b
                    nc.vector.tensor_tensor(xs[i + 1][:, :, lo:hi], xs[i][:, :, lo - a:hi - a], xs[i][:, :, lo + b:hi + b], ALU.add).then_inc(dve_done, dve_inc(f"s{wd}"))
                    dve.wait_ge(dve_done, dve_at(f"s{wd}"))
                dve.wait_ge(t_in, 16)
                for g in range(4):
                    h = slice(64 * (g % 2), 64 * (g % 2) + 64)
                    for a, b, s in STREAMS:
                        o = PAD * (1 + s)
                        i = nc.vector.tensor_tensor(mean[h, g // 2, a:b], xs[g + 1][h, g // 2, o + a:o + b], inv[h, g // 2, a:b], ALU.mult)
                i.then_inc(dve_done, dve_inc("mean"))
                dve.wait_ge(dve_done, dve_at("mean"))
                for a, b, s in STREAMS:
                    o = PAD * (1 + s)
                    i = nc.vector.tensor_tensor(dif[:, :, a:b], mean[:, :, a:b], xs[0][:, :, o + a:o + b], ALU.subtract)
                i.then_inc(dve_done, dve_inc("dif"))


CHAINS = [(1, 0, [2, 3, 4, 5], 3), (1, 1, [5, 4, 3, 2], 3), (0, 0, [0, 1], 0), (0, 1, [1, 0], 0)]
SLOTS = 8
CHAIN_STEPS = [(s, n) for s in range(4) for n, ch in enumerate(CHAINS) if s < len(ch[2])]


def before_slot(d, chunk):
    return next(first + chunks.index(chunk) for _, dr, chunks, first in CHAINS if dr == d and chunk in chunks)


def scan_buffers(R, sb):
    R.rkv_w, R.lora_up, R.state_in = sb("rkv_w", [P, 3, KT, P]), sb("lora_up", [P, 3, P]), sb("state_in", [HD, 2, 2, HD])
    R.scan_masks, R.same_head, R.chunk_starts = sb("scan_masks", [P, 2, 8, P]), sb("same_head", [P, P]), sb("chunk_starts", [P, TOK])
    R.rk_w_in, R.v_w_in, R.lora_up_in, R.state_in_loaded, R.scan_consts_in = (
        R.sem(n) for n in ("rk_w_in", "v_w_in", "lora_up_in", "state_in_loaded", "scan_consts_in"))


def rkv_loads(R, q, c, ms):
    w_dram = R.I["rw_w_in"][0].rearrange("(k p) n -> p k n", p=P)
    for m in ms:
        q.dma_start(R.rkv_w[:, m, :, :], w_dram[:, :, 256 + 768 * m:1024 + 768 * m][:, :, bass.ds(c, P)]).then_inc(R.rk_w_in if m < 2 else R.v_w_in, 16)


def pair_loads(R, q, c, h):
    ups = [R.I[n][0].rearrange("d l n -> (d l) n") for n in ("decay_up", "iclr_up")] + [R.I["gate_up"][0]]
    for m in range(3):
        q.dma_start(R.lora_up[:, m, :], ups[m][:, bass.ds(c, P)]).then_inc(R.lora_up_in, 16)
    st_in = R.I["state_wkv"][0, 0].rearrange("d h v k -> v d h k")
    for d in range(2):
        q.dma_start(R.state_in[:, d, :, :], st_in[:, d, bass.ds(h, 2), :]).then_inc(R.state_in_loaded, 16)


def scan_loads(R, sp):
    rkv_loads(R, sp, 0, range(3))
    pair_loads(R, sp, 0, 0)
    sp.dma_start(R.scan_masks[:, :, :, :], const(R, "masks").rearrange("p (d i n) -> p d i n", d=2, i=8)).then_inc(R.scan_consts_in, 16)
    sp.dma_start(R.same_head[:, :], const(R, "halves")).then_inc(R.scan_consts_in, 16)
    sp.dma_start(R.chunk_starts[:, :], const(R, "chunk")).then_inc(R.scan_consts_in, 16)


def rwkv(R):
    nc = R.nc
    stack, sb = local(R)
    with stack:
        W, up, s0, masks, halves, chunk = R.rkv_w, R.lora_up, R.state_in, R.scan_masks, R.same_head, R.chunk_starts
        par, par_next = sb("params_now", [P, N_PARAMS]), sb("params_next", [P, N_PARAMS])
        raw, mid, z = sb("rkv_raw", [P, 3, LINE]), sb("rkv_mid", [P, 3, LINE - 2]), sb("rkv", [P, 3, TOK])
        lw, a, g = sb("log_decay", [P, 2, TOK]), sb("in_rate", [P, 2, TOK]), sb("out_gate", [P, TOK])
        L, D0, D1 = sb("log_sum", [P, 2, TOK]), sb("before_own", [P, 2, TOK]), sb("after_own", [P, 2, TOK])
        E12 = sb("decay_before_and_to", [P, 2, 2, TOK])
        E1, E2 = E12[:, 0], E12[:, 1]
        E3, E4 = (sb(n, [P, 2, TOK]) for n in ("growth", "decay_after"))
        ET = sb("chunk_decay", [P, 2, NCH])
        kkr, sq, nrm, kk = (sb(n, [P, TOK]) for n in ("kk_raw", "kk_sq", "kk_norm", "kk"))
        rn = nrm
        km, nka = sb("k_mod", [P, 2, TOK]), sb("neg_kk_a", [P, 2, TOK])
        ka, rh, be, kt = E1, E2, sb("beta", [P, 2, 2, TOK]), sb("k_grown", [P, 2, 2, TOK])
        Kc, Bc = L, lw
        TM = sb("token_major", [P, TT, 7, P])
        LB = TM[:, 0, 0:3, :].rearrange("p q n -> p (q n)")
        AT, Q1, BT, Q2, T, TI, XM = (sb(n, [P, TT, 4, P]) for n in ("A_T", "Q1_T", "B_T", "Q2_T", "inv", "inv_T", "masked"))
        BV = km[:, :, :].rearrange("p a n -> p (a n)").rearrange("p (t q n) -> p t q n", t=TT, q=4)
        U = nka[:, :, :].rearrange("p a n -> p (a n)").rearrange("p (t d h n) -> p t d h n", t=TT, d=2, h=2)
        NN = T[:, :, :, :].rearrange("p t q n -> p (t q n)")[:, 0:TT * 4 * HD].rearrange("p (t q n) -> p t q n", t=TT, q=4)
        MX = E3[:, :, :].rearrange("p a n -> p (a n)").rearrange("p (t d n) -> p t d n", t=TT, d=2)
        ST = sb("states", [P, 2, SLOTS, HD])
        OS, so = E4[:, 0, :], sb("state_out", [HD, 2, P])
        rk, bonus, y = D0, D1, mid
        B = R.B
        w_in, wv_in, up_in, s_in, c_in, stored = R.rk_w_in, R.v_w_in, R.lora_up_in, R.state_in_loaded, R.scan_consts_in, R.sem("state_stored")
        NL = len(LEVELS)
        lvl = [(l, t) for l in range(NL) for t in range(TT)]
        projected, raw_ready = R.sem("rkv_projected"), R.sem("rkv_raw_ready")
        (proj_inc, proj_at), (raw_inc, raw_at) = steps("rkv"), steps("rkv")
        RAW_BANK = (6, 7, 0)
        early = R.sem("rk_prepared")
        early_inc, early_at = steps(["par", "z0", "z1", "z", "kkr"])
        pe_done = R.sem("scan_pe_done")
        pe_inc, pe_at = steps(["dec0", "dec1", "rate0", "rate1", "gate", "s0", "norm"]
                       + [f"{n}{t}" for t in range(TT) for n in "ab"]
                       + [f"t0_{t}" for t in range(TT)] + [f"tm{t}{i}" for t in range(TT) for i in "ab"]
                       + [f"{x}{l}_{t}" for l in range(NL) for x in ("x", "w", "tr") for t in range(TT) if (x, l) != ("tr", NL - 1)]
                       + [f"{n}{t}" for t in range(TT) for n in ("bv", "mx")]
                       + [f"nn{t}" for t in range(TT)]
                       + [f"{x}{s}_{n}" for s in range(4) for x in "us" for n in range(4) if (s, n) in CHAIN_STEPS]
                       + ["out", "mean", "bonus", "states", "var"])
        act_done = R.sem("scan_act_done")
        act_inc, act_at = steps(["th0", "th1", "lw", "rate0", "rate1", "a", "fac", "gate", "s0", "root", "exp"]
                        + [f"t0_{t}" for t in range(TT)] + [f"tm{t}{i}" for t in range(TT) for i in "ab"]
                        + [f"tr{l}_{t}" for l, t in lvl if l < NL - 1]
                        + [f"{n}{t}" for t in range(TT) for n in ("bv", "mx")]
                        + [f"nn{t}" for t in range(TT)] + ["out", "states", "root2"])
        dve_done = R.sem("scan_dve_done")
        dve_inc, dve_at = steps(["par", "sq", "z0v", "z1v", "zv", "norm", "L", "D", "LB", "rn", "kk", "km", "nka", "ops"]
                        + [x for t in range(TT) for x in (f"at{t}", f"q1{t}", f"bt{t}", f"q2{t}", f"m{t}", f"ti{t}")]
                        + [x for l in range(NL) for x in [f"xm{l}_{t}" for t in range(TT)] + [f"up{l}_{t}" for t in range(TT)]]
                        + [f"{x}{s}_{n}" for s in range(4) for x in "us" for n in range(4) if (s, n) in CHAIN_STEPS]
                        + ["d", "dd", "bonus", "var", "rstd", "yn", "yb", "y"])
        pool_done = R.sem("scan_pool_done")
        pool_inc, pool_at = steps(["zero", "ops", "rk0", "rk"])
        w_dram = R.I["rw_w_in"][0].rearrange("(k p) n -> p k n", p=P)
        ups = [R.I[n][0].rearrange("d l n -> (d l) n") for n in ("decay_up", "iclr_up")] + [R.I["gate_up"][0]]
        st_in = R.I["state_wkv"][0, 0].rearrange("d h v k -> v d h k")
        st_out = R.O["new_state"][0, 0].rearrange("d h v k -> v d h k")
        of = lambda name, par=par: par[:, PARAMS.index(name):PARAMS.index(name) + 1]
        four = lambda ap: ap.rearrange("p (q n) -> p q n", q=4)
        score_bank = lambda t, i, h: B[(4 * t + 2 * i + h) % 6]
        two = lambda ap: ap.unsqueeze(1).broadcast_to([P, 2, TOK])

        with nc.Block() as block:

            @block.sync
            def _(sp):
                sp.wait_ge(projected, proj_at("v", 0))
                rkv_loads(R, sp, P, range(3))
                with sp.Fori(0, PAIRS - 2) as j:
                    c, h, later = sp.snap(j * P + P), sp.snap(j * 2 + 2), sp.snap(j * P + 2 * P)
                    sp.wait_ge(pe_done, pe_at("s0", j))
                    pair_loads(R, sp, c, h)
                    sp.wait_ge(projected, proj_at("k", j + 1))
                    rkv_loads(R, sp, later, (0, 1))
                    sp.wait_ge(projected, proj_at("v", j + 1))
                    rkv_loads(R, sp, later, (2,))
                sp.wait_ge(pe_done, pe_at("s0", PAIRS - 2))
                pair_loads(R, sp, (PAIRS - 1) * P, (PAIRS - 1) * 2)

            @block.gpsimd
            def _(pool):
                with pool.Fori(0, PAIRS) as j:
                    nc.gpsimd.memset(ST[:, :, 0, :], 0.0).then_inc(pool_done, pool_inc("zero"))
                    pool.wait_ge(dve_done, dve_at("nka", j))
                    pool.wait_ge(act_done, act_at("exp", j))
                    nc.gpsimd.tensor_tensor(Kc[:, :, :], km[:, :, :], E4[:, :, :], ALU.mult)
                    nc.gpsimd.tensor_tensor(Bc[:, :, :], nka[:, :, :], E4[:, :, :], ALU.mult).then_inc(pool_done, pool_inc("ops"))
                    pool.wait_ge(dve_done, dve_at("ops", j))
                    pool.sem_inc(R.passed, 1)
                    nc.gpsimd.tensor_scalar(rk[:, 0, :], z[:, 0, :], of("r_k"), None, ALU.mult).then_inc(pool_done, pool_inc("rk0"))
                    pool.wait_ge(pool_done, pool_at("rk0", j))
                    nc.gpsimd.tensor_tensor(rk[:, 0, :], rk[:, 0, :], z[:, 1, :], ALU.mult).then_inc(pool_done, pool_inc("rk"))
                    pool.wait_ge(act_done, act_at("states", j))
                    for d in range(2):
                        pool.dma_start(st_out[:, d, bass.ds(j * 2, 2), :], so[:, d, :].rearrange("v (h k) -> v h k", h=2)).then_inc(stored, 16)
                    pool.wait_ge(dve_done, dve_at("y", j))
                    pool.wait_ge(pe_done, pe_at("states", j))
                pool.wait_ge(stored, 32 * PAIRS)

            @block.tensor
            def _(pe):

                def project(m, ks=range(KT)):
                    for k in ks:
                        mm = nc.tensor.matmul(B[RAW_BANK[m]][:, 0:TOK], W[:, m, k, :], R.HT[:, k, :], start=(k == 0), stop=(k == KT - 1))
                    if k == KT - 1:
                        mm.then_inc(projected, proj_inc("rkv"[m]))

                def turn(j, more):
                    pe.wait_ge(up_in, 48 * j + 48)
                    for m, name in enumerate(("dec", "rate")):
                        for d in range(2):
                            h = slice(64 * d, 64 * d + 64)
                            nc.tensor.matmul(B[3 + 2 * m + d][:, 0:TOK], up[h, m, :], R.lora[h, m, :], start=True, stop=True).then_inc(pe_done, pe_inc(f"{name}{d}"))
                    nc.tensor.matmul(B[7][:, 0:TOK], up[:, 2, :], R.lora[:, 2, :], start=True, stop=True).then_inc(pe_done, pe_inc("gate"))
                    pe.wait_ge(s_in, 32 * j + 32)
                    pe.wait_ge(raw_ready, raw_at("v", j))
                    pe.sem_inc(R.passed, 1)
                    for d in range(2):
                        mm = nc.tensor.transpose(B[0][:, d * HD:(d + 1) * HD], s0[:, d, :, :].rearrange("v h k -> v (h k)"), R.ident[0:HD, 0:HD])
                    mm.then_inc(pe_done, pe_inc("s0"))
                    pe.wait_ge(dve_done, dve_at("sq", j))
                    nc.tensor.matmul(B[1][:, 0:TOK], halves[:, :], sq[:, :], start=True, stop=True).then_inc(pe_done, pe_inc("norm"))
                    if more:
                        pe.wait_ge(w_in, 32 * j + 64)
                        pe.wait_ge(act_done, act_at("rate1", j))
                        project(0)
                    if more:
                        pe.wait_ge(act_done, act_at("gate", j))
                        project(1)
                    pe.wait_ge(dve_done, dve_at("ops", j))
                    pe.wait_ge(act_done, act_at("gate", j))
                    for t in range(TT):
                        cols = slice(t * P, (t + 1) * P)
                        for i, left in enumerate((be, kt)):
                            if 2 * t + i >= 3:
                                pe.wait_ge(dve_done, dve_at(f"{('q1', 'q2')[(2 * t + i - 3) % 2]}{(2 * t + i - 3) // 2}", j))
                            for h in range(2):
                                out = score_bank(t, i, h).rearrange("p (m d n) -> p m d n", m=2, d=2)
                                for d in range(2):
                                    mm = nc.tensor.matmul(out[:, :, d, :], left[:, h, d, cols], E12[:, :, d, cols], start=True, stop=True)
                            mm.then_inc(pe_done, pe_inc(f"{('a', 'b')[i]}{t}"))
                    for t in range(TT):
                        pe.wait_ge(dve_done, dve_at(f"ti{t}", j))
                        if t == 0:
                            pe.wait_ge(dve_done, dve_at("q22", j))
                        for q in range(4):
                            mm = nc.tensor.transpose(B[t][:, q * P:(q + 1) * P], TI[:, t, q, :], R.ident[:, :])
                        mm.then_inc(pe_done, pe_inc(f"t0_{t}"))
                    pe.wait_ge(pool_done, pool_at("ops", j))
                    if more:
                        pe.wait_ge(raw_ready, raw_at("k", j + 1))
                    for t in range(TT):
                        cols = slice(t * P, (t + 1) * P)
                        for i, srcs in enumerate(([ka[:, 0, cols], ka[:, 1, cols], Kc[:, 0, cols], Kc[:, 1, cols]],
                                                  [Bc[:, 0, cols], Bc[:, 1, cols], z[:, 2, cols]])):
                            if t:
                                pe.wait_ge(act_done, act_at(f"tm{t - 1}{'ab'[i]}", j))
                            for n, src in enumerate(srcs):
                                mm = nc.tensor.transpose(B[6 + i][:, n * P:(n + 1) * P], src, R.ident[:, :])
                            mm.then_inc(pe_done, pe_inc(f"tm{t}{'ab'[i]}"))
                    for l in range(NL):
                        for t in range(TT):
                            pe.wait_ge(act_done, act_at(f"tr{l - 1}_{t}" if l else f"t0_{t}", j))
                            for q in range(4):
                                mm = nc.tensor.matmul(B[t][:, q * P:(q + 1) * P], AT[:, t, q, :], T[:, t, q, :], start=True, stop=True)
                            mm.then_inc(pe_done, pe_inc(f"x{l}_{t}"))
                        for t in range(TT):
                            pe.wait_ge(dve_done, dve_at(f"xm{l}_{t}", j))
                            for q in range(4):
                                left, right = (TI, XM) if l < NL - 1 else (XM, TI)
                                mm = nc.tensor.matmul(B[3 + t][:, q * P:(q + 1) * P], left[:, t, q, :], right[:, t, q, :], start=True, stop=True)
                            mm.then_inc(pe_done, pe_inc(f"w{l}_{t}"))
                        if l < NL - 1:
                            for t in range(TT):
                                pe.wait_ge(dve_done, dve_at(f"up{l}_{t}", j))
                                for q in range(4):
                                    mm = nc.tensor.transpose(B[t][:, q * P:(q + 1) * P], T[:, t, q, :], R.ident[:, :])
                                mm.then_inc(pe_done, pe_inc(f"tr{l}_{t}"))
                    for t in range(TT):
                        pe.wait_ge(dve_done, dve_at(f"up{NL - 1}_{t}", j))
                        pe.wait_ge(act_done, act_at(f"tm{t}b", j))
                        for q in range(4):
                            h = slice(64 * (q % 2), 64 * (q % 2) + 64)
                            mm = nc.tensor.matmul(B[t][:, q * HD:(q + 1) * HD], BT[:, t, q, :], TM[:, t, 6, h], start=True, stop=True)
                        mm.then_inc(pe_done, pe_inc(f"bv{t}"))
                        for q in range(4):
                            h = slice(64 * (q % 2), 64 * (q % 2) + 64)
                            mm = nc.tensor.matmul(B[3 + t][h, (q // 2) * P:(q // 2 + 1) * P], TM[:, t, q // 2, h], TI[:, t, q, :], start=True, stop=True)
                        mm.then_inc(pe_done, pe_inc(f"mx{t}"))
                    for t in range(TT):
                        pe.wait_ge(act_done, act_at(f"bv{t}", j))
                        for q in range(4):
                            mm = nc.tensor.matmul(B[t][:, (4 + q) * HD:(5 + q) * HD], TI[:, t, q, :], BV[:, t, q, :], start=True, stop=True)
                        mm.then_inc(pe_done, pe_inc(f"nn{t}"))
                    pe.wait_ge(act_done, act_at("nn2", j))
                    pe.wait_ge(pool_done, pool_at("zero", j))
                    for s in range(4):
                        now = [n for n in range(4) if (s, n) in CHAIN_STEPS]
                        for n in now:
                            _, d, chunks, first = CHAINS[n]
                            t, cp = divmod(chunks[s], 2)
                            c = slice(64 * cp, 64 * cp + 64)
                            if s:
                                pe.wait_ge(dve_done, dve_at(f"s{s - 1}_{n}", j))
                                pe.sem_inc(R.passed, 1)
                            else:
                                pe.wait_ge(act_done, act_at("nn2", j))
                                pe.sem_inc(R.passed, 1)
                            for h in range(2):
                                hr = slice(64 * h, 64 * h + 64)
                                mm = nc.tensor.matmul(B[2 * n + h][c, 0:HD], MX[hr, t, d, c], ST[hr, d, first + s, :], start=True, stop=True)
                            mm.then_inc(pe_done, pe_inc(f"u{s}_{n}"))
                        for n in now:
                            _, d, chunks, first = CHAINS[n]
                            t, cp = divmod(chunks[s], 2)
                            c = slice(64 * cp, 64 * cp + 64)
                            pe.wait_ge(dve_done, dve_at(f"u{s}_{n}", j))
                            pe.sem_inc(R.passed, 1)
                            for h in range(2):
                                hr = slice(64 * h, 64 * h + 64)
                                out = B[2 * n][hr, 2 * HD:3 * HD]
                                nc.tensor.matmul(out, TM[c, t, 2 + d, hr], TM[c, t, 6, hr], start=True, stop=False)
                                mm = nc.tensor.matmul(out, TM[c, t, 4 + d, hr], U[c, t, d, h, :], start=False, stop=True)
                            mm.then_inc(pe_done, pe_inc(f"s{s}_{n}"))
                    for n in range(4):
                        pe.wait_ge(dve_done, dve_at(f"s{len(CHAINS[n][2]) - 1}_{n}", j))
                    for t in range(TT):
                        for h in range(2):
                            hr = slice(64 * h, 64 * h + 64)
                            for d in range(2):
                                q = 2 * d + h
                                out = B[4][hr, t * P:(t + 1) * P]
                                nc.tensor.matmul(out, TM[:, t, 6, hr], Q2[:, t, q, :], start=(d == 0), stop=False)
                                nc.tensor.matmul(out, U[:, t, d, h, :], Q1[:, t, q, :], start=False, stop=False)
                                for cp in range(2):
                                    ch = 2 * t + cp
                                    mm = nc.tensor.matmul(B[4][hr, ch * C:(ch + 1) * C], ST[hr, d, before_slot(d, ch), :],
                                                          rh[hr, d, ch * C:(ch + 1) * C], start=False, stop=(d == 1 and cp == 1))
                    mm.then_inc(pe_done, pe_inc("out"))
                    if more:
                        pe.wait_ge(wv_in, 16 * j + 32)
                        project(2, range(4))
                    pe.wait_ge(act_done, act_at("out", j))
                    nc.tensor.matmul(B[5][:, 0:TOK], halves[:, :], OS[:, :], start=True, stop=True).then_inc(pe_done, pe_inc("mean"))
                    pe.wait_ge(pool_done, pool_at("rk", j))
                    nc.tensor.matmul(B[6][:, 0:TOK], halves[:, :], rk[:, 0, :], start=True, stop=True).then_inc(pe_done, pe_inc("bonus"))
                    for d in range(2):
                        mm = nc.tensor.transpose(B[7][0:HD, d * P:(d + 1) * P], ST[:, d, 2, :], R.ident[:, :])
                    mm.then_inc(pe_done, pe_inc("states"))
                    if more:
                        project(2, range(4, KT))
                    pe.wait_ge(dve_done, dve_at("dd", j))
                    nc.tensor.matmul(B[4][:, 0:TOK], halves[:, :], sq[:, :], start=True, stop=True).then_inc(pe_done, pe_inc("var"))
                    pe.wait_ge(dve_done, dve_at("var", j))
                    pe.wait_ge(act_done, act_at("states", j))

                pe.wait_ge(w_in, 32)
                pe.wait_ge(wv_in, 16)
                for m in range(3):
                    project(m)
                pe.wait_ge(c_in, 48)
                pe.wait_ge(raw_ready, raw_at("v", 0))
                with pe.Fori(0, PAIRS - 1) as j:
                    turn(j, True)
                turn(PAIRS - 1, False)

            @block.scalar
            def _(act):
                def copy_raw(m, j):
                    act.wait_ge(projected, proj_at("rkv"[m], j))
                    for a0, b0, s in STREAMS:
                        i = nc.scalar.activation(raw[:, m, 1 + a0 + s:1 + b0 + s], B[RAW_BANK[m]][:, a0:b0], ACT.Copy)
                    i.then_inc(raw_ready, raw_inc("rkv"[m]))

                def turn(j, more):
                    act.wait_ge(early, early_at("par", j))
                    for m, (name, dst, ev) in enumerate((("dec", lw, "th"), ("rate", a, "rate"))):
                        for d in range(2):
                            act.wait_ge(pe_done, pe_at(f"{name}{d}", j))
                            nc.scalar.activation(dst[:, d, :], B[3 + 2 * m + d][:, 0:TOK], ACT.Tanh, scale=0.5,
                                                               bias=of(("half_w0_", "half_a0_")[m] + "fb"[d], par_next)).then_inc(act_done, act_inc(f"{ev}{d}"))
                        act.wait_ge(act_done, act_at(f"{ev}1", j))
                        if m == 0:
                            nc.scalar.activation(lw[:, :, :], lw[:, :, :], ACT.Copy, scale=-DECAY / 2, bias=-DECAY / 2).then_inc(act_done, act_inc("lw"))
                        else:
                            nc.scalar.activation(a[:, :, :], a[:, :, :], ACT.Copy, scale=0.5, bias=0.5).then_inc(act_done, act_inc("a"))
                            act.wait_ge(act_done, act_at("a", j))
                            nc.scalar.activation(km[:, :, :], a[:, :, :], ACT.Identity, scale=of("k_a", par_next), bias=of("one_less_k_a", par_next))\
                                .then_inc(act_done, act_inc("fac"))
                    act.wait_ge(pe_done, pe_at("gate", j))
                    act.wait_ge(dve_done, dve_at("par", j))
                    nc.scalar.activation(g[:, :], B[7][:, 0:TOK], ACT.Copy).then_inc(act_done, act_inc("gate"))
                    act.wait_ge(pe_done, pe_at("s0", j))
                    nc.scalar.activation(ST[:, :, 3, :], B[0][:, 0:P].rearrange("p (d n) -> p d n", d=2), ACT.Copy).then_inc(act_done, act_inc("s0"))
                    act.wait_ge(dve_done, dve_at("norm", j))
                    nc.scalar.activation(rn[:, :], nrm[:, :], ACT.Sqrt).then_inc(act_done, act_inc("root"))
                    tables_for(R, ACT.Exp, 2)
                    act.wait_ge(dve_done, dve_at("LB", j))
                    nc.scalar.activation(ET[:, :, :], L[:, :, C - 1:TOK:C], ACT.Exp)
                    for dst, f, b, sc in ((E3, L[:, 0, :], LB[:, :], -1.0), (E1, D0[:, 0, :], D1[:, 1, :], 1.0),
                                          (E2, L[:, 0, :], LB[:, :], 1.0), (E4, D1[:, 0, :], D0[:, 1, :], 1.0)):
                        nc.scalar.activation(dst[:, 0, :], f, ACT.Exp, scale=sc)
                        i = nc.scalar.activation(dst[:, 1, :], b, ACT.Exp, scale=sc)
                    i.then_inc(act_done, act_inc("exp"))
                    if more:
                        for m in range(2):
                            copy_raw(m, j + 1)
                    for t in range(TT):
                        act.wait_ge(pe_done, pe_at(f"t0_{t}", j))
                        nc.scalar.activation(T[:, t, :, :], four(B[t][:, :]), ACT.Copy).then_inc(act_done, act_inc(f"t0_{t}"))
                    for t in range(TT):
                        act.wait_ge(pe_done, pe_at(f"tm{t}a", j))
                        nc.scalar.activation(TM[:, t, 0:4, :], four(B[6][:, :]), ACT.Copy).then_inc(act_done, act_inc(f"tm{t}a"))
                        act.wait_ge(pe_done, pe_at(f"tm{t}b", j))
                        nc.scalar.activation(TM[:, t, 4:7, :], B[7][:, 0:TOK].rearrange("p (q n) -> p q n", q=3), ACT.Copy).then_inc(act_done, act_inc(f"tm{t}b"))
                    for l in range(NL - 1):
                        for t in range(TT):
                            act.wait_ge(pe_done, pe_at(f"tr{l}_{t}", j))
                            nc.scalar.activation(TI[:, t, :, :], four(B[t][:, :]), ACT.Copy).then_inc(act_done, act_inc(f"tr{l}_{t}"))
                    for t in range(TT):
                        act.wait_ge(pe_done, pe_at(f"bv{t}", j))
                        nc.scalar.activation(BV[:, t, :, :], B[t][:, 0:4 * HD].rearrange("p (q n) -> p q n", q=4), ACT.Copy).then_inc(act_done, act_inc(f"bv{t}"))
                        act.wait_ge(pe_done, pe_at(f"mx{t}", j))
                        nc.scalar.activation(MX[:, t, :, :], B[3 + t][:, 0:2 * P].rearrange("p (d n) -> p d n", d=2), ACT.Copy).then_inc(act_done, act_inc(f"mx{t}"))
                    for t in range(TT):
                        act.wait_ge(pe_done, pe_at(f"nn{t}", j))
                        nc.scalar.activation(NN[:, t, :, :], B[t][:, 4 * HD:8 * HD].rearrange("p (q n) -> p q n", q=4), ACT.Copy).then_inc(act_done, act_inc(f"nn{t}"))
                    act.wait_ge(pe_done, pe_at("out", j))
                    nc.scalar.activation(OS[:, :], B[4][:, 0:TOK], ACT.Copy).then_inc(act_done, act_inc("out"))
                    act.wait_ge(pe_done, pe_at("states", j))
                    act.wait_ge(stored, 32 * j)
                    nc.scalar.activation(so[:, :, :], B[7][0:HD, 0:2 * P].rearrange("p (d n) -> p d n", d=2), ACT.Copy).then_inc(act_done, act_inc("states"))
                    tables_for(R, ACT.Sqrt, 3)
                    act.wait_ge(dve_done, dve_at("var", j))
                    nc.scalar.activation(rn[:, :], nrm[:, :], ACT.Sqrt).then_inc(act_done, act_inc("root2"))
                    tables_for(R, ACT.Tanh, 4)
                    if more:
                        copy_raw(2, j + 1)

                for m in range(3):
                    copy_raw(m, 0)
                with act.Fori(0, PAIRS - 1) as j:
                    turn(j, True)
                turn(PAIRS - 1, False)

            @block.vector
            def _(dve):
                v = nc.vector
                for c in (0, SEQ + 1, LINE - 1):
                    v.memset(raw[:, :, c:c + 1], 0.0)
                for h in range(2):
                    other = slice(64 - 64 * h, 128 - 64 * h)
                    v.memset(be[other, h, :, :], 0.0)
                    v.memset(kt[other, h, :, :], 0.0)

                def shifted_keys(j, last):
                    v.tensor_copy(par_next[:, :], R.params[:, :, bass.ds(j, 1)].rearrange("p q a -> p (q a)")).then_inc(early, early_inc("par"))
                    dve.wait_ge(early, early_at("par", j))
                    dve.wait_ge(raw_ready, raw_at("k", j))
                    if last is not None:
                        dve.wait_ge(pool_done, pool_at("rk", last))
                    for m, name in enumerate("rk"):
                        i = v.tensor_scalar(mid[:, m, :], raw[:, m, 1:LINE - 1], of("self_" + name, par_next), None, ALU.mult)
                    i.then_inc(early, early_inc("z0"))
                    dve.wait_ge(early, early_at("z0", j))
                    for m, name in enumerate("rk"):
                        i = v.scalar_tensor_tensor(out=mid[:, m, :], in0=raw[:, m, 0:LINE - 2], scalar=of("prev_" + name, par_next), in1=mid[:, m, :],
                                                   op0=ALU.mult, op1=ALU.add)
                    i.then_inc(early, early_inc("z1"))
                    dve.wait_ge(early, early_at("z1", j))
                    for m, name in enumerate("rk"):
                        for a0, b0, s in STREAMS:
                            i = v.scalar_tensor_tensor(out=z[:, m, a0:b0], in0=raw[:, m, 2 + a0 + s:2 + b0 + s], scalar=of("next_" + name, par_next),
                                                       in1=mid[:, m, a0 + s:b0 + s], op0=ALU.mult, op1=ALU.add)
                    i.then_inc(early, early_inc("z"))
                    dve.wait_ge(early, early_at("z", j))
                    v.tensor_scalar(kkr[:, :], z[:, 1, :], of("k_k", par_next), None, ALU.mult).then_inc(early, early_inc("kkr"))

                def turn(j, more):

                    v.tensor_copy(par[:, :], R.params[:, :, bass.ds(j, 1)].rearrange("p q a -> p (q a)")).then_inc(dve_done, dve_inc("par"))
                    dve.wait_ge(early, early_at("kkr", j))
                    v.tensor_tensor(sq[:, :], kkr[:, :], kkr[:, :], ALU.mult).then_inc(dve_done, dve_inc("sq"))
                    dve.wait_ge(dve_done, dve_at("par", j))
                    dve.wait_ge(raw_ready, raw_at("v", j))
                    v.tensor_scalar(mid[:, 2, :], raw[:, 2, 1:LINE - 1], of("self_v"), None, ALU.mult).then_inc(dve_done, dve_inc("z0v"))
                    dve.wait_ge(dve_done, dve_at("z0v", j))
                    v.scalar_tensor_tensor(out=mid[:, 2, :], in0=raw[:, 2, 0:LINE - 2], scalar=of("prev_v"), in1=mid[:, 2, :],
                                           op0=ALU.mult, op1=ALU.add).then_inc(dve_done, dve_inc("z1v"))
                    dve.wait_ge(dve_done, dve_at("z1v", j))
                    for a0, b0, s in STREAMS:
                        i = v.scalar_tensor_tensor(out=z[:, 2, a0:b0], in0=raw[:, 2, 2 + a0 + s:2 + b0 + s], scalar=of("next_v"),
                                                   in1=mid[:, 2, a0 + s:b0 + s], op0=ALU.mult, op1=ALU.add)
                    i.then_inc(dve_done, dve_inc("zv"))
                    dve.wait_ge(pe_done, pe_at("norm", j))
                    v.tensor_scalar(nrm[:, :], B[1][:, 0:TOK], L2_EPS, None, ALU.add).then_inc(dve_done, dve_inc("norm"))
                    dve.wait_ge(act_done, act_at("lw", j))
                    for d in range(2):
                        i = v.tensor_tensor_scan(L[:, d, :], chunk[:, :], lw[:, d, :], 0.0, ALU.mult, ALU.add)
                    i.then_inc(dve_done, dve_inc("L"))
                    dve.wait_ge(dve_done, dve_at("L", j))
                    v.tensor_tensor(D0[:, :, :], L[:, :, :], lw[:, :, :], ALU.subtract)
                    by_chunk = lambda x: x[:, :, :].rearrange("p d (c n) -> p (d c) n", n=C)
                    v.tensor_tensor(by_chunk(D1), by_chunk(L)[:, :, C - 1:C].broadcast_to([P, 2 * NCH, C]), by_chunk(L), ALU.subtract).then_inc(dve_done, dve_inc("D"))
                    dve.wait_ge(dve_done, dve_at("D", j))
                    v.tensor_tensor(LB[:, :], D1[:, 1, :], lw[:, 1, :], ALU.add).then_inc(dve_done, dve_inc("LB"))
                    dve.wait_ge(act_done, act_at("root", j))
                    v.reciprocal(rn[:, :], rn[:, :]).then_inc(dve_done, dve_inc("rn"))
                    dve.wait_ge(dve_done, dve_at("rn", j))
                    v.tensor_tensor(kk[:, :], kkr[:, :], rn[:, :], ALU.mult).then_inc(dve_done, dve_inc("kk"))
                    dve.wait_ge(dve_done, dve_at("kk", j))
                    dve.wait_ge(act_done, act_at("fac", j))
                    v.tensor_tensor(km[:, :, :], km[:, :, :], two(z[:, 1, :]), ALU.mult).then_inc(dve_done, dve_inc("km"))
                    v.scalar_tensor_tensor(out=nka[:, :, :], in0=two(kk[:, :]), scalar=-1.0, in1=a[:, :, :], op0=ALU.mult, op1=ALU.mult).then_inc(dve_done, dve_inc("nka"))
                    dve.wait_ge(dve_done, dve_at("nka", j))
                    dve.wait_ge(act_done, act_at("exp", j))
                    for h in range(2):
                        hr = slice(64 * h, 64 * h + 64)
                        v.tensor_tensor(be[hr, h, :, :], nka[hr, :, :], E3[hr, :, :], ALU.mult)
                    v.tensor_tensor(ka[:, :, :], E1[:, :, :], two(kk[:, :]), ALU.mult)
                    v.tensor_tensor(rh[:, :, :], E2[:, :, :], two(z[:, 0, :]), ALU.mult)
                    for h in range(2):
                        hr = slice(64 * h, 64 * h + 64)
                        i = v.tensor_tensor(kt[hr, h, :, :], km[hr, :, :], E3[hr, :, :], ALU.mult)
                    i.then_inc(dve_done, dve_inc("ops"))
                    as4 = lambda ap: ap.rearrange("p (d h n) -> p d h n", d=2, h=2)
                    sq4 = lambda x, t: x[:, t, :, :].rearrange("p (d h) n -> p d h n", d=2)
                    for t in range(TT):
                        for i, (name, dst, m) in enumerate((("at", AT, 0), ("q1", Q1, 1), ("bt", BT, 0), ("q2", Q2, 1))):
                            dve.wait_ge(pe_done, pe_at(f"{'ab'[i // 2]}{t}", j))
                            for h in range(2):
                                src = score_bank(t, i // 2, h)[:, (i % 2) * 2 * P:(i % 2 + 1) * 2 * P].rearrange("p (d n) -> p d n", d=2)
                                ins = v.tensor_tensor(dst[:, t, h:4:2, :], src, masks[:, :, m, :], ALU.mult)
                            ins.then_inc(dve_done, dve_inc(f"{name}{t}"))
                        dve.wait_ge(dve_done, dve_at(f"at{t}", j))
                        for d in range(2):
                            ins = v.tensor_tensor(XM[:, t, 2 * d:2 * d + 2, :], AT[:, t, 2 * d:2 * d + 2, :],
                                                  masks[:, d, 2, :].unsqueeze(1).broadcast_to([P, 2, P]), ALU.mult)
                        ins.then_inc(dve_done, dve_inc(f"m{t}"))
                        dve.wait_ge(dve_done, dve_at(f"m{t}", j))
                        v.tensor_tensor(TI[:, t, :, :], XM[:, t, :, :], R.ident[:, :].unsqueeze(1).broadcast_to([P, 4, P]), ALU.add)\
                            .then_inc(dve_done, dve_inc(f"ti{t}"))
                    if more:
                        shifted_keys(j + 1, j)
                    for l in range(NL):
                        for t in range(TT):
                            dve.wait_ge(pe_done, pe_at(f"x{l}_{t}", j))
                            for d in range(2):
                                ins = v.tensor_tensor(XM[:, t, 2 * d:2 * d + 2, :], four(B[t][:, :])[:, 2 * d:2 * d + 2, :],
                                                      masks[:, d, 3 + l, :].unsqueeze(1).broadcast_to([P, 2, P]), ALU.mult)
                            ins.then_inc(dve_done, dve_inc(f"xm{l}_{t}"))
                        for t in range(TT):
                            dve.wait_ge(pe_done, pe_at(f"w{l}_{t}", j))
                            dst = T if l < NL - 1 else TI
                            v.tensor_tensor(dst[:, t, :, :], dst[:, t, :, :], four(B[3 + t][:, :]), ALU.add).then_inc(dve_done, dve_inc(f"up{l}_{t}"))
                    for s in range(4):
                        now = [n for n in range(4) if (s, n) in CHAIN_STEPS]
                        for n in now:
                            _, d, chunks, _ = CHAINS[n]
                            t, cp = divmod(chunks[s], 2)
                            c = slice(64 * cp, 64 * cp + 64)
                            dve.wait_ge(pe_done, pe_at(f"u{s}_{n}", j))
                            if s == 0:
                                dve.wait_ge(act_done, act_at("nn2", j))
                            v.tensor_tensor(U[c, t, d, :, :], R.PS[c, 2 * n:2 * n + 2, 0:HD], NN[c, t, 2 * d:2 * d + 2, :], ALU.add).then_inc(dve_done, dve_inc(f"u{s}_{n}"))
                        for n in now:
                            _, d, chunks, first = CHAINS[n]
                            dve.wait_ge(pe_done, pe_at(f"s{s}_{n}", j))
                            if s:
                                dve.wait_ge(dve_done, dve_at(f"s{s - 1}_{n}", j))
                            v.scalar_tensor_tensor(out=ST[:, d, first + s + 1, :], in0=ST[:, d, first + s, :], scalar=ET[:, d, chunks[s]:chunks[s] + 1],
                                                       in1=B[2 * n][:, 2 * HD:3 * HD], op0=ALU.mult, op1=ALU.add).then_inc(dve_done, dve_inc(f"s{s}_{n}"))
                    dve.wait_ge(pe_done, pe_at("mean", j))
                    v.scalar_tensor_tensor(out=OS[:, :], in0=B[5][:, 0:TOK], scalar=-1.0 / HD, in1=OS[:, :], op0=ALU.mult, op1=ALU.add).then_inc(dve_done, dve_inc("d"))
                    dve.wait_ge(dve_done, dve_at("d", j))
                    v.tensor_tensor(sq[:, :], OS[:, :], OS[:, :], ALU.mult).then_inc(dve_done, dve_inc("dd"))
                    dve.wait_ge(pe_done, pe_at("bonus", j))
                    v.tensor_tensor(bonus[:, 0, :], z[:, 2, :], B[6][:, 0:TOK], ALU.mult).then_inc(dve_done, dve_inc("bonus"))
                    dve.wait_ge(pe_done, pe_at("var", j))
                    v.tensor_scalar(nrm[:, :], B[4][:, 0:TOK], 1.0 / HD, GN_EPS, ALU.mult, ALU.add).then_inc(dve_done, dve_inc("var"))
                    dve.wait_ge(act_done, act_at("root2", j))
                    v.reciprocal(rn[:, :], rn[:, :]).then_inc(dve_done, dve_inc("rstd"))
                    dve.wait_ge(dve_done, dve_at("rstd", j))
                    v.scalar_tensor_tensor(out=y[:, 0, 0:TOK], in0=OS[:, :], scalar=of("gn_w"), in1=rn[:, :], op0=ALU.mult, op1=ALU.mult)\
                        .then_inc(dve_done, dve_inc("yn"))
                    dve.wait_ge(dve_done, dve_at("yn", j))
                    v.scalar_tensor_tensor(out=y[:, 0, 0:TOK], in0=y[:, 0, 0:TOK], scalar=of("gn_b"), in1=bonus[:, 0, :], op0=ALU.add, op1=ALU.add)\
                        .then_inc(dve_done, dve_inc("yb"))
                    dve.wait_ge(dve_done, dve_at("yb", j))
                    v.tensor_tensor(R.MT[:, :, :].rearrange("p k n -> p (k n)")[:, bass.ds(2 * TOK + j * TOK, TOK)],
                                        y[:, 0, 0:TOK], g[:, :], ALU.mult).then_inc(dve_done, dve_inc("y"))
                    dve.wait_ge(pe_done, pe_at("states", j))

                shifted_keys(0, None)
                dve.wait_ge(c_in, 48)
                with dve.Fori(0, PAIRS - 1) as j:
                    turn(j, True)
                turn(PAIRS - 1, False)


def moe(R):
    stack, sb = local(R)
    with stack:
        R.H = sb("normed_by_token", [P, TT, D])
        R.place = sb("place_in_item", [P, TT, ITEM_COLS])
        R.weight = sb("weight_in_item", [P, TT, ITEM_COLS])
        R.slots = sb("slot_numbers", [P, P])
        R.items = sb("item_experts", [1, ITEM_COLS + 1], I32)
        router_buffers(R, sb)
        expert_buffers(R, sb)

        def first_loads(sp):
            router_loads(R, sp)
            first_expert(R, sp)

        normed(R, 3, ahead=first_loads)
        routed(R)
        experts(R)


def router_buffers(R, sb):
    R.router = sb("router_cols", [P, KT, NE]), sb("router_bias", [1, NE])
    R.router_consts = sb("before_token", [P, P]), sb("all_ones", [P, P]), sb("item_numbers", [P, ITEM_COLS]), sb("lower_first", [P, NE])
    R.router_in = R.sem("router_loaded")


def router_loads(R, sp):
    RW, rb = R.router
    before, ones, item, lower = R.router_consts
    sp.dma_start(RW[:, :, :], R.I["router_w"][0].rearrange("(k p) e -> p k e", p=P)).then_inc(R.router_in, 16)
    sp.dma_start(rb[:, :], R.I["router_b"]).then_inc(R.router_in, 16)
    for buf, name in ((before, "before"), (ones, "ones"), (R.slots, "slot"), (item, "item"), (lower, "lower8")):
        sp.dma_start(buf[:, :], const(R, name)).then_inc(R.router_in, 16)


def routed(R):
    nc = R.nc
    stack, sb = local(R)
    with stack:
        (RW, rb), (before, ones, item, lower), one = R.router, R.router_consts, sb("router_one", [1, P])
        lg, eq, o1, o2, mk, cb, rank = (sb(f"route_{n}", [P, TT, NE]) for n in ("logits", "equal", "first", "second", "mask", "combine", "rank"))
        m1, m2, rm, df, g1, g2 = (sb(f"route_{n}", [P, TT]) for n in ("max1", "max2", "pick", "diff", "gate1", "gate2"))
        cnt, nb, big, end, start = (sb(f"expert_{n}", [P, NE]) for n in ("count", "blocks", "third", "end", "start"))
        own, low, prod = (sb(f"item_{n}", [P, ITEM_COLS, NE]) for n in ("owner", "low", "product"))
        base, ex, itf = sb("item_base", [P, ITEM_COLS]), sb("item_expert", [P, ITEM_COLS]), sb("item_row", [1, ITEM_COLS + 1])
        loaded = R.router_in
        turned, t_out = R.sem("h_turned"), R.sem("h_copied")
        pe_done = R.sem("route_pe_done")
        pe_inc, pe_at = steps(["logits", "rank"])
        act_done = R.sem("route_act_done")
        act_inc, act_at = steps(["exp"])
        dve_done = R.sem("route_dve_done")
        dve_inc, dve_at = steps(["one", "lg", "m1", "eq1", "pr1", "rm1", "o1", "lg2", "m2", "eq2", "pr2", "rm2", "o2", "df",
                                         "den", "g1", "g2", "mask", "c1", "c2", "cb", "cnt", "nb1", "nb2", "nb", "end", "start",
                                         "low", "own0", "own", "ps", "bs", "b1", "base", "pe", "ex", "ex1", "row", "items", "rk1", "rk2"]
                        + [x for t in range(TT) for x in (f"pp{t}", f"pl{t}", f"place{t}", f"pw{t}", f"w{t}")])
        with nc.Block() as block:

            @block.tensor
            def _(pe):
                pe.wait_ge(loaded, 7 * 16)
                pe.wait_ge(dve_done, dve_at("one"))
                for t in range(TT):
                    for k in range(KT):
                        nc.tensor.matmul(R.B[0][:, t * NE:(t + 1) * NE], R.HT[:, k, t * P:(t + 1) * P], RW[:, k, :], start=(k == 0), stop=False)
                    mm = nc.tensor.matmul(R.B[0][:, t * NE:(t + 1) * NE], one[0:1, :], rb[0:1, :], start=False, stop=True)
                mm.then_inc(pe_done, pe_inc("logits"))
                for t in range(TT):
                    for h in range(2):
                        for k in range(4):
                            mm = nc.tensor.transpose(R.B[2 + 2 * t + h][:, k * P:(k + 1) * P], R.HT[:, 4 * h + k, t * P:(t + 1) * P], R.ident[:, :])
                        mm.then_inc(turned, 1)
                pe.wait_ge(dve_done, dve_at("mask"))
                for t in range(TT):
                    for s in range(t):
                        nc.tensor.matmul(R.B[1][:, t * NE:(t + 1) * NE], ones[:, :], mk[:, s, :], start=(s == 0), stop=False)
                    nc.tensor.matmul(R.B[1][:, t * NE:(t + 1) * NE], before[:, :], mk[:, t, :], start=(t == 0), stop=True)
                for s in range(TT):
                    mm = nc.tensor.matmul(R.B[1][:, TT * NE:(TT + 1) * NE], ones[:, :], mk[:, s, :], start=(s == 0), stop=(s == TT - 1))
                mm.then_inc(pe_done, pe_inc("rank"))

            @block.scalar
            def _(act):
                for u in range(2 * TT):
                    act.wait_ge(turned, u + 1)
                    nc.scalar.activation(R.H[:, u // 2, (u % 2) * BANK:(u % 2 + 1) * BANK], R.B[2 + u][:, :], ACT.Copy)
                act.wait_ge(dve_done, dve_at("df"))
                nc.scalar.activation(g2[:, :], df[:, :], ACT.Exp).then_inc(act_done, act_inc("exp"))

            @block.vector
            def _(dve):
                v = nc.vector


                wide = lambda x: x.unsqueeze(2).broadcast_to([P, TT, NE])
                per_e = lambda x: x.unsqueeze(1).broadcast_to([P, ITEM_COLS, NE])
                per_i = lambda x: x.unsqueeze(2).broadcast_to([P, ITEM_COLS, NE])
                v.memset(one[:, :], 1.0).then_inc(dve_done, dve_inc("one"))
                dve.wait_ge(loaded, 7 * 16)
                dve.wait_ge(pe_done, pe_at("logits"))
                v.tensor_copy(lg[:, :, :], R.B[0][:, 0:TT * NE].rearrange("p (t e) -> p t e", t=TT)).then_inc(dve_done, dve_inc("lg"))
                dve.wait_ge(dve_done, dve_at("lg"))
                for n, (m, o) in enumerate(((m1, o1), (m2, o2)), 1):
                    v.tensor_reduce(m[:, :], lg[:, :, :], AX.X, ALU.max).then_inc(dve_done, dve_inc(f"m{n}"))
                    dve.wait_ge(dve_done, dve_at(f"m{n}"))
                    v.tensor_tensor(eq[:, :, :], lg[:, :, :], wide(m[:, :]), ALU.is_equal).then_inc(dve_done, dve_inc(f"eq{n}"))
                    dve.wait_ge(dve_done, dve_at(f"eq{n}"))
                    v.tensor_tensor(eq[:, :, :], eq[:, :, :], lower[:, :].unsqueeze(1).broadcast_to([P, TT, NE]), ALU.mult).then_inc(dve_done, dve_inc(f"pr{n}"))
                    dve.wait_ge(dve_done, dve_at(f"pr{n}"))
                    v.tensor_reduce(rm[:, :], eq[:, :, :], AX.X, ALU.max).then_inc(dve_done, dve_inc(f"rm{n}"))
                    dve.wait_ge(dve_done, dve_at(f"rm{n}"))
                    v.tensor_tensor(o[:, :, :], eq[:, :, :], wide(rm[:, :]), ALU.is_equal).then_inc(dve_done, dve_inc(f"o{n}"))
                    dve.wait_ge(dve_done, dve_at(f"o{n}"))
                    if n == 1:
                        v.scalar_tensor_tensor(out=lg[:, :, :], in0=o1[:, :, :], scalar=-1e30, in1=lg[:, :, :], op0=ALU.mult, op1=ALU.add).then_inc(dve_done, dve_inc("lg2"))
                        dve.wait_ge(dve_done, dve_at("lg2"))
                v.tensor_tensor(df[:, :], m2[:, :], m1[:, :], ALU.subtract).then_inc(dve_done, dve_inc("df"))
                dve.wait_ge(act_done, act_at("exp"))
                v.tensor_scalar(g1[:, :], g2[:, :], 1.0, None, ALU.add).then_inc(dve_done, dve_inc("den"))
                dve.wait_ge(dve_done, dve_at("den"))
                v.reciprocal(g1[:, :], g1[:, :]).then_inc(dve_done, dve_inc("g1"))
                dve.wait_ge(dve_done, dve_at("g1"))
                v.tensor_tensor(g2[:, :], g2[:, :], g1[:, :], ALU.mult).then_inc(dve_done, dve_inc("g2"))
                dve.wait_ge(dve_done, dve_at("g2"))
                v.tensor_tensor(mk[:, :, :], o1[:, :, :], o2[:, :, :], ALU.add).then_inc(dve_done, dve_inc("mask"))
                dve.wait_ge(dve_done, dve_at("mask"))
                v.tensor_tensor(o1[:, :, :], o1[:, :, :], wide(g1[:, :]), ALU.mult).then_inc(dve_done, dve_inc("c1"))
                v.tensor_tensor(o2[:, :, :], o2[:, :, :], wide(g2[:, :]), ALU.mult).then_inc(dve_done, dve_inc("c2"))
                dve.wait_ge(dve_done, dve_at("c2"))
                v.tensor_tensor(cb[:, :, :], o1[:, :, :], o2[:, :, :], ALU.add).then_inc(dve_done, dve_inc("cb"))
                dve.wait_ge(dve_done, dve_at("cb"))
                dve.wait_ge(pe_done, pe_at("rank"))
                v.tensor_copy(rank[:, :, :], R.B[1][:, 0:TT * NE].rearrange("p (t e) -> p t e", t=TT))
                v.tensor_copy(cnt[:, :], R.B[1][:, TT * NE:(TT + 1) * NE]).then_inc(dve_done, dve_inc("cnt"))
                dve.wait_ge(dve_done, dve_at("cnt"))
                v.tensor_scalar(nb[:, :], cnt[:, :], float(P), 1.0, ALU.is_gt, ALU.add).then_inc(dve_done, dve_inc("nb1"))
                v.tensor_scalar(big[:, :], cnt[:, :], float(2 * P), None, ALU.is_gt).then_inc(dve_done, dve_inc("nb2"))
                dve.wait_ge(dve_done, dve_at("nb2"))
                v.tensor_tensor(nb[:, :], nb[:, :], big[:, :], ALU.add).then_inc(dve_done, dve_inc("nb"))
                dve.wait_ge(dve_done, dve_at("nb"))
                v.tensor_tensor_scan(end[:, :], ones[:, 0:NE], nb[:, :], 0.0, ALU.mult, ALU.add).then_inc(dve_done, dve_inc("end"))
                dve.wait_ge(dve_done, dve_at("end"))
                v.tensor_tensor(start[:, :], end[:, :], nb[:, :], ALU.subtract).then_inc(dve_done, dve_inc("start"))
                dve.wait_ge(dve_done, dve_at("start"))
                v.tensor_tensor(low[:, :, :], per_i(item[:, :]), per_e(start[:, :]), ALU.is_ge).then_inc(dve_done, dve_inc("low"))
                v.tensor_tensor(own[:, :, :], per_i(item[:, :]), per_e(end[:, :]), ALU.is_lt).then_inc(dve_done, dve_inc("own0"))
                dve.wait_ge(dve_done, dve_at("own0"))
                v.tensor_tensor(own[:, :, :], own[:, :, :], low[:, :, :], ALU.mult).then_inc(dve_done, dve_inc("own"))
                dve.wait_ge(dve_done, dve_at("own"))
                v.tensor_tensor(prod[:, :, :], own[:, :, :], per_e(start[:, :]), ALU.mult).then_inc(dve_done, dve_inc("ps"))
                dve.wait_ge(dve_done, dve_at("ps"))
                v.tensor_reduce(base[:, :], prod[:, :, :], AX.X, ALU.add).then_inc(dve_done, dve_inc("bs"))
                dve.wait_ge(dve_done, dve_at("bs"))
                v.tensor_tensor(base[:, :], item[:, :], base[:, :], ALU.subtract).then_inc(dve_done, dve_inc("b1"))
                dve.wait_ge(dve_done, dve_at("b1"))
                v.tensor_scalar(base[:, :], base[:, :], float(P), None, ALU.mult).then_inc(dve_done, dve_inc("base"))
                dve.wait_ge(dve_done, dve_at("base"))
                v.tensor_tensor(prod[:, :, :], own[:, :, :], per_e(lower[:, :]), ALU.mult).then_inc(dve_done, dve_inc("pe"))
                dve.wait_ge(dve_done, dve_at("pe"))
                v.tensor_reduce(ex[:, :], prod[:, :, :], AX.X, ALU.add).then_inc(dve_done, dve_inc("ex"))
                dve.wait_ge(dve_done, dve_at("ex"))
                v.tensor_copy(itf[0:1, ITEM_COLS:ITEM_COLS + 1], end[0:1, NE - 1:NE])
                v.tensor_scalar(ex[0:1, :], ex[0:1, :], 1.0, None, ALU.max).then_inc(dve_done, dve_inc("ex1"))
                dve.wait_ge(dve_done, dve_at("ex1"))
                v.tensor_scalar(itf[0:1, 0:ITEM_COLS], ex[0:1, :], -1.0, float(NE), ALU.mult, ALU.add).then_inc(dve_done, dve_inc("row"))
                dve.wait_ge(dve_done, dve_at("row"))
                v.tensor_copy(R.items[:, :], itf[:, :]).then_inc(dve_done, dve_inc("items"))
                v.scalar_tensor_tensor(out=rank[:, :, :], in0=rank[:, :, :], scalar=1e4, in1=mk[:, :, :], op0=ALU.add, op1=ALU.mult).then_inc(dve_done, dve_inc("rk1"))
                dve.wait_ge(dve_done, dve_at("rk1"))
                v.tensor_scalar(rank[:, :, :], rank[:, :, :], -1e4, None, ALU.add).then_inc(dve_done, dve_inc("rk2"))
                dve.wait_ge(dve_done, dve_at("rk2"))
                for t in range(TT):
                    v.tensor_tensor(prod[:, :, :], own[:, :, :], per_e(rank[:, t, :]), ALU.mult).then_inc(dve_done, dve_inc(f"pp{t}"))
                    dve.wait_ge(dve_done, dve_at(f"pp{t}"))
                    v.tensor_reduce(R.place[:, t, :], prod[:, :, :], AX.X, ALU.add).then_inc(dve_done, dve_inc(f"pl{t}"))
                    dve.wait_ge(dve_done, dve_at(f"pl{t}"))
                    v.tensor_tensor(R.place[:, t, :], R.place[:, t, :], base[:, :], ALU.subtract).then_inc(dve_done, dve_inc(f"place{t}"))
                    v.tensor_tensor(prod[:, :, :], own[:, :, :], per_e(cb[:, t, :]), ALU.mult).then_inc(dve_done, dve_inc(f"pw{t}"))
                    dve.wait_ge(dve_done, dve_at(f"pw{t}"))
                    v.tensor_reduce(R.weight[:, t, :], prod[:, :, :], AX.X, ALU.add).then_inc(dve_done, dve_inc(f"w{t}"))
                    dve.wait_ge(dve_done, dve_at(f"w{t}"))


RAW, SPLIT, DOWN_RAW, DOWN_SPLIT = 4, 4, 5, 4
GU_CHUNKS, DOWN_CHUNKS = 2 * KT, FFE // P
EARLY = 2


def expert_buffers(R, sb):
    R.e_w, R.e_down = sb("expert_gate_up", [P, RAW, FFE]), sb("expert_down", [P, DOWN_RAW, D])
    R.e_w_in, R.e_down_in = [R.sem(f"gate_up_in{s}") for s in range(RAW)], [R.sem(f"down_in{s}") for s in range(DOWN_RAW)]


def gate_up_load(R, q, e, u):
    k, m = divmod(u, 2)
    w = R.I[("moe_w_gate", "moe_w_up")[m]]
    q.dma_start(R.e_w[:, u % RAW, :], w[0, bass.ds(e, 1), k * P:(k + 1) * P, :].rearrange("a p n -> (a p) n")).then_inc(R.e_w_in[u % RAW], 16)


def down_load(R, q, e, f):
    q.dma_start(R.e_down[:, f % DOWN_RAW, :], R.I["moe_w_down"][0, bass.ds(e, 1), f * P:(f + 1) * P, :].rearrange("a p n -> (a p) n"))\
        .then_inc(R.e_down_in[f % DOWN_RAW], 16)


def first_expert(R, sp):
    for u in range(RAW):
        gate_up_load(R, sp, 0, u)


def experts(R):
    nc = R.nc
    stack, sb = local(R)
    with stack:
        raw, raw_down, w_in, d_in = R.e_w, R.e_down, R.e_w_in, R.e_down_in
        WH, WL = sb("gate_up_high", [P, SPLIT, FFE], F32R), sb("gate_up_low", [P, SPLIT, FFE], F32R)
        DH, DL = sb("down_high", [P, DOWN_SPLIT, D], F32R), sb("down_low", [P, DOWN_SPLIT, D], F32R)
        hgH, hgL = sb("gathered_high", [P, KT, P], F32R), sb("gathered_low", [P, KT, P], F32R)
        gu = sb("expert_hidden", [P, FFE])
        guTH, guTL = sb("hidden_T_high", [P, DOWN_CHUNKS, P], F32R), sb("hidden_T_low", [P, DOWN_CHUNKS, P], F32R)
        Y = sb("expert_out", [P, D])
        G, GW, GT = (sb(n, [P, TT, P]) for n in ("one_hot", "one_hot_weighted", "scatter"))
        acc = R.HT[:, :, :].rearrange("p k n -> p (k n)").rearrange("p (t d) -> p t d", t=TT)
        B = R.B
        high, low, d_high, d_low = (R.sem(n) for n in ("gate_up_high_ready", "gate_up_low_ready", "down_high_ready", "down_low_ready"))
        w_used, d_used = R.sem("gate_up_multiplied"), R.sem("down_multiplied")
        down_uses = [len(range(s, DOWN_CHUNKS, DOWN_RAW)) for s in range(DOWN_RAW)]
        CH = ((0, 512), (512, 1024), (1024, FFE))
        pe_done = R.sem("exp_pe_done")
        pe_inc, pe_at = steps(["t0", "t1", "t2", "tw"] + [f"sc{u}" for u in range(6)])
        act_done = R.sem("exp_act_done")
        act_inc, act_at = steps(["silu", "t0", "t1", "t2", "y"])
        dve_done = R.sem("exp_dve_done")
        dve_inc, dve_at = steps(["GW", "gu", "tw", "t0", "t1", "t2", "y"])
        one_hot, gathered = R.sem("one_hot_ready"), R.sem("tokens_gathered")
        g_high, g_low = ([R.sem(f"gathered_{n}{h}") for h in range(2)] for n in ("high", "low"))
        gather_inc, gather_at = steps(["first half", "second half"])
        added = R.sem("scatter_added")
        zero = R.sem("acc_cleared")
        n_items = lambda e: e.value_load(R.items[0:1, ITEM_COLS:ITEM_COLS + 1], min_val=NE, max_val=MAX_ITEMS)
        expert_of = lambda q, i: q.value_load(R.items[0:1, bass.ds(i, 1)], min_val=0, max_val=NE - 1)
        all_multiplied = lambda i: GU_CHUNKS * i + (GU_CHUNKS + SPLIT)
        down_finished = lambda i: DOWN_CHUNKS * i + (DOWN_CHUNKS + 1)
        with nc.Block() as block:

            @block.sync
            def _(sp):
                n = n_items(sp)
                with sp.Fori(0, n) as i:
                    e, following = expert_of(sp, i), expert_of(sp, i + 1)
                    for u in range(RAW, GU_CHUNKS + RAW):
                        sp.wait_ge(low, GU_CHUNKS * i + (u - RAW + 1))
                        sp.sem_inc(R.passed, 1)
                        gate_up_load(R, sp, e if u < GU_CHUNKS else following, u % GU_CHUNKS)
                for s in range(RAW):
                    sp.wait_ge(w_in[s], n * (16 * GU_CHUNKS // RAW) + 16)
                    sp.sem_inc(R.passed, 1)

            @block.gpsimd
            def _(pool):
                n = n_items(pool)
                for f in range(DOWN_CHUNKS):
                    if f >= DOWN_RAW:
                        pool.wait_ge(d_low, f - DOWN_RAW + 1)
                    down_load(R, pool, 0, f)
                with pool.Fori(1, n) as i:
                    e = expert_of(pool, i)
                    for f in range(DOWN_CHUNKS):
                        pool.wait_ge(d_low, DOWN_CHUNKS * i + max(f - DOWN_RAW + 1, 0))
                        pool.sem_inc(R.passed, 1)
                        down_load(R, pool, e, f)

            @block.tensor
            def _(pe):
                pe.sem_inc(w_used, SPLIT)
                pe.sem_inc(d_used, 1)

                def gather(i):
                    pe.wait_ge(one_hot, i + 1)
                    for k in range(KT):
                        for t in range(TT):
                            mm = nc.tensor.matmul(B[6 + k // 4][:, (k % 4) * P:(k % 4 + 1) * P], R.H[:, t, k * P:(k + 1) * P], G[:, t, :],
                                                  start=(t == 0), stop=(t == TT - 1))
                        if k % 4 == 3:
                            mm.then_inc(gathered, gather_inc(("first half", "second half")[k // 4]))

                def split_product(out, a, b, first, last):
                    nc.tensor.matmul(out, a[0], b[0], start=first, stop=False)
                    nc.tensor.matmul(out, a[0], b[1], start=False, stop=False)
                    return nc.tensor.matmul(out, a[1], b[0], start=False, stop=last)

                n = n_items(pe)
                gather(0)
                with pe.Fori(0, n) as i:
                    for u in range(GU_CHUNKS):
                        k, m = divmod(u, 2)
                        s = u % SPLIT
                        pe.wait_ge(low, GU_CHUNKS * i + (u + 1))
                        if u % KT == 0:
                            pe.wait_ge(g_low[u // KT], i + 1)
                        for c, (a, b) in enumerate(CH):
                            if k == 0:
                                pe.wait_ge(added, 6 * i + (3 * m + c + 1))
                            mm = split_product(B[3 * m + c][:, 0:b - a], (hgH[:, k, :], hgL[:, k, :]), (WH[:, s, a:b], WL[:, s, a:b]),
                                               k == 0, k == KT - 1)
                        mm.then_inc(w_used, 1)
                    gather(i + 1)
                    pe.wait_ge(dve_done, dve_at("gu", i))
                    for c in range(3):
                        fs = range(4 * c, min(4 * c + 4, DOWN_CHUNKS))
                        for f in fs:
                            mm = nc.tensor.transpose(B[c][:, (f % 4) * P:(f % 4 + 1) * P], gu[:, f * P:(f + 1) * P], R.ident[:, :])
                        mm.then_inc(pe_done, pe_inc(f"t{c}"))
                    pe.wait_ge(g_low[1], i + 2)
                    for t in range(TT):
                        mm = nc.tensor.transpose(B[7][:, t * P:(t + 1) * P], GW[:, t, :], R.ident[:, :])
                    mm.then_inc(pe_done, pe_inc("tw"))
                    pe.wait_ge(g_low[0], i + 2)
                    pe.wait_ge(dve_done, dve_at("tw", i))
                    for f in range(DOWN_CHUNKS):
                        pe.wait_ge(d_low, DOWN_CHUNKS * i + (f + 1))
                        if f % 4 == 0:
                            pe.wait_ge(dve_done, dve_at(f"t{f // 4}", i))
                        s = f % DOWN_SPLIT
                        for h in range(2):
                            cols = slice(h * BANK, (h + 1) * BANK)
                            mm = split_product(B[6 + h][:, :], (guTH[:, f, :], guTL[:, f, :]), (DH[:, s, cols], DL[:, s, cols]),
                                               f == 0, f == DOWN_CHUNKS - 1)
                        mm.then_inc(d_used, 1)
                    pe.wait_ge(act_done, act_at("y", i))
                    pe.wait_ge(dve_done, dve_at("y", i))
                    pe.sem_inc(R.passed, 1)
                    for u in range(6):
                        t, h = divmod(u, 2)
                        nc.tensor.matmul(B[u][:, :], GT[:, t, :], Y[:, h * BANK:(h + 1) * BANK], start=True, stop=True).then_inc(pe_done, pe_inc(f"sc{u}"))

            @block.scalar
            def _(act):
                n = n_items(act)

                def keep_gathered(i):
                    for h in range(2):
                        act.wait_ge(gathered, gather_at(("first half", "second half")[h], i))
                        nc.scalar.activation(hgH[:, 4 * h:4 * h + 4, :], B[6 + h][:, :].rearrange("p (k n) -> p k n", k=4), ACT.Copy).then_inc(g_high[h], 1)

                def split_down(f, i):
                    act.wait_ge(d_used, DOWN_CHUNKS * i + (max(f - DOWN_SPLIT + 1, 0) + 1))
                    act.wait_ge(d_in[f % DOWN_RAW], 16 * down_uses[f % DOWN_RAW] * i + 16 * (f // DOWN_RAW + 1))
                    nc.scalar.activation(DH[:, f % DOWN_SPLIT, :], raw_down[:, f % DOWN_RAW, :], ACT.Copy).then_inc(d_high, 1)

                def split_gate_up(u, i):
                    act.wait_ge(w_used, GU_CHUNKS * i + (u + 1))
                    act.wait_ge(w_in[u % RAW], (16 * GU_CHUNKS // RAW) * i + 16 * (u // RAW + 1))
                    nc.scalar.activation(WH[:, u % SPLIT, :], raw[:, u % RAW, :], ACT.Copy).then_inc(high, 1)

                keep_gathered(0)
                for u in range(EARLY):
                    split_gate_up(u, 0)
                with act.Fori(0, n) as i:
                    for u in range(EARLY, GU_CHUNKS):
                        split_gate_up(u, i)
                    for f in range(DOWN_SPLIT):
                        split_down(f, i)
                    act.wait_ge(w_used, all_multiplied(i) - 1)
                    for c, (a, b) in enumerate(CH):
                        ins = nc.scalar.activation(gu[:, a:b], B[c][:, 0:b - a], ACT.Silu)
                    ins.then_inc(act_done, act_inc("silu"))
                    keep_gathered(i + 1)
                    for c in range(3):
                        fs = slice(4 * c, min(4 * c + 4, DOWN_CHUNKS))
                        w = (fs.stop - fs.start) * P
                        act.wait_ge(pe_done, pe_at(f"t{c}", i))
                        nc.scalar.activation(guTH[:, fs, :], B[c][:, 0:w].rearrange("p (k n) -> p k n", n=P), ACT.Copy).then_inc(act_done, act_inc(f"t{c}"))
                    for f in range(DOWN_SPLIT, DOWN_CHUNKS):
                        split_down(f, i)
                    for u in range(EARLY):
                        split_gate_up(GU_CHUNKS + u, i)
                    act.wait_ge(d_used, down_finished(i))
                    nc.scalar.activation(Y[:, 0:BANK], B[6][:, :], ACT.Copy).then_inc(act_done, act_inc("y"))

            @block.vector
            def _(dve):
                v = nc.vector
                n = n_items(dve)
                dve.sem_inc(added, 6)

                def mark(i):
                    for t in range(TT):
                        ins = v.tensor_scalar(G[:, t, :], R.slots[:, :], R.place[:, t, bass.ds(i, 1)], None, ALU.is_equal)
                    ins.then_inc(one_hot, 1)

                def keep_gathered(i):
                    for h in range(2):
                        ks = slice(4 * h, 4 * h + 4)
                        dve.wait_ge(g_high[h], i + 1)
                        v.tensor_tensor(hgL[:, ks, :], B[6 + h][:, :].rearrange("p (k n) -> p k n", k=4), hgH[:, ks, :], ALU.subtract).then_inc(g_low[h], 1)

                def split_down(f, i):
                    dve.wait_ge(d_high, DOWN_CHUNKS * i + (f + 1))
                    s = f % DOWN_SPLIT
                    v.tensor_tensor(DL[:, s, :], raw_down[:, f % DOWN_RAW, :], DH[:, s, :], ALU.subtract).then_inc(d_low, 1)

                def split_gate_up(u, i):
                    dve.wait_ge(high, GU_CHUNKS * i + (u + 1))
                    v.tensor_tensor(WL[:, u % SPLIT, :], raw[:, u % RAW, :], WH[:, u % SPLIT, :], ALU.subtract).then_inc(low, 1)

                mark(0)
                v.memset(acc, 0.0).then_inc(zero, 1)
                keep_gathered(0)
                dve.wait_ge(zero, 1)
                for u in range(EARLY):
                    split_gate_up(u, 0)
                with dve.Fori(0, n) as i:
                    mark(i + 1)
                    for t in range(TT):
                        ins = v.tensor_scalar(GW[:, t, :], R.slots[:, :], R.place[:, t, bass.ds(i, 1)], R.weight[:, t, bass.ds(i, 1)],
                                              ALU.is_equal, ALU.mult)
                    ins.then_inc(dve_done, dve_inc("GW"))
                    for u in range(EARLY, GU_CHUNKS):
                        split_gate_up(u, i)
                    for f in range(DOWN_SPLIT):
                        split_down(f, i)
                    dve.wait_ge(w_used, all_multiplied(i))
                    dve.wait_ge(act_done, act_at("silu", i))
                    for c, (a, b) in enumerate(CH):
                        ins = v.tensor_tensor(gu[:, a:b], gu[:, a:b], B[3 + c][:, 0:b - a], ALU.mult)
                    ins.then_inc(dve_done, dve_inc("gu"))
                    keep_gathered(i + 1)
                    dve.wait_ge(pe_done, pe_at("tw", i))
                    v.tensor_copy(GT[:, :, :], B[7][:, 0:TT * P].rearrange("p (t n) -> p t n", t=TT)).then_inc(dve_done, dve_inc("tw"))
                    for c in range(3):
                        fs = slice(4 * c, min(4 * c + 4, DOWN_CHUNKS))
                        w = (fs.stop - fs.start) * P
                        dve.wait_ge(act_done, act_at(f"t{c}", i))
                        v.tensor_tensor(guTL[:, fs, :], B[c][:, 0:w].rearrange("p (k n) -> p k n", n=P), guTH[:, fs, :], ALU.subtract)\
                            .then_inc(dve_done, dve_inc(f"t{c}"))
                    for f in range(DOWN_SPLIT, DOWN_CHUNKS):
                        split_down(f, i)
                    split_gate_up(GU_CHUNKS, i)
                    dve.wait_ge(d_used, down_finished(i))
                    v.tensor_copy(Y[:, BANK:D], B[7][:, :]).then_inc(dve_done, dve_inc("y"))
                    for u in range(6):
                        t, h = divmod(u, 2)
                        x = acc[:, t, h * BANK:(h + 1) * BANK]
                        dve.wait_ge(pe_done, pe_at(f"sc{u}", i))
                        v.tensor_tensor(x, x, B[u][:, :], ALU.add).then_inc(added, 1)
                        if u == 2:
                            split_gate_up(GU_CHUNKS + 1, i)
                    dve.wait_ge(added, 6 * i + 12)


def finish(R):
    nc = R.nc
    stack, sb = local(R)
    with stack:
        XN = sb("final", [P, TT, D])
        wrow = sb("final_weight", [P, D])
        ss, ms, rt, rs = (sb(f"{w}_last", [P, TT]) for w in ("sumsq", "meansq", "root", "rstd"))
        acc = R.HT[:, :, :].rearrange("p k n -> p (k n)").rearrange("p (t d) -> p t d", t=TT)
        act_done = R.sem("last_act_done")
        act_inc, act_at = steps([f"square{t}" for t in range(TT)] + ["root"])
        dve_done = R.sem("last_dve_done")
        dve_inc, dve_at = steps([f"{x}{t}" for t in range(TT) for x in ("gated", "x")] + ["mean", "rstd"] + [f"y{t}" for t in range(TT)])
        w_loaded, stored = R.sem("final_weight_loaded"), R.sem("y_stored")
        with nc.Block() as block:

            @block.sync
            def _(sp):
                sp.dma_start(wrow[:, :], R.I["norm_final"].partition_broadcast(P)).then_inc(w_loaded, 16)
                ys = R.O["y_sample"][0].rearrange("(t p) d -> p t d", p=P)
                for t in range(TT):
                    sp.wait_ge(dve_done, dve_at(f"y{t}"))
                    sp.dma_start(R.O["y_prompt"][0] if t == 0 else ys[:, t - 1, :], XN[:, t, :]).then_inc(stored, 16)
                sp.wait_ge(stored, 16 * TT)

            @block.scalar
            def _(act):
                tables_for(R, ACT.Sqrt, 5)
                for t in range(TT):
                    act.wait_ge(dve_done, dve_at(f"x{t}"))
                    nc.scalar.activation(XN[:, t, :], R.X[:, t, :], ACT.Square, accum_out=ss[:, t:t + 1]).then_inc(act_done, act_inc(f"square{t}"))
                act.wait_ge(dve_done, dve_at("mean"))
                nc.scalar.activation(rt[:, :], ms[:, :], ACT.Sqrt).then_inc(act_done, act_inc("root"))

            @block.vector
            def _(dve):
                for t in range(TT):
                    nc.vector.tensor_tensor(acc[:, t, :], acc[:, t, :], R.ffn_gate[:, min(t, 1), :], ALU.mult).then_inc(dve_done, dve_inc(f"gated{t}"))
                    dve.wait_ge(dve_done, dve_at(f"gated{t}"))
                    nc.vector.tensor_tensor(R.X[:, t, :], R.X[:, t, :], acc[:, t, :], ALU.add).then_inc(dve_done, dve_inc(f"x{t}"))
                dve.wait_ge(act_done, act_at(f"square{TT - 1}"))
                nc.vector.tensor_scalar(ms[:, :], ss[:, :], 1.0 / D, RMS_EPS, ALU.mult, ALU.add).then_inc(dve_done, dve_inc("mean"))
                dve.wait_ge(act_done, act_at("root"))
                nc.vector.reciprocal(rs[:, :], rt[:, :]).then_inc(dve_done, dve_inc("rstd"))
                dve.wait_ge(dve_done, dve_at("rstd"))
                dve.wait_ge(w_loaded, 16)
                for t in range(TT):
                    nc.vector.scalar_tensor_tensor(out=XN[:, t, :], in0=R.X[:, t, :], scalar=rs[:, t:t + 1], in1=wrow[:, :],
                                                   op0=ALU.mult, op1=ALU.mult).then_inc(dve_done, dve_inc(f"y{t}"))


def constants(np):
    a = np.zeros((P, N_CONSTS), np.float32)

    def put(name, x):
        lo, hi = CONSTS[name]
        a[:, lo:hi] = np.asarray(x, np.float32).reshape(P, hi - lo)

    p, f = np.arange(P)[:, None], np.arange(P)[None, :]
    put("ident", p == f)
    put("pick", np.stack([np.broadcast_to(p % 32 == c, (P, P)) for c in range(2)], 1))
    same = (p // 64 == f // 64)
    ang = 2 * np.pi * ((p % 64) * (f % 64) % 64) / 64
    put("dft_c", np.concatenate([same * np.cos(ang), same * np.sin(ang)], 1))
    n, m = np.arange(DEC)[:, None], np.arange(DEC)[None, :]
    ang = 2 * np.pi * (n * m % DEC) / DEC
    both = np.stack([np.cos(ang), -np.sin(ang)]) / np.sqrt(DEC * 64)
    put("dft_s", both.reshape(2, 2, P, DEC).transpose(2, 0, 1, 3))
    n, m = np.arange(SEQ)[:, None], np.arange(SEQ)[None, :]
    ang = 2 * np.pi * (n * m % SEQ) / SEQ
    put("dft_p", (np.stack([np.cos(ang), -np.sin(ang)]) / np.sqrt(SEQ * 64)).transpose(1, 0, 2))
    c0 = np.clip(p % GRID_W - WIN // 2, 0, GRID_W - WIN)
    k = np.arange(GRID_W)[None, :]
    put("window", np.where((k >= c0) & (k < c0 + WIN), 0.0, -1e30))
    masks = np.zeros((P, 2, 8, P))
    for d in range(2):
        early = (p < f) if d == 0 else (p > f)
        masks[:, d, 0] = same & early
        masks[:, d, 1] = same & (early | (p == f))
        masks[:, d, 2] = early & (p // 2 == f // 2)
        for i, m in enumerate(LEVELS):
            late = (p > f) if d == 0 else (p < f)
            masks[:, d, 3 + i] = late & (p // (2 * m) == f // (2 * m)) & (p // m != f // m)
    put("masks", masks)
    put("halves", same)
    put("chunk", np.broadcast_to(np.arange(TOK) % C != 0, (P, TOK)))
    inv = np.zeros((P, 2, TOK))
    for g, w in enumerate(POOL_WINDOWS):
        for o, n in ((0, SEQ), (SEQ, DEC)):
            t = np.arange(n)
            inv[64 * (g % 2):64 * (g % 2) + 64, g // 2, o:o + n] = 1.0 / (np.clip(t + w - w // 2, 0, n) - np.clip(t - w // 2, 0, n))
    put("inv_count", inv)
    put("before", p < f)
    put("ones", np.ones((P, P)))
    put("slot", np.broadcast_to(f, (P, P)))
    put("item", np.broadcast_to(np.arange(ITEM_COLS), (P, ITEM_COLS)))
    put("lower8", np.broadcast_to(NE - np.arange(NE), (P, NE)))
    return a


_OUTS = [("y_prompt", (1, SEQ, D)), ("y_sample", (1, DEC, D)), ("new_k", (1, 1, SEQ, 12, HD)),
         ("new_v", (1, 1, SEQ, 12, HD)), ("new_state", (1, 1, 2, 12, HD, HD))]


def kernel(**inputs):
    import numpy as np
    from concourse import bacc
    from concourse.bass_utils import run_bass_kernel_spmd

    nc = bacc.Bacc("TRN2", target_bir_lowering=False, num_devices=1)
    arrays = {f"in_{n}": np.ascontiguousarray(a) for n, a in inputs.items()}
    arrays["in_consts"] = constants(np)
    I = {n[3:]: nc.dram_tensor(n, a.shape, mybir.dt.from_np(a.dtype), kind="ExternalInput").ap() for n, a in arrays.items()}
    O = {n: nc.dram_tensor(f"out_{n}", s, F32, kind="ExternalOutput").ap() for n, s in _OUTS}
    build(nc, I, O)
    r = run_bass_kernel_spmd(nc, [arrays], core_ids=[0])
    return tuple(r.results[0][f"out_{n}"] for n, _ in _OUTS)
```
